# Optimizing a Trainium2 kernel written in Bass

```python
import jax, jax.numpy as jnp
from jax import lax
import numpy as np

D_MODEL = 1024
BATCH = 1
SEQ = 256
DEPTH = 2

CHUNK = 64
MEM_LEN = 256
EPS = 1e-6
ROPE_THETA = 10000.0
MIX_WIDTH = D_MODEL // 2

A_HEAD_DIM = 64
A_HEADS = MIX_WIDTH // A_HEAD_DIM
A_KV_HEADS = A_HEADS // 4
A_WINDOW = 128
A_WIN_CHUNKS = A_WINDOW // CHUNK

B_BLOCK = 128
B_GROUPS = 4
B_GROUP_DIM = MIX_WIDTH // B_GROUPS

C_GROUPS = 8
C_CONV = 3

N_BRANCH = 3

X_HEADS = 4
X_HEAD_DIM = D_MODEL // X_HEADS

N_GROUPS = 4
EXPERTS_PER_GROUP = 8
N_EXPERTS = N_GROUPS * EXPERTS_PER_GROUP
TOP_K = 2
EXPERT_FF = D_MODEL // 2
MOE_BLOCK = 128

IN_WIDTHS = (A_HEADS * A_HEAD_DIM, A_KV_HEADS * A_HEAD_DIM, A_KV_HEADS * A_HEAD_DIM,
             MIX_WIDTH, MIX_WIDTH, MIX_WIDTH, MIX_WIDTH, MIX_WIDTH, N_BRANCH * D_MODEL)
IN_TOTAL = (A_HEADS + 2 * A_KV_HEADS) * A_HEAD_DIM + 5 * MIX_WIDTH + N_BRANCH * D_MODEL

kernel_name = 'hybrid_chunk_causal_swa_gmlp_shortconv_hmoe'

def rms_norm(x, g):
    xf = x.astype(jnp.float32)
    y = xf * lax.rsqrt(jnp.mean(xf * xf, axis=-1, keepdims=True) + EPS)
    return (y * g.astype(jnp.float32)).astype(x.dtype)

def split_columns(p):
    outs = []
    start = 0
    for w in IN_WIDTHS:
        outs.append(p[..., start:start + w])
        start += w
    return outs

def apply_rope(t, positions):
    half = t.shape[-1] // 2
    inv = ROPE_THETA ** (-jnp.arange(half, dtype=jnp.float32) / half)
    ang = positions.astype(jnp.float32)[..., None] * inv
    cos = jnp.cos(ang)[:, :, None, :]
    sin = jnp.sin(ang)[:, :, None, :]
    tf = t.astype(jnp.float32)
    t1, t2 = tf[..., :half], tf[..., half:]
    return jnp.concatenate([t1 * cos - t2 * sin, t2 * cos + t1 * sin], axis=-1).astype(t.dtype)

def sliding_window_gqa(q, k, v, sinks):
    bsz, seq = q.shape[0], q.shape[1]
    nc = seq // CHUNK
    grp = A_HEADS // A_KV_HEADS
    kw = A_WIN_CHUNKS * CHUNK
    qc = q.reshape(bsz, nc, CHUNK, A_KV_HEADS, grp, A_HEAD_DIM)
    lead = (A_WIN_CHUNKS - 1) * CHUNK
    pad = ((0, 0), (lead, 0), (0, 0), (0, 0))
    kp = jnp.pad(k, pad).reshape(bsz, nc + A_WIN_CHUNKS - 1, CHUNK, A_KV_HEADS, A_HEAD_DIM)
    vp = jnp.pad(v, pad).reshape(bsz, nc + A_WIN_CHUNKS - 1, CHUNK, A_KV_HEADS, A_HEAD_DIM)
    kb = jnp.concatenate([kp[:, j:j + nc] for j in range(A_WIN_CHUNKS)], axis=2)
    vb = jnp.concatenate([vp[:, j:j + nc] for j in range(A_WIN_CHUNKS)], axis=2)
    key_chunk = jnp.arange(nc)[:, None] - (A_WIN_CHUNKS - 1) + jnp.arange(kw)[None, :] // CHUNK
    valid = key_chunk >= 0
    s = jnp.einsum('bcqhgd,bckhd->bchgqk', qc, kb).astype(jnp.float32) * (A_HEAD_DIM ** -0.5)
    s = jnp.where(valid[None, :, None, None, None, :], s, -1e30)
    sink = jnp.broadcast_to(sinks.astype(jnp.float32).reshape(1, 1, A_KV_HEADS, grp, 1, 1),
                            s.shape[:-1] + (1,))
    p = jax.nn.softmax(jnp.concatenate([s, sink], axis=-1), axis=-1)[..., :kw]
    o = jnp.einsum('bchgqk,bckhd->bcqhgd', p.astype(v.dtype), vb)
    return o.reshape(bsz, seq, A_HEADS * A_HEAD_DIM)

def spatial_gating(u, v, ln_g, ln_b, w_s, b_s):
    bsz, seq = u.shape[0], u.shape[1]
    nb = seq // B_BLOCK
    vg = v.reshape(bsz, seq, B_GROUPS, B_GROUP_DIM).astype(jnp.float32)
    mu = jnp.mean(vg, axis=-1, keepdims=True)
    var = jnp.mean(jnp.square(vg - mu), axis=-1, keepdims=True)
    vn = ((vg - mu) * lax.rsqrt(var + EPS) * ln_g.astype(jnp.float32).reshape(B_GROUPS, B_GROUP_DIM)
          + ln_b.astype(jnp.float32).reshape(B_GROUPS, B_GROUP_DIM))
    vn = vn.astype(u.dtype).reshape(bsz, nb, B_BLOCK, B_GROUPS, B_GROUP_DIM)
    pos_chunk = jnp.arange(B_BLOCK) // CHUNK
    mask = (pos_chunk[:, None] >= pos_chunk[None, :]).astype(w_s.dtype)
    mixed = jnp.einsum('gij,bnjgc->bnigc', w_s * mask, vn) + b_s.T[None, None, :, :, None]
    return u * mixed.reshape(bsz, seq, MIX_WIDTH)

def short_conv(cx, cb, cc, conv_w):
    z = cc * cx
    y = lax.conv_general_dilated(z, conv_w[:, None, :].astype(z.dtype), window_strides=(1,),
                                 padding=[(C_CONV - 1, 0)],
                                 dimension_numbers=('NWC', 'WIO', 'NWC'),
                                 feature_group_count=MIX_WIDTH)
    return cb * y

def memory_cross_attention(h, m, w_q, w_kv, w_o):
    bsz, seq = h.shape[0], h.shape[1]
    q = (h @ w_q).reshape(bsz, seq, X_HEADS, X_HEAD_DIM)
    kv = (m @ w_kv).reshape(bsz, m.shape[1], 2, X_HEADS, X_HEAD_DIM)
    k, v = kv[:, :, 0], kv[:, :, 1]
    s = jnp.einsum('bshd,bmhd->bhsm', q, k).astype(jnp.float32) * (X_HEAD_DIM ** -0.5)
    p = jax.nn.softmax(s, axis=-1).astype(v.dtype)
    o = jnp.einsum('bhsm,bmhd->bshd', p, v).reshape(bsz, seq, D_MODEL)
    return o @ w_o

def hierarchical_moe(h, w_rg, b_rg, w_re, b_re, w_e1, w_e2):
    bsz, seq, dm = h.shape
    n_tok = bsz * seq
    xt = h.reshape(n_tok, dm)
    pg = jax.nn.softmax((xt @ w_rg + b_rg).astype(jnp.float32), axis=-1)
    gv, gi = lax.top_k(pg, 1)
    g_w, g_idx = gv[:, 0], gi[:, 0]
    le = (xt @ w_re + b_re).astype(jnp.float32).reshape(n_tok, N_GROUPS, EXPERTS_PER_GROUP)
    le_sel = le[jnp.arange(n_tok), g_idx]
    tv, tj = lax.top_k(le_sel, TOP_K)
    w_top = jax.nn.softmax(tv, axis=-1) * g_w[:, None]
    e_id = g_idx[:, None] * EXPERTS_PER_GROUP + tj

    n_asg = n_tok * TOP_K
    a_e = e_id.reshape(n_asg).astype(jnp.int32)
    a_w = w_top.reshape(n_asg)
    a_t = jnp.repeat(jnp.arange(n_tok, dtype=jnp.int32), TOP_K)
    order = jnp.argsort(a_e, stable=True)
    s_e, s_t, s_w = a_e[order], a_t[order], a_w[order]
    counts = jnp.bincount(a_e, length=N_EXPERTS).astype(jnp.int32)
    starts = jnp.cumsum(counts) - counts
    padded = (counts + MOE_BLOCK - 1) // MOE_BLOCK * MOE_BLOCK
    pad_ends = jnp.cumsum(padded)
    pad_starts = pad_ends - padded
    dest = pad_starts[s_e] + (jnp.arange(n_asg, dtype=jnp.int32) - starts[s_e])
    n_blk = -(-n_asg // MOE_BLOCK) + N_EXPERTS
    n_slot = n_blk * MOE_BLOCK
    slot_t = jnp.full((n_slot,), n_tok, jnp.int32).at[dest].set(s_t)
    slot_w = jnp.zeros((n_slot,), xt.dtype).at[dest].set(s_w.astype(xt.dtype))
    blk_e = jnp.minimum(jnp.searchsorted(pad_ends, jnp.arange(n_blk, dtype=jnp.int32) * MOE_BLOCK,
                                         side='right'), N_EXPERTS - 1)
    x_pad = jnp.concatenate([xt, jnp.zeros((1, dm), xt.dtype)], axis=0)
    xs = x_pad[slot_t].reshape(n_blk, MOE_BLOCK, dm)

    def expert_block(args):
        xb, e = args
        gu = xb @ w_e1[e]
        return (jax.nn.silu(gu[:, :EXPERT_FF]) * gu[:, EXPERT_FF:]) @ w_e2[e]

    ys = lax.map(expert_block, (xs, blk_e)).reshape(n_slot, dm)
    y = jnp.zeros((n_tok + 1, dm), xt.dtype).at[slot_t].add(ys * slot_w[:, None])[:n_tok]
    return y.reshape(bsz, seq, dm)

def setup_inputs(seed: int = 0) -> dict:
    key = jax.random.key(seed)
    ks = jax.random.split(key, 27)
    L, D = DEPTH, D_MODEL

    def nrm(k, shape, scale):
        return jax.random.normal(k, shape, jnp.float32) * scale

    return {
        'x': nrm(ks[0], (BATCH, SEQ, D), 1.0),
        'mem': nrm(ks[1], (BATCH, MEM_LEN, D), 1.0),
        'positions': jnp.broadcast_to(jnp.arange(SEQ, dtype=jnp.int32), (BATCH, SEQ)),
        'mix_norm': 1.0 + nrm(ks[2], (L, D), 0.05),
        'w_in': nrm(ks[3], (L, D, IN_TOTAL), D ** -0.5),
        'b_gate': nrm(ks[4], (L, N_BRANCH * D), 0.1),
        'attn_sinks': nrm(ks[5], (L, A_HEADS), 0.5),
        'gmlp_ln_g': 1.0 + nrm(ks[6], (L, MIX_WIDTH), 0.05),
        'gmlp_ln_b': nrm(ks[7], (L, MIX_WIDTH), 0.02),
        'gmlp_w_s': nrm(ks[8], (L, B_GROUPS, B_BLOCK, B_BLOCK), B_BLOCK ** -0.5),
        'gmlp_b_s': 1.0 + nrm(ks[9], (L, B_GROUPS, B_BLOCK), 0.1),
        'conv_w': nrm(ks[10], (L, C_CONV, MIX_WIDTH), C_CONV ** -0.5),
        'w_branch': nrm(ks[11], (L, N_BRANCH, MIX_WIDTH, D), MIX_WIDTH ** -0.5),
        'w_out': nrm(ks[12], (L, D, D), D ** -0.5),
        'xattn_norm': 1.0 + nrm(ks[13], (L, D), 0.05),
        'mem_norm': 1.0 + nrm(ks[14], (L, D), 0.05),
        'w_xq': nrm(ks[15], (L, D, D), D ** -0.5),
        'w_xkv': nrm(ks[16], (L, D, 2 * D), D ** -0.5),
        'w_xo': nrm(ks[17], (L, D, D), D ** -0.5),
        'ffn_norm': 1.0 + nrm(ks[18], (L, D), 0.05),
        'w_router_group': nrm(ks[19], (L, D, N_GROUPS), D ** -0.5),
        'b_router_group': nrm(ks[20], (L, N_GROUPS), 0.01),
        'w_router_expert': nrm(ks[21], (L, D, N_EXPERTS), D ** -0.5),
        'b_router_expert': nrm(ks[22], (L, N_EXPERTS), 0.01),
        'w_expert_in': nrm(ks[23], (L, N_EXPERTS, D, 2 * EXPERT_FF), D ** -0.5),
        'w_expert_out': nrm(ks[24], (L, N_EXPERTS, EXPERT_FF, D), EXPERT_FF ** -0.5),
        'final_norm': 1.0 + nrm(ks[25], (D,), 0.05),
    }

def reference(x, mem, positions, mix_norm, w_in, b_gate, attn_sinks, gmlp_ln_g, gmlp_ln_b,
              gmlp_w_s, gmlp_b_s, conv_w, w_branch, w_out, xattn_norm, mem_norm, w_xq, w_xkv,
              w_xo, ffn_norm, w_router_group, b_router_group, w_router_expert, b_router_expert,
              w_expert_in, w_expert_out, final_norm):
    bsz, seq = x.shape[0], x.shape[1]
    for l in range(DEPTH):
        h = rms_norm(x, mix_norm[l])
        q, k, v, u, vg, cx, cb, cc, gl = split_columns(h @ w_in[l])
        q = apply_rope(q.reshape(bsz, seq, A_HEADS, A_HEAD_DIM), positions)
        k = apply_rope(k.reshape(bsz, seq, A_KV_HEADS, A_HEAD_DIM), positions)
        v = v.reshape(bsz, seq, A_KV_HEADS, A_HEAD_DIM)
        y_a = sliding_window_gqa(q, k, v, attn_sinks[l])
        y_b = spatial_gating(jax.nn.gelu(u), jax.nn.gelu(vg), gmlp_ln_g[l], gmlp_ln_b[l],
                             gmlp_w_s[l], gmlp_b_s[l])
        y_c = short_conv(cx, cb, cc, conv_w[l])
        gates = jax.nn.sigmoid((gl + b_gate[l]).astype(jnp.float32)).astype(x.dtype)
        gates = gates.reshape(bsz, seq, N_BRANCH, D_MODEL)
        merged = (gates[:, :, 0] * (y_a @ w_branch[l, 0])
                  + gates[:, :, 1] * (y_b @ w_branch[l, 1])
                  + gates[:, :, 2] * (y_c @ w_branch[l, 2]))
        x = x + merged @ w_out[l]
        x = x + memory_cross_attention(rms_norm(x, xattn_norm[l]), rms_norm(mem, mem_norm[l]),
                                       w_xq[l], w_xkv[l], w_xo[l])
        x = x + hierarchical_moe(rms_norm(x, ffn_norm[l]), w_router_group[l], b_router_group[l],
                                 w_router_expert[l], b_router_expert[l],
                                 w_expert_in[l], w_expert_out[l])
    return rms_norm(x, final_norm)


_drawn_inputs = setup_inputs


def setup_inputs(seed=0):
    import zlib

    import numpy as np

    out = dict(_drawn_inputs(seed))
    spreads = {}
    factors = {'attn_sinks': 8.0,
     'xattn_norm': 3.108,
     'mem_norm': 3.115,
     'b_router_expert': 2.929,
     'b_router_group': 3.493}
    for name, (base, spread) in spreads.items():
        noise = np.random.default_rng([zlib.crc32(name.encode()), seed]).standard_normal(out[name].shape)
        drawn = base * np.exp(spread * noise) if base else spread * noise
        out[name] = __import__('jax').numpy.asarray(drawn.astype(out[name].dtype))
    for name, factor in factors.items():
        out[name] = (out[name] * factor).astype(out[name].dtype)
    return out
```

```python
from contextlib import ExitStack

import numpy as np

import concourse.bass as bass
from concourse import mybir

F32 = mybir.dt.float32
I32 = mybir.dt.int32
ALU = mybir.AluOpType
ACT = mybir.ActivationFunctionType
AX = mybir.AxisListType

P = 128
D = 1024
T = 256
L = 2
KC = D // P
TB = T // P
MW = 512
MC = MW // P
NE = 32
NG = 4
EPG = NE // NG
SL = 32
XB = (2 * T) // SL - 1
EPS = 1e-6
NEG = -1e30
R = 6
UNIT = 4096
EI = 8
TURNS = NE // EI

ROW_MIX, ROW_GATE, ROW_CONV, ROW_XN, ROW_MN, ROW_FF, ROW_FIN = 0, 8, 32, 44, 52, 60, 68
ROWS = 76
C_ID, C_TRI, C_ROT, C_INV, C_IOTA, C_IDX, C_THR, C_END = 0, 128, 256, 384, 385, 641, 642, 649

UNITS = (["q", "kv", "u", "vg", "cx", "cb", "cc"]
         + [f"{n}{i}{h}" for h in range(2) for i in range(3) for n in ("gate", "br")]
         + ["wo0", "wo1", "xk0", "xk1", "xv0", "xv1", "xq0", "xq1", "xo0", "xo1"])
DENSE = len(UNITS)
PER_LAYER = DENSE + 3 * NE

JOBS = ([("norm0", 1), ("q", 2), ("k", 1), ("v", 1), ("u", 2), ("rot", 3), ("vg", 2), ("ws", 1), ("s", 4),
         ("cx", 2), ("cb", 2), ("pt", 4), ("cc", 2), ("pv", 2), ("mixed", 2)]
        + [(f"{n}{i}{h}", 2) for h in range(2) for i in range(3) for n in ("gate", "br")]
        + [("wo", 4), ("xk", 4), ("xv", 4), ("norm1", 1), ("xq", 4), ("xs", 4), ("xpt", 4), ("xpv", 4), ("xo", 4),
           ("norm2", 1), ("htok", 4), ("router", 1), ("place", 1), ("start", 1), ("table", 1), ("moe", 4)])


def plan_jobs():
    order = [(0, "x", i) for i in range(4)] + [(0, "mem", i) for i in range(4)]
    order += [(0, "vec", 0), (0, "vec", 1), (0, "memnorm", 0)]
    for layer in range(L):
        order += [(layer, name, i) for name, n in JOBS for i in range(n)]
    order += [(L, "norm0", 0)] + [(L, "out", i) for i in range(4)]
    plan, used, at = {}, [0] * 8, 0
    for n, key in enumerate(order):
        bank = key[2] if key[1] == "moe" else at % 8
        plan[key] = (bank, n + 1, used[bank])
        used[bank] += 1
        at = bank + 1
    return plan


JOB = plan_jobs()


def trunk(nc, A, out):
    with ExitStack() as ctx:
        def sb(name, shape, dt=F32):
            return ctx.enter_context(nc.sbuf_tensor(name, shape, dt))

        def sem(name):
            return ctx.enter_context(nc.semaphore(name))

        ring = sb("ring", [P, R, UNIT])
        xT = sb("xT", [P, KC, T])
        hT = sb("hT", [P, KC, T])
        mhatT = sb("mhatT", [P, KC, T])
        mT = sb("mT", [P, KC, T])
        AW = 14728
        arena = sb("arena", [P, AW])
        psum = ctx.enter_context(nc.psum_tensor("banks", [P, 8, 512], F32))
        cst = sb("cst", [P, C_END])
        ones = sb("ones", [P, P])
        cosT = sb("cosT", [P, T])
        sinT = sb("sinT", [P, T])
        vec = sb("vec", [P, L, ROWS])
        sinks = sb("sinks", [P, L, 8])
        rbias = sb("rbias", [P, L, NG + NE])
        bs = sb("bs", [1, L, 512])
        stat = sb("stat", [P, 512])
        rstd = stat[:, 0:T]
        std = stat[:, T:2 * T]
        small = sb("small", [P, 96])

        ident = cst[:, C_ID:C_ID + P]
        tri = cst[:, C_TRI:C_TRI + P]
        rotm = cst[:, C_ROT:C_ROT + P]
        inv = cst[:, C_INV:C_INV + 1]
        iota = cst[:, C_IOTA:C_IOTA + T]
        idx = cst[:, C_IDX:C_IDX + 1]
        thr = cst[:, C_THR:C_THR + 7]

        def region(at, *shape):
            n = int(np.prod(shape))
            assert at + n <= AW, (at, n)
            v = arena[:, at:at + n]
            if len(shape) == 2:
                v = v.rearrange("p (a b) -> p a b", b=shape[1])
            if len(shape) == 3:
                v = v.rearrange("p (a b c) -> p a b c", b=shape[1], c=shape[2])
            return v

        qT = region(0, MC, T)
        kbd = region(1024, 2, 2, T)
        merged = region(0, KC, T)
        vtok = region(2048, 3, P)
        uT = region(2432, MC, T)
        vg = region(3456, TB, MW)
        cx = region(4480, MC, T)
        cb = region(5504, MC, T)
        z = region(6528, MC, T + 2)
        yaT = region(7560, MC, T)
        ybT = region(8584, MC, T)
        ycT = region(9608, MC, T)
        prob = region(10632, 4, 4, P)
        sig = region(10632, 2, 512)
        gtmp = region(11656, 512)
        probT = region(12680, 4, 512)
        kraw = region(14728 - 512, 512)
        qraw = region(5504, MC, T)
        lng = region(10632, 1, MW)
        kxT = region(2048, KC, T)
        vx = region(4096, TB, D)
        qxT = region(6144, KC, T)
        oT = region(8192, KC, T)
        xprob = region(10240, 4, 512)
        xprobT = region(12288, TB, 4, T)
        htok = region(0, TB, D)
        xTe = region(2048, KC, EI * SL)
        swt = region(4096, EI, T)
        sel = region(6144, TB, EI, SL)
        selw = region(10000, TB, EI, 4 * SL)
        logit = region(7168, TB, NG + NE)
        rt = region(7300, 24, NE)
        place = region(8100, TB, NE)
        wtok = region(8164, TB, NE)
        mask = region(8228, TB, NE)
        sg = region(8400, P)
        hh = region(8528, P)
        hhT = region(8656, P)
        ysb = region(8784, T)
        tab = region(9040, 64)
        wr = sb("wr", [P, KC, NG + NE])
        lnt = sb("lnt", [P, 2, MW])
        wsr = region(12680, 4, P)
        vecrows = region(12000, L, P)[0:ROWS]
        posrow = region(13200, T).bitcast(I32)
        wsT = sb("wsT", [P, 4, P])
        tabi = sb("tabi", [1, 2 * 16 + 1], I32)
        zero = sb("zero", [P, P])

        slot_loaded = [sem(f"slot_loaded{i}") for i in range(R)]
        bank_free = [sem(f"bank_free{i}") for i in range(8)]
        S = {n: sem(n) for n in (
            "acc_ready", "units_used", "act_step", "dve_step", "pool_step", "x_loaded", "mem_loaded", "cst_loaded",
            "ws_loaded", "ws_used", "ln_used", "wr_used", "x_ready", "mem_ready", "sq_ready", "std_ready", "h_ready", "vec_ready", "mem_scaled",
            "angles", "rope_ready", "qraw_ready", "qk_ready", "v_ready", "gelu_ready", "ln_std", "ln_var", "vn_ready", "ws_ready",
            "s_shifted", "s_exped", "prob_ready", "probT_ready", "c_ready", "ya_ready", "yb_ready", "yc_ready",
            "sig_ready", "sig_used", "merged_ready", "kx_ready", "vx_ready", "qx_ready", "xs_shifted", "xs_exped",
            "xprob_ready", "xprobT_ready", "o_ready", "htok_ready", "r_shift", "r_exp", "mask_ready", "extra_ready", "span_ready",
            "table_ready", "out_ready", "stored", "mem_hat", "moe_init", "eps_ready")}
        small_loads = [sem(f"layer_vectors_loaded{i}") for i in range(L)]

        def moe_sems(tag):
            return {n: sem(f"{n}_{tag}") for n in (
                "sel_ready", "sel_used", "swt_turned", "swt_ready", "gathered", "xe_ready", "gu_ready", "silu_ready",
                "hid_ready", "hid_turned", "hidT_ready", "y_done", "y_ready")}

        main_sems = moe_sems("main")
        extra_sems = [dict(moe_sems(f"extra{i}"), loaded=sem(f"extra_loaded{i}"), used=sem(f"extra_used{i}")) for i in range(L)]

        def unit_no(layer, name):
            return layer * PER_LAYER + UNITS.index(name)

        def job_begin(pe, layer, name, i=0):
            bank, _, before = JOB[layer, name, i]
            if before:
                pe.wait_ge(bank_free[bank], before)
            return psum[:, bank, :]

        def job_wait(eng, layer, name, i=0):
            bank, ready, _ = JOB[layer, name, i]
            eng.wait_ge(S["acc_ready"], ready)
            return psum[:, bank, :]

        def free(layer, name, i=0):
            return bank_free[JOB[layer, name, i][0]]

        block = ctx.enter_context(nc.Block())

        @block.sync
        def _(sp):
            def load(u, src, words, k, cut=0):
                slot = u % R
                if u >= R:
                    sp.wait_ge(S["units_used"], u - R + 1)
                dst = ring[:, slot, 0:words].rearrange("p (k n) -> p k n", k=k)
                sp.dma_start(dst, src).then_inc(slot_loaded[slot], 16)

            def cols(w, a, b):
                return w.rearrange("(k p) n -> p k n", p=P)[:, :, a:b]

            sp.dma_start(arena[:, 0:2048].rearrange("p (t d) -> p t d", t=TB),
                         A["x"][0].rearrange("(t p) d -> p t d", p=P)).then_inc(S["x_loaded"], 16)
            sp.dma_start(arena[:, 2048:4096].rearrange("p (t d) -> p t d", t=TB),
                         A["mem"][0].rearrange("(t p) d -> p t d", p=P)).then_inc(S["mem_loaded"], 16)
            for layer in range(L):
                u = layer * PER_LAYER
                w_in = A["w_in"][layer]
                for name in UNITS:
                    if name in ("q", "kv", "u", "vg", "cx", "cb", "cc"):
                        a = {"q": 0, "kv": 512, "u": 768, "vg": 1280, "cx": 1792, "cb": 2304, "cc": 2816}[name]
                        n = 256 if name == "kv" else 512
                        load(u, cols(w_in, a, a + n), KC * n, KC)
                    elif name.startswith("gate"):
                        a = 3328 + int(name[4]) * D + int(name[5]) * 512
                        load(u, cols(w_in, a, a + 512), KC * 512, KC)
                    elif name.startswith("br"):
                        h = int(name[3])
                        load(u, cols(A["w_branch"][layer, int(name[2])], h * 512, h * 512 + 512), MC * 512, MC)
                    else:
                        w, a = {"wo": ("w_out", 0), "xk": ("w_xkv", 0), "xv": ("w_xkv", D), "xq": ("w_xq", 0),
                                "xo": ("w_xo", 0)}[name[:2]]
                        a += int(name[2]) * 512
                        load(u, cols(A[w][layer], a, a + 512), KC * 512, KC)
                    u += 1
                w1 = A["w_expert_in"][layer].rearrange("e (h k p) n -> e h p k n", h=2, p=P)
                w2 = A["w_expert_out"][layer].rearrange("e (k p) n -> e p k n", p=P)

                def expert_units(e, put):
                    put(0, w1[bass.ds(e, 1), 0])
                    put(1, w1[bass.ds(e, 1), 1])
                    put(2, w2[bass.ds(e, 1)])

                with sp.Fori(0, TURNS) as turn:
                    for e in range(EI):
                        def put(x, src, e=e):
                            n = u + 3 * e + x
                            sp.wait_ge(S["units_used"], turn * (3 * EI) + (n - R + 1))
                            sp.dma_start(ring[:, n % R, :].rearrange("p (k n) -> p k n", k=4),
                                         src.squeeze(0)).then_inc(slot_loaded[n % R], 16)
                        expert_units(turn * EI + e, put)
                u += 3 * NE
                X = extra_sems[layer]
                sp.wait_ge(S["table_ready"], layer + 1)
                count = sp.value_load(tabi[0:1, 32:33], min_val=0, max_val=XB)
                with sp.If(count > 0):
                    with sp.Fori(0, count) as k:
                        e = sp.value_load(tabi[0:1, bass.ds(k, 1)], min_val=0, max_val=NE - 1)
                        sp.wait_ge(S["units_used"], u)
                        sp.wait_ge(X["used"], k + 1)

                        def put(x, src):
                            sp.dma_start(ring[:, (u + x) % R, :].rearrange("p (k n) -> p k n", k=4),
                                         src.squeeze(0)).then_inc(X["loaded"], 16)
                        expert_units(e, put)
                sp.wait_ge(X["used"], count + 1)
            for i in range(4):
                sp.wait_ge(S["out_ready"], i + 1)
                sp.dma_start(out[0].rearrange("(t p) d -> t p d", p=P)[i // 2, :, (i % 2) * 512:(i % 2) * 512 + 512],
                             arena[:, i * 512:(i + 1) * 512]).then_inc(S["stored"], 16)
            sp.wait_ge(S["stored"], 64)

        @block.gpsimd
        def _(pool):
            pool.memset(ones[:, :], 1.0).then_inc(S["pool_step"], 1)
            for layer in range(L):
                pool.wait_ge(S["mem_hat"], 1)
                pool.wait_ge(S["vec_ready"], 2)
                if layer:
                    pool.wait_ge(S["acc_ready"], JOB[layer - 1, "xv", 3][1])
                for k in range(KC):
                    pool.tensor_scalar(mT[:, k, :], mhatT[:, k, :], vec[:, layer, ROW_MN + k:ROW_MN + k + 1], None,
                                       ALU.mult).then_inc(S["mem_scaled"], 1)

        @block.scalar
        def _(act):
            steps = [0]

            def link(ins):
                steps[0] += 1
                ins.then_inc(S["act_step"], 1)
                act.wait_ge(S["act_step"], steps[0])

            def post(ins, stage):
                link(ins)
                act.sem_inc(S[stage], 1)

            act.dma_start(cst[:, :], A["cst"]).then_inc(S["cst_loaded"], 16)
            act.dma_start(posrow[:, :], A["positions"].broadcast_to([P, T])).then_inc(S["cst_loaded"], 16)
            for layer in range(L):
                for src, at in ((A["mix_norm"][layer], ROW_MIX), (A["b_gate"][layer], ROW_GATE),
                                (A["conv_w"][layer].rearrange("k n -> (k n)"), ROW_CONV),
                                (A["xattn_norm"][layer], ROW_XN), (A["mem_norm"][layer], ROW_MN),
                                (A["ffn_norm"][layer], ROW_FF), (A["final_norm"], ROW_FIN)):
                    rows = src.rearrange("(r p) -> r p", p=P)
                    act.dma_start(vecrows[at:at + rows.shape[0], layer, :], rows).then_inc(small_loads[layer], 16)
            act.dma_start(sinks[:, :, :], A["attn_sinks"].unsqueeze(0).broadcast_to([P, L, 8])).then_inc(S["cst_loaded"], 16)
            act.dma_start(rbias[:, :, 0:NG], A["b_router_group"].unsqueeze(0).broadcast_to([P, L, NG])).then_inc(S["cst_loaded"], 16)
            act.dma_start(rbias[:, :, NG:], A["b_router_expert"].unsqueeze(0).broadcast_to([P, L, NE])).then_inc(S["cst_loaded"], 16)
            act.dma_start(bs[0:1, :, :], A["gmlp_b_s"].rearrange("l g i -> l (g i)").unsqueeze(0)).then_inc(S["cst_loaded"], 16)

            def layer_tables(layer):
                if layer:
                    act.wait_ge(S["acc_ready"], JOB[layer - 1, "router", 0][1])
                    act.wait_ge(S["vn_ready"], layer)
                act.dma_start(wsr[:, :, :], A["gmlp_w_s"][layer].rearrange("g i j -> i g j")).then_inc(S["ws_loaded"], 16)
                act.dma_start(lnt[:, 0, :], A["gmlp_ln_g"][layer:layer + 1].broadcast_to([P, MW])).then_inc(S["ws_loaded"], 16)
                act.dma_start(lnt[:, 1, :], A["gmlp_ln_b"][layer:layer + 1].broadcast_to([P, MW])).then_inc(S["ws_loaded"], 16)
                act.dma_start(wr[:, :, 0:NG], A["w_router_group"][layer].rearrange("(k p) n -> p k n", p=P)).then_inc(S["ws_loaded"], 16)
                act.dma_start(wr[:, :, NG:], A["w_router_expert"][layer].rearrange("(k p) n -> p k n", p=P)).then_inc(S["ws_loaded"], 16)

            layer_tables(0)

            def norm(no, layer, name, src):
                link(act.activation(hT[:, :, :], src, ACT.Square))
                act.sem_inc(S["sq_ready"], 1)
                acc = job_wait(act, layer, name)
                post(act.activation(std, acc[:, 0:T], ACT.Sqrt, bias=small[:, 95:96], scale=1.0 / D), "std_ready")
                act.wait_ge(S["std_ready"], no + 1)
                act.sem_inc(free(layer, name), 1)

            for i in range(4):
                acc = job_wait(act, 0, "x", i)
                post(act.copy(xT[:, 2 * i:2 * i + 2, :], acc.rearrange("p (c t) -> p c t", c=2)), "x_ready")
                act.wait_ge(S["x_ready"], i + 1)
                act.sem_inc(free(0, "x", i), 1)
            for i in range(4):
                acc = job_wait(act, 0, "mem", i)
                post(act.copy(mhatT[:, 2 * i:2 * i + 2, :], acc.rearrange("p (c t) -> p c t", c=2)), "mem_ready")
                act.wait_ge(S["mem_ready"], i + 1)
                act.sem_inc(free(0, "mem", i), 1)
            act.wait_ge(S["angles"], 1)
            post(act.activation(sinT[:, :], stat[:, 0:T], ACT.Sin), "rope_ready")
            act.wait_ge(S["angles"], 2)
            post(act.activation(cosT[:, :], stat[:, T:2 * T], ACT.Sin), "rope_ready")
            norm(0, 0, "memnorm", mhatT[:, :, :])
            n_norm = [1]

            def x_norm(layer, name, count):
                act.wait_ge(S["x_ready"], count)
                norm(n_norm[0], layer, name, xT[:, :, :])
                n_norm[0] += 1

            def evac(layer, name, i, dst, signal, func=None, bias=None, view=None):
                acc = job_wait(act, layer, name, i)
                src = acc if view is None else view(acc)
                if func is None:
                    ins = act.copy(dst, src)
                else:
                    ins = act.activation(dst, src, func)
                post(ins, signal)
                act.sem_inc(free(layer, name, i), 1)

            two = lambda acc: acc.rearrange("p (c t) -> p c t", c=2)

            def softmax_exp(n0, per, shifted, exped, buf, after=None):
                for i in range(per):
                    act.wait_ge(S[shifted], n0 + i + 1)
                    act.activation(buf[:, i], buf[:, i], ACT.Exp).then_inc(S[exped], 1)

            act.wait_ge(S["h_ready"], KC)
            for layer in range(L):
                x_norm(layer, "norm0", 4 + 12 * layer)
                for i in range(2):
                    evac(layer, "q", i, qraw[:, 2 * i:2 * i + 2, :], "qraw_ready", view=two)
                evac(layer, "k", 0, kraw, "qraw_ready")
                evac(layer, "v", 0, vtok[:, 0:2, :], "v_ready", view=lambda a: a[:, 0:2 * P].rearrange("p (c t) -> p c t", c=2))
                post(act.copy(vtok[0:64, 2, :], vtok[0:64, 1, :]), "v_ready")
                post(act.copy(vtok[64:P, 2, :], vtok[64:P, 0, :]), "v_ready")
                for i in range(2):
                    evac(layer, "u", i, uT[:, 2 * i:2 * i + 2, :], "gelu_ready", func=ACT.Gelu_apprx_tanh, view=two)
                for i in range(2):
                    evac(layer, "vg", i, vg[:, i, :], "gelu_ready", func=ACT.Gelu_apprx_tanh)
                evac(layer, "ws", 0, wsT[:, :, :], "ws_ready", view=lambda a: a.rearrange("p (g i) -> p g i", g=4))
                act.wait_ge(S["ln_var"], layer + 1)
                post(act.activation(small[:, 8:16], small[:, 0:8], ACT.Sqrt, bias=small[:, 95:96], scale=1.0 / P), "ln_std")
                for i in range(4):
                    act.wait_ge(S["s_shifted"], 4 * layer + i + 1)
                    post(act.activation(prob[:, i].rearrange("p h k -> p (h k)"), prob[:, i].rearrange("p h k -> p (h k)"), ACT.Exp), "s_exped")
                    post(act.activation(small[:, 32 + 4 * i:36 + 4 * i], small[:, 32 + 4 * i:36 + 4 * i], ACT.Exp), "s_exped")
                for i in range(2):
                    evac(layer, "cx", i, cx[:, 2 * i:2 * i + 2, :], "c_ready", view=two)
                for i in range(2):
                    evac(layer, "cb", i, cb[:, 2 * i:2 * i + 2, :], "c_ready", view=two)
                for i in range(4):
                    evac(layer, "pt", i, probT[:, i, :], "probT_ready")
                for i in range(2):
                    evac(layer, "pv", i, yaT[:, 2 * i:2 * i + 2, :], "ya_ready", view=two)
                n = 12 * layer
                for h in range(2):
                    for i in range(3):
                        for j in range(2):
                            acc = job_wait(act, layer, f"gate{i}{h}", j)
                            if n >= 2:
                                act.wait_ge(S["sig_used"], n - 1)
                            if n % 12 < 2:
                                act.wait_ge(S["acc_ready"], JOB[layer, "pt", 3][1])
                                act.wait_ge(S["yb_ready"], 2 * layer + 2)
                            for c in range(2):
                                col = ROW_GATE + i * KC + h * 4 + j * 2 + c
                                link(act.activation(sig[:, j, c * T:(c + 1) * T], acc[:, c * T:(c + 1) * T], ACT.Sigmoid,
                                                    bias=vec[:, layer, col:col + 1]))
                            act.sem_inc(free(layer, f"gate{i}{h}", j), 1)
                            act.sem_inc(S["sig_ready"], 1)
                            n += 1
                act.wait_ge(S["merged_ready"], 4 * layer + 4)
                if layer + 1 < L:
                    pass
                for i in range(4):
                    evac(layer, "xk", i, kxT[:, 2 * i:2 * i + 2, :], "kx_ready", view=two)
                for i in range(4):
                    evac(layer, "xv", i, vx[:, i // 2, (i % 2) * 512:(i % 2) * 512 + 512], "vx_ready")
                x_norm(layer, "norm1", 8 + 12 * layer)
                for i in range(4):
                    evac(layer, "xq", i, qxT[:, 2 * i:2 * i + 2, :], "qx_ready", view=two)
                for i in range(4):
                    act.wait_ge(S["xs_shifted"], 4 * layer + i + 1)
                    post(act.activation(xprob[:, i, :], xprob[:, i, :], ACT.Exp), "xs_exped")
                for i in range(4):
                    tb, hp = i // 2, i % 2
                    acc = job_wait(act, layer, "xpt", i)
                    for kb in range(2):
                        link(act.copy(xprobT[:, kb, 2 * hp:2 * hp + 2, tb * P:(tb + 1) * P],
                                      acc.rearrange("p (h b q) -> p h b q", h=2, b=2)[:, :, kb, :]))
                    act.sem_inc(free(layer, "xpt", i), 1)
                    act.sem_inc(S["xprobT_ready"], 1)
                for i in range(4):
                    evac(layer, "xpv", i, oT[:, 2 * i:2 * i + 2, :], "o_ready", view=two)
                x_norm(layer, "norm2", 12 + 12 * layer)
                for i in range(4):
                    evac(layer, "htok", i, htok[:, i // 2, (i % 2) * 512:(i % 2) * 512 + 512], "htok_ready")
                act.wait_ge(S["r_shift"], layer + 1)
                post(act.activation(rt[:, 20, 0:8], rt[:, 20, 0:8], ACT.Exp), "r_exp")
                post(act.activation(rt[:, 21, 0:2], rt[:, 21, 0:2], ACT.Exp), "r_exp")
                if layer + 1 < L:
                    layer_tables(layer + 1)

                def experts(Q, turn, ne):
                    n0 = turn * ne
                    for e in range(ne):
                        act.wait_ge(Q["swt_turned"], n0 + (e + 1))
                        act.copy(swt[:, e, :], psum[:, 6, 0:T]).then_inc(Q["swt_ready"], 1)
                    for r in range(4):
                        act.wait_ge(Q["gathered"], turn * 4 + (r + 1))
                        act.copy(xTe[:, 2 * r:2 * r + 2, 0:ne * SL],
                                 psum[:, 7, :].rearrange("p (c s) -> p c s", c=2)[:, :, 0:ne * SL]).then_inc(Q["xe_ready"], 1)
                    for e in range(ne):
                        act.wait_ge(Q["gu_ready"], n0 + (e + 1))
                        act.activation(sg, psum[:, 4, (e % 2) * T:(e % 2) * T + P], ACT.Silu).then_inc(Q["silu_ready"], 1)
                        act.wait_ge(Q["hid_turned"], n0 + (e + 1))
                        act.copy(hhT, psum[:, 6, T:T + P]).then_inc(Q["hidT_ready"], 1)

                base = layer * TURNS
                with act.Fori(base, base + TURNS) as turn:
                    experts(main_sems, turn, EI)
                act.wait_ge(S["table_ready"], layer + 1)
                count = act.value_load(tabi[0:1, 32:33], min_val=0, max_val=XB)
                with act.If(count > 0):
                    with act.Fori(0, count) as k:
                        experts(extra_sems[layer], k, 1)
            x_norm(L, "norm0", 4 + 12 * L)
            for i in range(4):
                acc = job_wait(act, L, "out", i)
                post(act.copy(arena[:, i * 512:(i + 1) * 512], acc), "out_ready")

        @block.vector
        def _(dve):
            steps = [0]

            def link(ins):
                steps[0] += 1
                ins.then_inc(S["dve_step"], 1)
                dve.wait_ge(S["dve_step"], steps[0])

            def post(ins, stage):
                link(ins)
                dve.sem_inc(S[stage], 1)

            def bc(v, n):
                return v.unsqueeze(2).broadcast_to([P, v.shape[1], n])

            post(dve.memset(zero[:, :], 0.0), "moe_init")
            link(dve.memset(small[:, 95:96], EPS))
            dve.sem_inc(S["eps_ready"], 1)
            link(dve.memset(z[:, :, 0:2], 0.0))
            for i in range(2):
                acc = job_wait(dve, 0, "vec", i)
                post(dve.tensor_copy(vec[:, i, :], acc[:, 0:ROWS]), "vec_ready")
                dve.wait_ge(S["vec_ready"], i + 1)
                dve.sem_inc(free(0, "vec", i), 1)
            dve.wait_ge(S["cst_loaded"], 96)
            ang = cosT[:, :]
            turns_f = sinT[:, :]
            link(dve.tensor_copy(stat[:, 0:T], posrow[:, :]))
            link(dve.tensor_scalar(ang, stat[:, 0:T], inv, None, ALU.mult))
            C1, C2 = 6.28125, 0.0019350051879882812
            C3 = 2 * np.pi - C1 - C2
            for half in range(2):
                dst = stat[:, half * T:(half + 1) * T]
                if half:
                    link(dve.tensor_scalar(turns_f, ang, 1.0 / (2 * np.pi), 0.25, ALU.mult, ALU.add))
                else:
                    link(dve.tensor_scalar(turns_f, ang, 1.0 / (2 * np.pi), None, ALU.mult))
                link(dve.tensor_copy(posrow[:, :], turns_f))
                link(dve.tensor_copy(turns_f, posrow[:, :]))
                link(dve.scalar_tensor_tensor(dst, turns_f, -C1, ang, ALU.mult, ALU.add))
                link(dve.scalar_tensor_tensor(dst, turns_f, -C2, dst, ALU.mult, ALU.add))
                link(dve.scalar_tensor_tensor(dst, turns_f, -C3, dst, ALU.mult, ALU.add))
                if half:
                    link(dve.tensor_scalar(dst, dst, np.pi / 2, None, ALU.add))
                link(dve.tensor_scalar(turns_f, dst, float(np.pi), -2 * np.pi, ALU.is_gt, ALU.mult))
                link(dve.tensor_tensor(dst, dst, turns_f, ALU.add))
                link(dve.tensor_scalar(turns_f, dst, -float(np.pi), 2 * np.pi, ALU.is_lt, ALU.mult))
                link(dve.tensor_tensor(dst, dst, turns_f, ALU.add))
                link(dve.tensor_scalar(dst, dst, 3.1415925, -3.1415925, ALU.min, ALU.max))
                if half:
                    dve.sem_inc(S["angles"], 1)
                    dve.sem_inc(S["angles"], 1)
            dve.wait_ge(S["rope_ready"], 2)

            n_norm = [0]

            def norm(dst, src, col, layer):
                no = n_norm[0]
                dve.wait_ge(S["std_ready"], no + 1)
                link(dve.reciprocal(rstd, std))
                for k in range(KC):
                    if col is None:
                        ins = dve.tensor_tensor(dst[:, k, :], src[:, k, :], rstd, ALU.mult)
                    else:
                        ins = dve.scalar_tensor_tensor(dst[:, k, :], src[:, k, :], vec[:, layer, col + k:col + k + 1], rstd,
                                                       ALU.mult, ALU.mult)
                    post(ins, "h_ready")
                n_norm[0] += 1

            norm(mhatT[:, :, :], mhatT[:, :, :], None, 0)
            dve.sem_inc(S["mem_hat"], 1)
            dve.wait_ge(S["x_ready"], 4)

            n_x = [4]

            def add_x(layer, name, i):
                acc = job_wait(dve, layer, name, i)
                n_x[0] += 1
                dst = xT[:, 2 * i:2 * i + 2, :]
                post(dve.tensor_tensor(dst, dst, acc.rearrange("p (c t) -> p c t", c=2), ALU.add), "x_ready")
                dve.wait_ge(S["x_ready"], n_x[0])
                dve.sem_inc(free(layer, name, i), 1)

            for layer in range(L):
                norm(hT[:, :, :], xT[:, :, :], ROW_MIX, layer)
                if layer:
                    link(dve.memset(z[:, :, 0:2], 0.0))
                link(dve.memset(kbd[:, :, :, :], 0.0))
                cos2 = cosT[:, :].unsqueeze(1).broadcast_to([P, 2, T])
                sin2 = sinT[:, :].unsqueeze(1).broadcast_to([P, 2, T])
                for i in range(3):
                    acc = job_wait(dve, layer, "rot", i).rearrange("p (c t) -> p c t", c=2)
                    raw = qraw[:, 2 * i:2 * i + 2, :] if i < 2 else kraw.rearrange("p (c t) -> p c t", c=2)
                    tmp = stat[:, :].rearrange("p (c t) -> p c t", c=2)
                    link(dve.tensor_tensor(tmp, acc, sin2, ALU.mult))
                    dve.sem_inc(free(layer, "rot", i), 1)
                    dve.wait_ge(S["qraw_ready"], 3 * layer + i + 1)
                    link(dve.tensor_tensor(raw, raw, cos2, ALU.mult))
                    if i < 2:
                        link(dve.tensor_tensor(qT[:, 2 * i:2 * i + 2, :], raw, tmp, ALU.add))
                    else:
                        link(dve.tensor_tensor(kbd[0:64, :, 0, :], raw[0:64], tmp[0:64], ALU.add))
                        link(dve.tensor_tensor(kbd[64:P, :, 1, :], raw[64:P], tmp[64:P], ALU.add))
                    dve.sem_inc(S["qk_ready"], 1)
                dve.wait_ge(S["gelu_ready"], 4 * layer + 4)
                vgv = vg[:, :, :].rearrange("p t (g c) -> p (t g) c", c=P)
                sqv = yaT[:, :, :].rearrange("p c t -> p (c t)").rearrange("p (a c) -> p a c", c=P)
                link(dve.tensor_reduce(small[:, 0:8], vgv, AX.X, ALU.add))
                link(dve.tensor_scalar(small[:, 0:8], small[:, 0:8], 1.0 / P, None, ALU.mult))
                link(dve.tensor_tensor(vgv, vgv, bc(small[:, 0:8], P), ALU.subtract))
                link(dve.tensor_tensor(sqv, vgv, vgv, ALU.mult))
                post(dve.tensor_reduce(small[:, 0:8], sqv, AX.X, ALU.add), "ln_var")
                dve.wait_ge(S["ws_loaded"], 80 * (layer + 1))
                dve.wait_ge(S["ln_std"], layer + 1)
                link(dve.reciprocal(small[:, 16:24], small[:, 8:16]))
                link(dve.tensor_tensor(vgv, vgv, bc(small[:, 16:24], P), ALU.mult))
                link(dve.tensor_tensor(vg[:, :, :], vg[:, :, :], lnt[:, 0:1, :].broadcast_to([P, TB, MW]), ALU.mult))
                post(dve.tensor_tensor(vg[:, :, :], vg[:, :, :], lnt[:, 1:2, :].broadcast_to([P, TB, MW]), ALU.add), "vn_ready")
                dve.wait_ge(S["ws_ready"], layer + 1)
                link(dve.memset(wsT[64:P, :, 0:64], 0.0))
                dve.sem_inc(S["ws_ready"], 1) if False else dve.sem_inc(S["ws_used"], 1)
                for i in range(4):
                    g, p = i // 2, i % 2
                    acc = job_wait(dve, layer, "s", i).rearrange("p (h k) -> p h k", h=4)
                    mx = small[:, 24:28]
                    if p == 0:
                        link(dve.memset(acc[0:64, :, 64:P], NEG))
                    link(dve.tensor_reduce(mx, acc, AX.X, ALU.max))
                    link(dve.scalar_tensor_tensor(mx, mx, 0.125, sinks[:, layer, 4 * g:4 * g + 4], ALU.mult, ALU.max))
                    link(dve.tensor_tensor(small[:, 32 + 4 * i:36 + 4 * i], sinks[:, layer, 4 * g:4 * g + 4], mx, ALU.subtract))
                    link(dve.scalar_tensor_tensor(prob[:, i], acc, 0.125, bc(mx, P), ALU.mult, ALU.subtract))
                    dve.sem_inc(free(layer, "s", i), 1)
                    dve.sem_inc(S["s_shifted"], 1)
                for i in range(4):
                    dve.wait_ge(S["s_exped"], 8 * layer + 2 * i + 2)
                    link(dve.tensor_reduce(small[:, 24:28], prob[:, i], AX.X, ALU.add))
                    link(dve.tensor_tensor(small[:, 24:28], small[:, 24:28], small[:, 32 + 4 * i:36 + 4 * i], ALU.add))
                    link(dve.reciprocal(small[:, 24:28], small[:, 24:28]))
                    post(dve.tensor_tensor(prob[:, i], prob[:, i], bc(small[:, 24:28], P), ALU.mult), "prob_ready")
                dve.wait_ge(S["c_ready"], 4 * layer + 4)
                for i in range(2):
                    acc = job_wait(dve, layer, "cc", i)
                    link(dve.tensor_tensor(z[:, 2 * i:2 * i + 2, 2:T + 2], cx[:, 2 * i:2 * i + 2, :],
                                           acc.rearrange("p (c t) -> p c t", c=2), ALU.mult))
                    dve.sem_inc(free(layer, "cc", i), 1)
                for c in range(MC):
                    w = [vec[:, layer, ROW_CONV + 4 * k + c:ROW_CONV + 4 * k + c + 1] for k in range(3)]
                    link(dve.tensor_scalar(ycT[:, c, :], z[:, c, 0:T], w[0], None, ALU.mult))
                    link(dve.scalar_tensor_tensor(ycT[:, c, :], z[:, c, 1:T + 1], w[1], ycT[:, c, :], ALU.mult, ALU.add))
                    link(dve.scalar_tensor_tensor(ycT[:, c, :], z[:, c, 2:T + 2], w[2], ycT[:, c, :], ALU.mult, ALU.add))
                post(dve.tensor_tensor(ycT[:, :, :], ycT[:, :, :], cb[:, :, :], ALU.mult), "yc_ready")
                for tb in range(TB):
                    acc = job_wait(dve, layer, "mixed", tb)
                    link(dve.tensor_tensor(ybT[:, :, tb * P:(tb + 1) * P], uT[:, :, tb * P:(tb + 1) * P],
                                           acc.rearrange("p (g i) -> p g i", g=4), ALU.mult))
                    dve.sem_inc(free(layer, "mixed", tb), 1)
                    dve.sem_inc(S["yb_ready"], 1)
                n = 12 * layer
                for h in range(2):
                    for i in range(3):
                        for j in range(2):
                            acc = job_wait(dve, layer, f"br{i}{h}", j)
                            dve.wait_ge(S["sig_ready"], n + 1)
                            c0 = 4 * h + 2 * j
                            dst = merged[:, c0:c0 + 2, :].rearrange("p c t -> p (c t)")
                            if i == 0:
                                link(dve.tensor_tensor(dst, sig[:, j, :], acc, ALU.mult))
                            else:
                                link(dve.tensor_tensor(gtmp, sig[:, j, :], acc, ALU.mult))
                                link(dve.tensor_tensor(dst, dst, gtmp, ALU.add))
                            dve.sem_inc(free(layer, f"br{i}{h}", j), 1)
                            dve.sem_inc(S["sig_used"], 1)
                            if i == 2:
                                dve.sem_inc(S["merged_ready"], 1)
                            n += 1
                for i in range(4):
                    add_x(layer, "wo", i)
                norm(hT[:, :, :], xT[:, :, :], ROW_XN, layer)
                for i in range(4):
                    acc = job_wait(dve, layer, "xs", i).rearrange("p (h k) -> p h k", h=2)
                    mx = small[:, 24:26]
                    buf = xprob[:, i, :].rearrange("p (h k) -> p h k", h=2)
                    link(dve.tensor_reduce(mx, acc, AX.X, ALU.max))
                    link(dve.tensor_scalar(mx, mx, 0.0625, None, ALU.mult))
                    link(dve.scalar_tensor_tensor(buf, acc, 0.0625, bc(mx, T), ALU.mult, ALU.subtract))
                    dve.sem_inc(free(layer, "xs", i), 1)
                    dve.sem_inc(S["xs_shifted"], 1)
                for i in range(4):
                    buf = xprob[:, i, :].rearrange("p (h k) -> p h k", h=2)
                    dve.wait_ge(S["xs_exped"], 4 * layer + i + 1)
                    link(dve.tensor_reduce(small[:, 24:26], buf, AX.X, ALU.add))
                    link(dve.reciprocal(small[:, 24:26], small[:, 24:26]))
                    post(dve.tensor_tensor(buf, buf, bc(small[:, 24:26], T), ALU.mult), "xprob_ready")
                for i in range(4):
                    add_x(layer, "xo", i)
                norm(hT[:, :, :], xT[:, :, :], ROW_FF, layer)
                acc = job_wait(dve, layer, "router")
                link(dve.tensor_tensor(logit[:, :, :], acc[:, 0:TB * (NG + NE)].rearrange("p (t n) -> p t n", t=TB),
                                       rbias[:, layer:layer + 1, :].broadcast_to([P, TB, NG + NE]), ALU.add))
                dve.sem_inc(free(layer, "router"), 1)
                gm, ge, gi = rt[:, 0, 0:2], rt[:, 1, 0:8].rearrange("p (t n) -> p t n", t=2), rt[:, 2, 0:2]
                ex = rt[:, 20, 0:8].rearrange("p (t n) -> p t n", t=2)
                gl, el = logit[:, :, 0:NG], logit[:, :, NG:]

                def first_max(values, n, best, onehot, where):
                    io = iota[:, 0:n].unsqueeze(1).broadcast_to([P, TB, n])
                    link(dve.tensor_reduce(best, values, AX.X, ALU.max))
                    link(dve.tensor_tensor(onehot, values, bc(best, n), ALU.is_lt))
                    link(dve.scalar_tensor_tensor(onehot, onehot, 1000.0, io, ALU.mult, ALU.add))
                    link(dve.tensor_reduce(where, onehot, AX.X, ALU.min))
                    link(dve.tensor_tensor(onehot, io, bc(where, n), ALU.is_equal))

                first_max(gl, NG, gm, ge, gi)
                link(dve.tensor_tensor(ex, gl, bc(gm, NG), ALU.subtract))
                lem = rt[:, 4:6, :]
                oh1, oh2 = rt[:, 6:8, :], rt[:, 8:10, :]
                t1, t2, wi = rt[:, 10, 0:2], rt[:, 11, 0:2], rt[:, 12, 0:2]
                off = rt[:, 13, 0:8].rearrange("p (t n) -> p t n", t=2)
                link(dve.tensor_scalar(off, ge, -NEG, NEG, ALU.mult, ALU.add))
                for tb in range(TB):
                    e4 = el[:, tb, :].rearrange("p (g e) -> p g e", g=NG)
                    l4 = lem[:, tb, :].rearrange("p (g e) -> p g e", g=NG)
                    link(dve.tensor_tensor(l4, e4, bc(ge[:, tb, :], EPG), ALU.mult))
                    link(dve.tensor_tensor(l4, l4, bc(off[:, tb, :], EPG), ALU.add))
                first_max(lem, NE, t1, oh1, wi)
                link(dve.scalar_tensor_tensor(lem, oh1, 2 * NEG, lem, ALU.mult, ALU.add))
                first_max(lem, NE, t2, oh2, wi)
                link(dve.tensor_tensor(rt[:, 21, 0:2], t2, t1, ALU.subtract))
                dve.sem_inc(S["r_shift"], 1)
                post(dve.tensor_tensor(mask[:, :, :], oh1, oh2, ALU.add), "mask_ready")
                dve.wait_ge(S["r_exp"], 2 * layer + 2)
                gs, w1, w2 = rt[:, 14, 0:2], rt[:, 15, 0:2], rt[:, 16, 0:2]
                link(dve.tensor_reduce(gs, ex, AX.X, ALU.add))
                link(dve.tensor_scalar(w1, rt[:, 21, 0:2], 1.0, None, ALU.add))
                link(dve.tensor_tensor(w1, w1, gs, ALU.mult))
                link(dve.reciprocal(w1, w1))
                link(dve.tensor_tensor(w2, w1, rt[:, 21, 0:2], ALU.mult))
                link(dve.tensor_tensor(oh1, oh1, bc(w1, NE), ALU.mult))
                link(dve.tensor_tensor(oh2, oh2, bc(w2, NE), ALU.mult))
                link(dve.tensor_tensor(wtok[:, :, :], oh1, oh2, ALU.add))
                acc = job_wait(dve, layer, "place")
                pl = acc[:, 0:TB * NE].rearrange("p (t n) -> p t n", t=TB)
                dve.wait_ge(S["mask_ready"], layer + 1)
                link(dve.scalar_tensor_tensor(place[:, :, :], pl, 1.0, mask[:, :, :], ALU.add, ALU.mult))
                link(dve.tensor_scalar(place[:, :, :], place[:, :, :], -1.0, None, ALU.add))
                link(dve.tensor_scalar(tab[0:NE, 0:7], thr[0:NE], acc[0:NE, 64:65], None, ALU.is_lt))
                dve.sem_inc(free(layer, "place"), 1)
                link(dve.tensor_reduce(tab[0:NE, 8:9], tab[0:NE, 0:7], AX.X, ALU.add))
                dve.sem_inc(S["extra_ready"], 1)
                acc = job_wait(dve, layer, "start")
                link(dve.tensor_copy(tab[0:NE, 9:10], acc[0:NE, 0:1]))
                dve.sem_inc(free(layer, "start"), 1)
                link(dve.tensor_tensor(tab[0:NE, 10:11], tab[0:NE, 9:10], tab[0:NE, 8:9], ALU.add))
                link(dve.tensor_scalar(tab[0:NE, 32:48], iota[0:NE, 0:16], tab[0:NE, 9:10], None, ALU.is_ge))
                link(dve.tensor_scalar(tab[0:NE, 48:64], iota[0:NE, 0:16], tab[0:NE, 10:11], None, ALU.is_lt))
                link(dve.tensor_tensor(tab[0:NE, 48:64], tab[0:NE, 48:64], tab[0:NE, 32:48], ALU.mult))
                link(dve.tensor_scalar(tab[0:NE, 16:32], iota[0:NE, 0:16], tab[0:NE, 9:10], 1.0, ALU.subtract, ALU.add))
                link(dve.tensor_tensor(tab[0:NE, 16:32], tab[0:NE, 16:32], tab[0:NE, 48:64], ALU.mult))
                link(dve.tensor_scalar(tab[0:NE, 0:8], iota[0:NE, 0:8], 0.0, None, ALU.mult))
                link(dve.tensor_scalar(tab[0:NE, 32:48], tab[0:NE, 48:64], idx[0:NE], None, ALU.mult))
                dve.sem_inc(S["span_ready"], 1)
                acc = job_wait(dve, layer, "table")
                link(dve.tensor_copy(tabi[0:1, 0:33], acc[0:1, 0:33]))
                dve.sem_inc(free(layer, "table"), 1)
                dve.sem_inc(S["table_ready"], 1)

                def experts(Q, turn, ne, build):
                    n0 = turn * ne
                    dve.wait_ge(Q["sel_used"], turn + 1)
                    build()
                    for e in range(ne):
                        dve.wait_ge(Q["silu_ready"], n0 + (e + 1))
                        dve.tensor_tensor(hh, sg, psum[:, 4, (e % 2) * T + P:(e % 2) * T + T], ALU.mult).then_inc(Q["hid_ready"], 1)
                        dve.wait_ge(Q["y_done"], n0 + (e + 1))
                        dve.tensor_copy(ysb, psum[:, 5, 0:T]).then_inc(Q["y_ready"], 1)

                base = layer * TURNS
                with dve.Fori(base, base + TURNS) as turn:
                    def build():
                        Q = main_sems
                        io = iota[:, 0:SL].unsqueeze(1).broadcast_to([P, EI, SL])
                        at = (turn - base) * EI
                        for tb in range(TB):
                            dve.tensor_tensor(sel[:, tb], bc(place[:, tb, bass.ds(at, EI)], SL), io,
                                              ALU.is_equal).then_inc(Q["sel_ready"], 1)
                        for tb in range(TB):
                            dve.wait_ge(Q["sel_ready"], turn * 4 + (tb * 2 + tb + 2 - tb * 2))
                            four = selw[:, tb].rearrange("p e (j s) -> p e j s", j=4)
                            w = wtok[:, tb, bass.ds(at, EI)].unsqueeze(2).unsqueeze(3).broadcast_to([P, EI, 4, SL])
                            dve.tensor_tensor(four, w, sel[:, tb].unsqueeze(2).broadcast_to([P, EI, 4, SL]), ALU.mult).then_inc(Q["sel_ready"], 1)
                    experts(main_sems, turn, EI, build)
                count = dve.value_load(tabi[0:1, 32:33], min_val=0, max_val=XB)
                with dve.If(count > 0):
                    with dve.Fori(0, count) as k:
                        e = dve.value_load(tabi[0:1, bass.ds(k, 1)], min_val=0, max_val=NE - 1)
                        b = dve.value_load(tabi[0:1, bass.ds(k + 16, 1)], min_val=0, max_val=7)

                        def build():
                            Q = extra_sems[layer]
                            for tb in range(TB):
                                dve.tensor_tensor(sel[:, tb, 0, :], place[:, tb, bass.ds(e, 1)].broadcast_to([P, SL]),
                                                  iota[:, bass.ds(b * SL, SL)], ALU.is_equal).then_inc(Q["sel_ready"], 1)
                            for tb in range(TB):
                                dve.wait_ge(Q["sel_ready"], k * 4 + (tb + 2))
                                four = selw[:, tb, 0, :].rearrange("p (j s) -> p j s", j=4)
                                w = wtok[:, tb, bass.ds(e, 1)].unsqueeze(2).broadcast_to([P, 4, SL])
                                dve.tensor_tensor(four, w, sel[:, tb, 0:1, :].broadcast_to([P, 4, SL]), ALU.mult).then_inc(Q["sel_ready"], 1)
                        experts(extra_sems[layer], k, 1, build)
                for i in range(4):
                    add_x(layer, "moe", i)
            norm(hT[:, :, :], xT[:, :, :], ROW_FIN, 0)

        @block.tensor
        def _(pe):
            def done(ins):
                ins.then_inc(S["acc_ready"], 1)

            def turn_in(name, src, loaded):
                pe.wait_ge(S[loaded], 16)
                for i in range(4):
                    acc = job_begin(pe, 0, name, i)
                    for c in range(2):
                        for tb in range(TB):
                            d = (2 * i + c) * P
                            ins = pe.transpose(acc[:, c * T + tb * P:c * T + (tb + 1) * P], src[:, tb, d:d + P], ident)
                    done(ins)

            pe.wait_ge(S["cst_loaded"], 96)
            turn_in("x", arena[:, 0:2048].rearrange("p (t d) -> p t d", t=TB), "x_loaded")
            turn_in("mem", arena[:, 2048:4096].rearrange("p (t d) -> p t d", t=TB), "mem_loaded")
            for layer in range(L):
                pe.wait_ge(small_loads[layer], 16 * 7)
                acc = job_begin(pe, 0, "vec", layer)
                done(pe.transpose(acc[:, 0:ROWS], vecrows[:, layer, :], ident[0:ROWS, 0:ROWS]))
            pe.wait_ge(S["pool_step"], 1)

            n_norm = [0]

            def norm(layer, name):
                pe.wait_ge(S["sq_ready"], n_norm[0] + 1)
                acc = job_begin(pe, layer, name)
                for k in range(KC):
                    ins = pe.matmul(acc[:, 0:T], ones[:, :], hT[:, k, :], start=k == 0, stop=k == KC - 1)
                done(ins)
                n_norm[0] += 1

            norm(0, "memnorm")

            def h_wait():
                pe.wait_ge(S["h_ready"], KC * n_norm[0])

            def unit(layer, name, words, k):
                u = unit_no(layer, name)
                pe.wait_ge(slot_loaded[u % R], 16 * (u // R + 1))
                return ring[:, u % R, 0:words].rearrange("p (k n) -> p k n", k=k)

            def project(layer, job, i, w, cols, rhs, kc, out=None):
                acc = job_begin(pe, layer, job, i)
                for c, at in enumerate(cols):
                    for k in range(kc):
                        ins = pe.matmul(acc[:, c * T:(c + 1) * T], w[:, k, at:at + P], rhs[:, k, :],
                                        start=k == 0, stop=k == kc - 1)
                return ins

            def dense(layer, name, job, rhs, kc=KC, i0=0):
                w = unit(layer, name, kc * 512, kc)
                for i in range(2):
                    ins = project(layer, job, i0 + i, w, [2 * i * P, 2 * i * P + P], rhs, kc)
                    done(ins)
                release()

            def release():
                pe.drain().then_inc(S["units_used"], 1)

            for layer in range(L):
                norm(layer, "norm0")
                h_wait()
                dense(layer, "q", "q", hT)
                wkv = unit(layer, "kv", KC * 256, KC)
                acc = job_begin(pe, layer, "k")
                for g in range(2):
                    for half in range(2):
                        for k in range(KC):
                            ins = pe.matmul(acc[half * 64:half * 64 + 64, g * T:(g + 1) * T], wkv[:, k, g * 64:g * 64 + 64],
                                            hT[:, k, :], start=k == 0, stop=k == KC - 1)
                done(ins)
                acc = job_begin(pe, layer, "v")
                for tb in range(TB):
                    for k in range(KC):
                        ins = pe.matmul(acc[:, tb * P:(tb + 1) * P], hT[:, k, tb * P:(tb + 1) * P], wkv[:, k, P:2 * P],
                                        start=k == 0, stop=k == KC - 1)
                done(ins)
                release()
                dense(layer, "u", "u", hT)
                pe.wait_ge(S["qraw_ready"], 3 * layer + 3)
                for i in range(3):
                    acc = job_begin(pe, layer, "rot", i)
                    src = qraw[:, 2 * i:2 * i + 2, :].rearrange("p c t -> p (c t)") if i < 2 else kraw
                    done(pe.matmul(acc, rotm, src, start=True, stop=True))
                w = unit(layer, "vg", KC * 512, KC)
                for tb in range(TB):
                    acc = job_begin(pe, layer, "vg", tb)
                    for k in range(KC):
                        ins = pe.matmul(acc, hT[:, k, tb * P:(tb + 1) * P], w[:, k, :], start=k == 0, stop=k == KC - 1)
                    done(ins)
                release()
                pe.wait_ge(S["ws_loaded"], 80 * (layer + 1))
                acc = job_begin(pe, layer, "ws")
                for g in range(4):
                    ins = pe.transpose(acc[:, g * P:(g + 1) * P], wsr[:, g, :], ident)
                done(ins)
                pe.wait_ge(S["qk_ready"], 3 * layer + 3)
                for i in range(4):
                    g, p = i // 2, i % 2
                    acc = job_begin(pe, layer, "s", i).rearrange("p (h k) -> p h k", h=4)
                    for half in range(2):
                        c = 2 * p + half
                        for hp in range(2):
                            q = qT[:, 2 * g + hp, c * 64:(c + 1) * 64]
                            rows = slice(half * 64, half * 64 + 64)
                            wins = [(0, 128, 64), (64, 64, 64)] if c == 2 else [(0, (0, 0, None, 128)[c], 128)]
                            for at, first, n in wins:
                                ins = pe.matmul(acc[rows, 2 * hp:2 * hp + 2, at:at + n], q, kbd[:, g, :, first:first + n],
                                                start=True, stop=True)
                    done(ins)
                dense(layer, "cx", "cx", hT)
                dense(layer, "cb", "cb", hT)
                for i in range(4):
                    pe.wait_ge(S["prob_ready"], 4 * layer + i + 1)
                    acc = job_begin(pe, layer, "pt", i)
                    for h in range(4):
                        ins = pe.transpose(acc[:, h * P:(h + 1) * P], prob[:, i, h, :], ident)
                    done(ins)
                dense(layer, "cc", "cc", hT)
                pe.wait_ge(S["v_ready"], 3 * layer + 3)
                pe.wait_ge(S["probT_ready"], 4 * layer + 4)
                for g in range(2):
                    acc = job_begin(pe, layer, "pv", g).rearrange("p (c t) -> p c t", c=2)
                    for c in range(4):
                        v = vtok[:, (0, 0, 2, 1)[c], g * 64:g * 64 + 64]
                        pt = probT[:, 2 * g + c // 2, :].rearrange("p (a b q) -> p a b q", a=2, b=2)
                        for par in range(2):
                            ins = pe.matmul(acc[par * 64:par * 64 + 64, :, c * 64:(c + 1) * 64], v,
                                            pt[:, :, par, (c % 2) * 64:(c % 2) * 64 + 64], start=True, stop=True)
                    done(ins)
                pe.wait_ge(S["vn_ready"], layer + 1)
                pe.wait_ge(S["ws_used"], layer + 1)
                for tb in range(TB):
                    acc = job_begin(pe, layer, "mixed", tb)
                    pe.matmul(acc, ones[0:1, :], bs[0:1, layer, :], start=True, stop=False, skip_group_check=True)
                    for g in range(4):
                        ins = pe.matmul(acc[:, g * P:(g + 1) * P], vg[:, tb, g * P:(g + 1) * P], wsT[:, g, :],
                                        start=False, stop=g == 3, skip_group_check=True)
                    done(ins)
                for h in range(2):
                    for i in range(3):
                        dense(layer, f"gate{i}{h}", f"gate{i}{h}", hT)
                        if h == 0:
                            pe.wait_ge(S[("ya_ready", "yb_ready", "yc_ready")[i]], (2, 2, 1)[i] * (layer + 1))
                        dense(layer, f"br{i}{h}", f"br{i}{h}", (yaT, ybT, ycT)[i], kc=MC)
                pe.wait_ge(S["merged_ready"], 4 * layer + 4)
                for h in range(2):
                    dense(layer, f"wo{h}", "wo", merged, i0=2 * h)
                pe.wait_ge(S["mem_scaled"], KC * (layer + 1))
                for h in range(2):
                    dense(layer, f"xk{h}", "xk", mT, i0=2 * h)
                ws = [unit(layer, "xv0", KC * 512, KC), unit(layer, "xv1", KC * 512, KC)]
                for i in range(4):
                    tb, h = i // 2, i % 2
                    acc = job_begin(pe, layer, "xv", i)
                    for k in range(KC):
                        ins = pe.matmul(acc, mT[:, k, tb * P:(tb + 1) * P], ws[h][:, k, :], start=k == 0, stop=k == KC - 1)
                    done(ins)
                release()
                release()
                norm(layer, "norm1")
                h_wait()
                for h in range(2):
                    dense(layer, f"xq{h}", "xq", hT, i0=2 * h)
                pe.wait_ge(S["kx_ready"], 4 * layer + 4)
                pe.wait_ge(S["qx_ready"], 4 * layer + 4)
                for i in range(4):
                    tb, hp = i // 2, i % 2
                    acc = job_begin(pe, layer, "xs", i)
                    for h in range(2):
                        for k in range(2):
                            c = 2 * (2 * hp + h) + k
                            ins = pe.matmul(acc[:, h * T:(h + 1) * T], qxT[:, c, tb * P:(tb + 1) * P], kxT[:, c, :],
                                            start=k == 0, stop=k == 1)
                    done(ins)
                for i in range(4):
                    pe.wait_ge(S["xprob_ready"], 4 * layer + i + 1)
                    acc = job_begin(pe, layer, "xpt", i)
                    for j in range(4):
                        ins = pe.transpose(acc[:, j * P:(j + 1) * P], xprob[:, i, j * P:(j + 1) * P], ident)
                    done(ins)
                pe.wait_ge(S["xprobT_ready"], 4 * layer + 4)
                pe.wait_ge(S["vx_ready"], 4 * layer + 4)
                for h in range(4):
                    acc = job_begin(pe, layer, "xpv", h)
                    for c in range(2):
                        for kb in range(2):
                            ins = pe.matmul(acc[:, c * T:(c + 1) * T], vx[:, kb, (2 * h + c) * P:(2 * h + c + 1) * P],
                                            xprobT[:, kb, h, :], start=kb == 0, stop=kb == 1)
                    done(ins)
                pe.wait_ge(S["o_ready"], 4 * layer + 4)
                for h in range(2):
                    dense(layer, f"xo{h}", "xo", oT, i0=2 * h)
                norm(layer, "norm2")
                h_wait()
                for i in range(4):
                    tb, half = i // 2, i % 2
                    acc = job_begin(pe, layer, "htok", i)
                    for c in range(4):
                        ins = pe.transpose(acc[:, c * P:(c + 1) * P], hT[:, 4 * half + c, tb * P:(tb + 1) * P], ident)
                    done(ins)
                acc = job_begin(pe, layer, "router")
                for tb in range(TB):
                    for k in range(KC):
                        ins = pe.matmul(acc[:, tb * (NG + NE):(tb + 1) * (NG + NE)], hT[:, k, tb * P:(tb + 1) * P], wr[:, k, :],
                                        start=k == 0, stop=k == KC - 1)
                done(ins)
                pe.wait_ge(S["mask_ready"], layer + 1)
                acc = job_begin(pe, layer, "place")
                pe.matmul(acc[:, 0:NE], tri, mask[:, 0, :], start=True, stop=True)
                pe.matmul(acc[:, NE:2 * NE], tri, mask[:, 1, :], start=True, stop=False)
                pe.matmul(acc[:, NE:2 * NE], ones[:, :], mask[:, 0, :], start=False, stop=True)
                pe.matmul(acc[0:NE, 64:65], mask[:, 0, :], ones[:, 0:1], start=True, stop=False)
                done(pe.matmul(acc[0:NE, 64:65], mask[:, 1, :], ones[:, 0:1], start=False, stop=True))
                pe.wait_ge(S["extra_ready"], layer + 1)
                acc = job_begin(pe, layer, "start")
                done(pe.matmul(acc[0:NE, 0:1], tri[0:NE, 0:NE], tab[0:NE, 8:9], start=True, stop=True))
                pe.wait_ge(S["span_ready"], layer + 1)
                acc = job_begin(pe, layer, "table")
                pe.matmul(acc[0:1, 0:16], ones[0:NE, 0:1], tab[0:NE, 32:48], start=True, stop=True)
                pe.matmul(acc[0:1, 16:32], ones[0:NE, 0:1], tab[0:NE, 16:32], start=True, stop=True)
                done(pe.matmul(acc[0:1, 32:33], ones[0:NE, 0:1], tab[0:NE, 8:9], start=True, stop=True))
                any2 = iota.unsqueeze(1).broadcast_to([P, 2, T])
                pe.wait_ge(S["moe_init"], 1)
                for j in range(4):
                    acc = job_begin(pe, layer, "moe", j)
                    row = slice(32 * j, 32 * j + 1)
                    pe.matmul(acc, zero[row, :], any2[row], start=True, stop=False, skip_group_check=True,
                              tile_position=(32 * j, 0))
                pe.wait_ge(S["htok_ready"], 4 * layer + 4)

                def experts(Q, turn, ne, slot_wait, slot_done, slot):
                    n0 = turn * ne
                    sel_n = turn * 4 + 4
                    pe.wait_ge(Q["sel_ready"], sel_n)
                    for e in range(ne):
                        if e:
                            pe.wait_ge(Q["swt_ready"], n0 + e)
                        for tb in range(TB):
                            ins = pe.transpose(psum[:, 6, tb * P:(tb + 1) * P], selw[:, tb, e, :], ident)
                        ins.then_inc(Q["swt_turned"], 1)
                    for r in range(4):
                        if r:
                            pe.wait_ge(Q["xe_ready"], turn * 4 + r)
                        for c in range(2):
                            for tb in range(TB):
                                d = (2 * r + c) * P
                                ins = pe.matmul(psum[:, 7, c * T:c * T + ne * SL], htok[:, tb, d:d + P],
                                                sel[:, tb, 0:ne, :].rearrange("p e s -> p (e s)"), start=tb == 0, stop=tb == 1)
                        ins.then_inc(Q["gathered"], 1)
                    pe.wait_ge(Q["xe_ready"], turn * 4 + 4)
                    pe.wait_ge(Q["swt_ready"], n0 + ne)
                    for e in range(ne):
                        G = psum[:, 4, (e % 2) * T:(e % 2) * T + T]
                        for k in range(KC):
                            if k % 4 == 0:
                                slot_wait(e, k // 4)
                            w = ring[:, slot(e, k // 4), :].rearrange("p (k a b) -> p k a b", k=4, a=2)
                            for j in range(4):
                                ins = pe.matmul(G[32 * j:32 * j + 32, :], xTe[:, k, e * SL:(e + 1) * SL],
                                                w[:, k % 4, :, j * P:(j + 1) * P], start=k == 0, stop=k == KC - 1,
                                                tile_position=(0, 32 * j))
                                if e == 0 and k == 0 and j == 0:
                                    ins.then_inc(Q["sel_used"], 1)
                            if k == 3:
                                slot_done(ins)
                        ins.then_inc(Q["gu_ready"], 1)
                        pe.wait_ge(Q["hid_ready"], n0 + (e + 1))
                        pe.transpose(psum[:, 6, T:T + P], hh, ident).then_inc(Q["hid_turned"], 1)
                        pe.wait_ge(Q["hidT_ready"], n0 + (e + 1))
                        slot_wait(e, 2)
                        w = ring[:, slot(e, 2), :].rearrange("p (k n) -> p k n", k=4)
                        for k in range(4):
                            for j in range(4):
                                ins = pe.matmul(psum[32 * j:32 * j + 32, 5, 0:T], hhT[:, k * SL:(k + 1) * SL],
                                                w[:, k, j * T:(j + 1) * T], start=k == 0, stop=k == 3, tile_position=(0, 32 * j))
                                if k == 0 and j == 0:
                                    slot_done(ins)
                        ins.then_inc(Q["y_done"], 1)
                        pe.wait_ge(Q["y_ready"], n0 + (e + 1))
                        for c in range(2):
                            for j in range(4):
                                ins = pe.matmul(psum[:, j, c * T:(c + 1) * T], ysb[32 * j:32 * j + 32, c * P:(c + 1) * P],
                                                swt[32 * j:32 * j + 32, e, :], start=False, stop=False,
                                                skip_group_check=True, tile_position=(32 * j, 0))
                                if c == 0 and j == 0:
                                    slot_done(ins)
                    return ins

                base = layer * TURNS
                pe.drain().then_inc(main_sems["sel_used"], 1) if layer == 0 else None
                u0 = layer * PER_LAYER + DENSE
                with pe.Fori(base, base + TURNS) as turn:
                    def slot(e, x):
                        return (u0 + 3 * e + x) % R

                    def slot_wait(e, x):
                        u = u0 + 3 * e + x
                        per = 3 * EI // R
                        pe.wait_ge(slot_loaded[u % R], turn * (16 * per) + 16 * (u // R + 1 - base * per))

                    def slot_done(ins):
                        ins.then_inc(S["units_used"], 1)
                    experts(main_sems, turn, EI, slot_wait, slot_done, slot)
                X = extra_sems[layer]
                pe.drain().then_inc(X["sel_used"], 1)
                pe.drain().then_inc(X["used"], 1)
                pe.wait_ge(S["table_ready"], layer + 1)
                count = pe.value_load(tabi[0:1, 32:33], min_val=0, max_val=XB)
                u1 = (layer + 1) * PER_LAYER
                with pe.If(count > 0):
                    with pe.Fori(0, count) as k:
                        def slot(e, x):
                            return (u1 + x) % R

                        def slot_wait(e, x):
                            pe.wait_ge(X["loaded"], k * 48 + 48)

                        def slot_done(ins):
                            pass
                        experts(X, k, 1, slot_wait, slot_done, slot).then_inc(X["used"], 1)
                for j in range(4):
                    row = slice(32 * j, 32 * j + 1)
                    done(pe.matmul(psum[:, j, :], zero[row, :], any2[row], start=False, stop=True, skip_group_check=True,
                                   tile_position=(32 * j, 0)))
            norm(L, "norm0")
            h_wait()
            for i in range(4):
                acc = job_begin(pe, L, "out", i)
                for c in range(4):
                    ins = pe.transpose(acc[:, c * P:(c + 1) * P], hT[:, 4 * (i % 2) + c, (i // 2) * P:(i // 2 + 1) * P], ident)
                done(ins)


_INS = ['x', 'mem', 'positions', 'mix_norm', 'w_in', 'b_gate', 'attn_sinks', 'gmlp_ln_g', 'gmlp_ln_b',
        'gmlp_w_s', 'gmlp_b_s', 'conv_w', 'w_branch', 'w_out', 'xattn_norm', 'mem_norm', 'w_xq', 'w_xkv',
        'w_xo', 'ffn_norm', 'w_router_group', 'b_router_group', 'w_router_expert', 'b_router_expert',
        'w_expert_in', 'w_expert_out', 'final_norm']


def constants():
    c = np.zeros((P, C_END), np.float32)
    p = np.arange(P)
    c[:, C_ID:C_ID + P] = np.eye(P)
    c[:, C_TRI:C_TRI + P] = p[:, None] < p[None, :]
    for m in range(P):
        if m % 64 < 32:
            c[m + 32, C_ROT + m] = -1.0
        else:
            c[m - 32, C_ROT + m] = 1.0
    half = 32
    inv = np.power(np.float32(10000.0), -np.arange(half, dtype=np.float32) / np.float32(half)).astype(np.float32)
    c[:, C_INV] = inv[p % half]
    c[:, C_IOTA:C_IOTA + T] = np.arange(T)
    c[:, C_IDX] = p
    c[:, C_THR:C_THR + 7] = SL * np.arange(1, 8)
    return c


def kernel(**inputs):
    import concourse.bacc as bacc
    from concourse.bass_utils import run_bass_kernel_spmd

    nc = bacc.Bacc("TRN2", target_bir_lowering=False, num_devices=1)
    arrays, aps = {}, {}
    for name in _INS:
        a = np.ascontiguousarray(inputs[name])
        arrays[f"in_{name}"] = a
        aps[name] = nc.dram_tensor(f"in_{name}", a.shape, mybir.dt.from_np(a.dtype), kind="ExternalInput").ap()
    arrays["in_cst"] = constants()
    aps["cst"] = nc.dram_tensor("in_cst", (P, C_END), F32, kind="ExternalInput").ap()
    out = nc.dram_tensor("out", (1, T, D), F32, kind="ExternalOutput").ap()
    trunk(nc, aps, out)
    r = run_bass_kernel_spmd(nc, [arrays], core_ids=[0])
    return r.results[0]["out"]
```

```python
from contextlib import ExitStack

import numpy as np

import concourse.bass as bass
from concourse import mybir

F32 = mybir.dt.float32
F32R = mybir.dt.float32r
I32 = mybir.dt.int32
ALU = mybir.AluOpType
ACT = mybir.ActivationFunctionType
AX = mybir.AxisListType

P = 128
D = 1024
T = 256
L = 2
KC = D // P
TB = T // P
MW = 512
MC = MW // P
NE = 32
NG = 4
EPG = NE // NG
SL = 32
XB = (2 * T) // SL - 1
EPS = 1e-6
NEG = -1e30
R = 6
UNIT = 4096
EI = 8
TURNS = NE // EI

ROW_MIX, ROW_GATE, ROW_CONV, ROW_XN, ROW_MN, ROW_FF, ROW_FIN = 0, 8, 32, 44, 52, 60, 68
ROWS = 76
C_ID, C_TRI, C_ROT, C_SWAP, C_RSW, C_INV, C_IOTA, C_IDX, C_THR, C_END = 0, 128, 256, 384, 512, 640, 641, 897, 898, 905

KV_UNITS = ["xk0", "xk1", "xv0", "xv1"]
MIX_UNITS = (["q", "kv", "u", "vg", "cx", "cb", "cc"]
             + [f"{n}{i}{h}" for h in range(2) for i in range(3) for n in ("gate", "br")]
             + ["wo0", "wo1", "xq0", "xq1", "xo0", "xo1"])


def plan_units():
    number, first_expert, pieces, at = {}, [], [], 0
    for layer in range(L):
        names = [(layer, n) for n in (KV_UNITS if layer == 0 else []) + MIX_UNITS]
        names += [(layer + 1, n) for n in KV_UNITS if layer + 1 < L]
        for key in names:
            number[key] = at
            at += 1
            pieces += [key + (h,) for h in range(1 if key[1] == "kv" else 2)]
        first_expert.append(at)
        at += 3 * NE
    return number, first_expert, pieces


UNIT_NO, FIRST_EXPERT, PIECES = plan_units()
PIECE_NO = {key: n for n, key in enumerate(PIECES)}
HI = 3

KV_JOBS = [("xk", 4), ("xv", 4)]
MIX_JOBS = ([("q", 2), ("k", 1), ("v", 1), ("u", 2), ("rot", 4), ("vg", 2), ("ws", 1), ("s", 4),
             ("cx", 2), ("pt", 4), ("cb", 2), ("pv", 2), ("cc", 2), ("mixed", 2)]
            + [(f"{n}{i}{h}", 2) for h in range(2) for i in range(3) for n in ("gate", "br")]
            + [("wo", 4), ("norm1", 1), ("xq", 4), ("xs", 4), ("xpt", 4), ("xpv", 4), ("xo", 4),
               ("norm2", 1), ("router", 1), ("htok", 4)])


def plan_jobs():
    def jobs(layer, table):
        return [(layer, name, i) for name, n in table for i in range(n)]

    order = jobs(0, [("mem", 4), ("vec", 2), ("memnorm", 1), ("x", 4), ("xk", 4), ("norm0", 1), ("xv", 4)])
    for layer in range(L):
        order += jobs(layer, ([("norm0", 1)] if layer else []) + MIX_JOBS)
        order += jobs(layer + 1, KV_JOBS) if layer + 1 < L else []
        order += jobs(layer, [("place", 1), ("start", 1), ("table", 1), ("moe", 4)])
    order += jobs(L, [("norm0", 1), ("out", 4)])
    plan, used, at = {}, [0] * 8, 0
    for n, key in enumerate(order):
        bank = key[2] if key[1] == "moe" else at % 8
        plan[key] = (bank, n + 1, used[bank])
        used[bank] += 1
        at = bank + 1
    return plan


JOB = plan_jobs()


def piece_job(layer, unit, half):
    if unit == "kv":
        return JOB[layer, "v", 0]
    if unit[:2] in ("xk", "xv", "wo", "xq", "xo"):
        return JOB[layer, unit[:2], 2 * int(unit[2]) + half]
    return JOB[layer, unit, half]


def trunk(nc, A, out):
    with ExitStack() as ctx:
        def sb(name, shape, dt=F32):
            return ctx.enter_context(nc.sbuf_tensor(name, shape, dt))

        def sem(name):
            return ctx.enter_context(nc.semaphore(name))

        def placed(name, shape, dt=F32):
            at = -(-nc.sbuf_base // 32) * 32
            return sb(name, shape, dt), at

        ring, ring_at = placed("ring", [P, R, UNIT])
        xT = sb("xT", [P, KC, T])
        hT, hT_at = placed("hT", [P, KC, T])
        AW = 10640
        h_hi, hhi_at = placed("h_hi", [P, KC, T], F32R)
        w_hi = sb("w_hi", [P, HI, UNIT // 2], F32R)
        arena, arena_at = placed("arena", [P, AW])
        psum = ctx.enter_context(nc.psum_tensor("banks", [P, 8, 512], F32))
        cst = sb("cst", [P, C_END])
        ones = sb("ones", [P, P])
        cosT = sb("cosT", [P, T])
        sinT = sb("sinT", [P, T])
        vec = sb("vec", [P, L, ROWS])
        sinks = sb("sinks", [P, L, 8])
        rbias = sb("rbias", [P, L, NG + NE])
        bs = sb("bs", [1, 512])
        stat = sb("stat", [P, 512])
        rstd = stat[:, 0:T]
        std = stat[:, T:2 * T]
        small = sb("small", [P, 96])
        wr = sb("wr", [P, KC, NG + NE])
        lnt = sb("lnt", [P, 2, MW])
        wsT = sb("wsT", [P, 4, P])
        tabi = sb("tabi", [1, 2 * 16 + 1], I32)
        zero = sb("zero", [P, P])
        mhat_dram = nc.dram_tensor("mhat", (P, KC * T), F32).ap()
        kv_dram = nc.dram_tensor("kv", (L, 2, P, KC * T), F32).ap()

        ident = cst[:, C_ID:C_ID + P]
        tri = cst[:, C_TRI:C_TRI + P]
        rotm = cst[:, C_ROT:C_ROT + P]
        swapm = cst[:, C_SWAP:C_SWAP + P]
        rotswap = cst[:, C_RSW:C_RSW + P]
        inv = cst[:, C_INV:C_INV + 1]
        iota = cst[:, C_IOTA:C_IOTA + T]
        idx = cst[:, C_IDX:C_IDX + 1]
        thr = cst[:, C_THR:C_THR + 7]

        def shaped(v, shape):
            if len(shape) == 2:
                v = v.rearrange("p (a b) -> p a b", b=shape[1])
            if len(shape) == 3:
                v = v.rearrange("p (a b c) -> p a b c", b=shape[1], c=shape[2])
            return v

        def region(at, *shape):
            n = int(np.prod(shape))
            assert at + n <= AW, (at, n)
            return shaped(arena[:, at:at + n], shape)

        def over(name, base, at, *shape, dt=F32R):
            v = nc.alloc_sbuf_tensor_at(name, [P, int(np.prod(shape))], dt, offset=base + 4 * at)
            return shaped(v[:, :], shape)

        w_lo = over("w_lo", ring_at, 0, R, UNIT)
        h_lo = over("h_lo", hT_at, 0, KC, T)
        htok = over("htok", hhi_at, 0, TB, D, dt=F32)

        mhatT = region(2048, KC, T)
        m_lo = over("m_lo", arena_at, 2048, KC, T)
        m_hi = over("m_hi", arena_at, 4480, KC, T)
        k_made = region(6528, KC, T)
        v_made = region(0, TB, D)
        mem_raw = region(6528, TB, D)
        x_raw = region(8576, TB, D)
        vecrows = region(4096, L, P)[0:ROWS]
        posrow = region(0, T).bitcast(I32)
        qT = region(0, MC, T)
        kbd = region(1024, 2, 2, T)
        cx = region(0, MC, T)
        cb = region(1024, MC, T)
        merged = region(0, KC, T)
        merged_lo = over("merged_lo", arena_at, 0, KC, T)
        vtok = region(2048, 3, P)
        uT = region(2432, MC, T)
        yb_lo = over("yb_lo", arena_at, 2432, MC, T)
        vg = region(3456, TB, MW)
        gtmp = region(3456, 512)
        prob = region(4480, 4, 4, P)
        qraw = region(4480, MC, T)
        kraw = region(5504, 2, T)
        z = region(4480, MC, T + 2)
        sig = region(4480, 2, 512)
        ycT = region(5512, MC, T)
        yc_lo = over("yc_lo", arena_at, 5512, MC, T)
        probT = region(6536, 4, 512)
        yb_hi = over("yb_hi", arena_at, 6536, MC, T)
        yc_hi = over("yc_hi", arena_at, 7560, MC, T)
        wsr = region(8584, 4, P)
        ya_lo = over("ya_lo", arena_at, 8584, MC, T)
        ya_hi = over("ya_hi", arena_at, 9608, MC, T)
        ln_sq = region(8584, 2 * MC, P)
        qxT = region(0, KC, T)
        o_lo = over("o_lo", arena_at, 0, KC, T)
        xprob = region(2048, 4, 512)
        kxT = region(4480, KC, T)
        vx = region(6528, TB, D)
        xprobT = region(8576, TB, 4, T)
        xTe = region(2048, KC, EI * SL)
        swt = region(4480, EI, T)
        selw = region(6528, TB, EI, 4 * SL)
        logit = region(8576, TB, NG + NE)
        rt = region(8660, 22, NE)
        place = region(9370, TB, NE)
        wtok = region(9434, TB, NE)
        mask = region(9498, TB, NE)
        tab = region(9562, 64)
        sg = region(9626, P)
        hh = region(9754, P)
        hhT = region(9882, P)
        sel = region(10010, TB, EI, SL)
        ysb = region(0, T)

        slot_loaded = [sem(f"slot_loaded{i}") for i in range(R)]
        bank_free = [sem(f"bank_free{i}") for i in range(8)]
        S = {n: sem(n) for n in (
            "acc_ready", "units_used", "act_step", "dve_step", "pool_step", "x_loaded", "mem_loaded", "cst_loaded", "rows_loaded",
            "ws_loaded", "ln_loaded", "wr_loaded", "x_ready", "mem_ready", "sq_ready", "std_ready", "h_full", "h_high", "h_ready",
            "vec_ready", "angles", "rope_ready", "qraw_ready", "qk_ready", "v_ready", "gelu_ready", "ln_std", "ln_var", "vn_ready",
            "ws_ready", "ws_masked", "s_shifted", "s_exped", "prob_ready", "probT_ready", "c_ready", "y_full", "y_high", "y_ready",
            "sig_ready", "sig_used", "merged_full", "merged_high", "merged_ready", "kv_made", "kv_stored", "kv_loaded",
            "mhat_ready", "mhat_stored", "mhat_loaded", "m_high", "m_ready",
            "qx_ready", "xs_shifted", "xs_exped", "xprob_ready", "xprobT_ready", "o_high", "o_ready", "htok_ready", "r_shift",
            "r_exp", "mask_ready", "extra_ready", "span_ready", "table_ready", "out_ready", "stored", "zero_ready", "eps_ready",
            "w_high", "w_split_dve", "w_split_pool")}

        def moe_sems(tag):
            return {n: sem(f"{n}_{tag}") for n in (
                "sel_ready", "sel_used", "swt_turned", "swt_ready", "gathered", "xe_ready", "gu_ready", "silu_ready",
                "hid_ready", "hid_turned", "hidT_ready", "y_done", "y_copied")}

        main_sems = moe_sems("main")
        extra_sems = [dict(moe_sems(f"extra{i}"), loaded=sem(f"extra_loaded{i}"), used=sem(f"extra_used{i}")) for i in range(L)]

        def piece_view(tensor, layer, unit, half):
            kc = MC if unit.startswith("br") else KC
            n = 256 if unit == "kv" else 512
            w = tensor[:, UNIT_NO[layer, unit] % R, 0:kc * n].rearrange("p (k n) -> p k n", k=kc)
            return w[:, :, half * 256:half * 256 + 256]

        def high_view(layer, unit, half):
            kc = MC if unit.startswith("br") else KC
            return w_hi[:, PIECE_NO[layer, unit, half] % HI, 0:kc * 256].rearrange("p (k n) -> p k n", k=kc)

        def ahead_of(layer, unit, half, ahead):
            n = PIECE_NO[layer, unit, half]
            ends = [PIECE_NO[i + 1, KV_UNITS[-1], 1] for i in range(L - 1)] + [len(PIECES) - 1]
            return min([n + ahead] + [end for end in ends if end >= n])

        def by_pool(unit):
            return unit[:2] in ("xk", "xv")

        def split_count(n):
            mine = by_pool(PIECES[n][1])
            return sum(by_pool(p[1]) == mine for p in PIECES[:n + 1])

        def job_begin(pe, layer, name, i=0):
            bank, _, before = JOB[layer, name, i]
            if before:
                pe.wait_ge(bank_free[bank], before)
            return psum[:, bank, :]

        def job_wait(eng, layer, name, i=0):
            bank, ready, _ = JOB[layer, name, i]
            eng.wait_ge(S["acc_ready"], ready)
            return psum[:, bank, :]

        def free(layer, name, i=0):
            return bank_free[JOB[layer, name, i][0]]

        block = ctx.enter_context(nc.Block())

        @block.sync
        def _(sp):
            def cols(w, a, b):
                return w.rearrange("(k p) n -> p k n", p=P)[:, :, a:b]

            def source(layer, name):
                if name in ("q", "kv", "u", "vg", "cx", "cb", "cc"):
                    a = {"q": 0, "kv": 512, "u": 768, "vg": 1280, "cx": 1792, "cb": 2304, "cc": 2816}[name]
                    return cols(A["w_in"][layer], a, a + (256 if name == "kv" else 512))
                if name.startswith("gate"):
                    a = 3328 + int(name[4]) * D + int(name[5]) * 512
                    return cols(A["w_in"][layer], a, a + 512)
                if name.startswith("br"):
                    h = int(name[3])
                    return cols(A["w_branch"][layer, int(name[2])], h * 512, h * 512 + 512)
                w, a = {"wo": ("w_out", 0), "xk": ("w_xkv", 0), "xv": ("w_xkv", D), "xq": ("w_xq", 0),
                        "xo": ("w_xo", 0)}[name[:2]]
                a += int(name[2]) * 512
                return cols(A[w][layer], a, a + 512)

            def slot_is_free(u):
                if u < R:
                    return
                before = [key for key, n in UNIT_NO.items() if n == u - R]
                if before:
                    layer, name = before[0]
                    sp.wait_ge(S["acc_ready"], piece_job(layer, name, 0 if name == "kv" else 1)[1])
                else:
                    layer = max(i for i in range(L) if FIRST_EXPERT[i] <= u - R)
                    sp.wait_ge(S["units_used"], 3 * NE * layer + u - R - FIRST_EXPERT[layer] + 1)

            def load_dense(layer, name):
                u = UNIT_NO[layer, name]
                src = source(layer, name)
                slot_is_free(u)
                _, kc, n = src.shape
                sp.dma_start(ring[:, u % R, 0:kc * n].rearrange("p (k n) -> p k n", k=kc), src).then_inc(slot_loaded[u % R], 16)

            sp.dma_start(mem_raw, A["mem"][0].rearrange("(t p) d -> p t d", p=P)).then_inc(S["mem_loaded"], 16)
            sp.dma_start(x_raw, A["x"][0].rearrange("(t p) d -> p t d", p=P)).then_inc(S["x_loaded"], 16)
            sp.wait_ge(S["rows_loaded"], 16 * 14)
            for name in KV_UNITS:
                load_dense(0, name)
            for layer in range(L):
                for name in MIX_UNITS:
                    load_dense(layer, name)
                for name in KV_UNITS if layer + 1 < L else []:
                    load_dense(layer + 1, name)
                u0 = FIRST_EXPERT[layer]
                w1 = A["w_expert_in"][layer].rearrange("e (h k p) n -> e h p k n", h=2, p=P)
                w2 = A["w_expert_out"][layer].rearrange("e (k p) n -> e p k n", p=P)

                def expert_unit(slot, e, x, loaded):
                    src = w1[bass.ds(e, 1), x] if x < 2 else w2[bass.ds(e, 1)]
                    sp.dma_start(ring[:, slot, :].rearrange("p (k n) -> p k n", k=4), src.squeeze(0)).then_inc(loaded, 16)

                for n in range(R):
                    slot_is_free(u0 + n)
                    expert_unit((u0 + n) % R, n // 3, n % 3, slot_loaded[(u0 + n) % R])
                with sp.Fori(0, TURNS - 1) as turn:
                    for n in range(R, R + 3 * EI):
                        sp.wait_ge(S["units_used"], turn * (3 * EI) + (3 * NE * layer + n - R + 1))
                        expert_unit((u0 + n) % R, turn * EI + n // 3, n % 3, slot_loaded[(u0 + n) % R])
                for n in range(R + 3 * EI * (TURNS - 1), 3 * NE):
                    slot_is_free(u0 + n)
                    expert_unit((u0 + n) % R, n // 3, n % 3, slot_loaded[(u0 + n) % R])
                X = extra_sems[layer]
                u1 = u0 + 3 * NE
                sp.wait_ge(S["table_ready"], layer + 1)
                count = sp.value_load(tabi[0:1, 32:33], min_val=0, max_val=XB)
                with sp.If(count > 0):
                    with sp.Fori(0, count) as k:
                        e = sp.value_load(tabi[0:1, bass.ds(k, 1)], min_val=0, max_val=NE - 1)
                        sp.wait_ge(S["units_used"], 3 * NE * (layer + 1))
                        sp.wait_ge(X["used"], k + 1)
                        for x in range(3):
                            expert_unit((u1 + x) % R, e, x, X["loaded"])
                sp.wait_ge(X["used"], count + 1)
            for i in range(4):
                sp.wait_ge(S["out_ready"], i + 1)
                sp.dma_start(out[0].rearrange("(t p) d -> t p d", p=P)[i // 2, :, (i % 2) * 512:(i % 2) * 512 + 512],
                             arena[:, i * 512:(i + 1) * 512]).then_inc(S["stored"], 16)
            sp.wait_ge(S["stored"], 64)

        @block.gpsimd
        def _(pool):
            pool.memset(ones[:, :], 1.0).then_inc(S["pool_step"], 1)
            for n, key in enumerate(PIECES):
                if by_pool(key[1]):
                    pool.wait_ge(S["w_high"], n + 1)
                    pool.tensor_tensor(piece_view(w_lo, *key), piece_view(ring, *key), high_view(*key).bitcast(F32),
                                       ALU.subtract).then_inc(S["w_split_pool"], 1)

        @block.scalar
        def _(act):
            steps = [0]

            def link(ins):
                steps[0] += 1
                ins.then_inc(S["act_step"], 1)
                act.wait_ge(S["act_step"], steps[0])

            def post(ins, stage):
                link(ins)
                act.sem_inc(S[stage], 1)

            split = [0]

            def split_to(layer, unit, half, ahead=2):
                while split[0] <= ahead_of(layer, unit, half, ahead):
                    n = split[0]
                    key = PIECES[n]
                    u = UNIT_NO[key[:2]]
                    act.wait_ge(slot_loaded[u % R], 16 * (u // R + 1))
                    if n >= HI:
                        act.wait_ge(S["acc_ready"], piece_job(*PIECES[n - HI])[1])
                    post(act.copy(high_view(*key), piece_view(ring, *key)), "w_high")
                    split[0] += 1

            act.dma_start(cst[:, :], A["cst"]).then_inc(S["cst_loaded"], 16)
            for layer in range(L):
                for src, at in ((A["mix_norm"][layer], ROW_MIX), (A["b_gate"][layer], ROW_GATE),
                                (A["conv_w"][layer].rearrange("k n -> (k n)"), ROW_CONV),
                                (A["xattn_norm"][layer], ROW_XN), (A["mem_norm"][layer], ROW_MN),
                                (A["ffn_norm"][layer], ROW_FF), (A["final_norm"], ROW_FIN)):
                    rows = src.rearrange("(r p) -> r p", p=P)
                    act.dma_start(vecrows[at:at + rows.shape[0], layer, :], rows).then_inc(S["rows_loaded"], 16)
            act.dma_start(posrow[:, :], A["positions"].broadcast_to([P, T])).then_inc(S["cst_loaded"], 16)
            act.dma_start(sinks[:, :, :], A["attn_sinks"].unsqueeze(0).broadcast_to([P, L, 8])).then_inc(S["cst_loaded"], 16)
            act.dma_start(rbias[:, :, 0:NG], A["b_router_group"].unsqueeze(0).broadcast_to([P, L, NG])).then_inc(S["cst_loaded"], 16)
            act.dma_start(rbias[:, :, NG:], A["b_router_expert"].unsqueeze(0).broadcast_to([P, L, NE])).then_inc(S["cst_loaded"], 16)

            two = lambda acc: acc.rearrange("p (c t) -> p c t", c=2)

            def evac(layer, name, i, dst, signal, func=None, view=two):
                src = view(job_wait(act, layer, name, i))
                post(act.copy(dst, src) if func is None else act.activation(dst, src, func), signal)
                act.sem_inc(free(layer, name, i), 1)

            def root(no, layer, name):
                acc = job_wait(act, layer, name)
                post(act.activation(std, acc[:, 0:T], ACT.Sqrt, bias=small[:, 95:96], scale=1.0 / D), "std_ready")
                act.sem_inc(free(layer, name), 1)

            def squares(src):
                for i in range(4):
                    post(act.activation(hT[:, 2 * i:2 * i + 2, :], src[:, 2 * i:2 * i + 2, :], ACT.Square), "sq_ready")

            n_norm, n_x, n_high = [1], [0], [0]

            def x_norm(layer, name, split_high):
                for i in range(4):
                    act.wait_ge(S["x_ready"], 4 * n_x[0] + i + 1)
                    post(act.activation(hT[:, 2 * i:2 * i + 2, :], xT[:, 2 * i:2 * i + 2, :], ACT.Square), "sq_ready")
                n_x[0] += 1
                root(n_norm[0], layer, name)
                n_norm[0] += 1
                if split_high:
                    n_high[0] += 1
                    for i in range(4):
                        act.wait_ge(S["h_full"], 4 * (n_norm[0] - 1) + i + 1)
                        post(act.copy(h_hi[:, 2 * i:2 * i + 2, :], hT[:, 2 * i:2 * i + 2, :]), "h_high")

            def memory_high(layer):
                for k in range(KC):
                    post(act.activation(m_hi[:, k, :], mhatT[:, k, :], ACT.Copy,
                                        scale=vec[:, layer, ROW_MN + k:ROW_MN + k + 1]), "m_high")

            def make_k(layer):
                for i in range(4):
                    split_to(layer, f"xk{i // 2}", i % 2)
                    evac(layer, "xk", i, k_made[:, 2 * i:2 * i + 2, :], "kv_made")
                act.dma_start(kv_dram[layer, 0], k_made.rearrange("p a b -> p (a b)")).then_inc(S["kv_stored"], 16)

            def make_v(layer):
                for i in range(4):
                    split_to(layer, f"xv{i // 2}", i % 2)
                    evac(layer, "xv", i, v_made[:, :, i * 256:i * 256 + 256], "kv_made")
                act.dma_start(kv_dram[layer, 1], v_made.rearrange("p a b -> p (a b)")).then_inc(S["kv_stored"], 16)

            for i in range(4):
                evac(0, "mem", i, mhatT[:, 2 * i:2 * i + 2, :], "mem_ready")
            act.wait_ge(S["eps_ready"], 1)
            squares(mhatT)
            root(0, 0, "memnorm")
            for i in range(4):
                evac(0, "x", i, xT[:, 2 * i:2 * i + 2, :], "x_ready")
            act.wait_ge(S["angles"], 1)
            post(act.activation(sinT[:, :], cosT[:, :], ACT.Sin), "rope_ready")
            act.wait_ge(S["angles"], 2)
            post(act.activation(cosT[:, :], cosT[:, :], ACT.Sin), "rope_ready")
            act.wait_ge(S["mhat_ready"], 1)
            act.dma_start(mhat_dram, mhatT.rearrange("p a b -> p (a b)")).then_inc(S["mhat_stored"], 16)
            memory_high(0)
            act.wait_ge(S["h_ready"], 1)
            split_to(0, "xk0", 0)
            make_k(0)
            x_norm(0, "norm0", True)
            make_v(0)
            for layer in range(L):
                if layer:
                    x_norm(layer, "norm0", True)
                act.dma_start(wsr[:, :, :], A["gmlp_w_s"][layer].rearrange("g i j -> i g j")).then_inc(S["ws_loaded"], 16)
                act.dma_start(lnt[:, 0, :], A["gmlp_ln_g"][layer:layer + 1].broadcast_to([P, MW])).then_inc(S["ln_loaded"], 16)
                act.dma_start(lnt[:, 1, :], A["gmlp_ln_b"][layer:layer + 1].broadcast_to([P, MW])).then_inc(S["ln_loaded"], 16)
                act.dma_start(bs[0:1, :], A["gmlp_b_s"][layer].rearrange("g i -> (g i)").unsqueeze(0)).then_inc(S["ln_loaded"], 16)
                act.dma_start(wr[:, :, 0:NG], A["w_router_group"][layer].rearrange("(k p) n -> p k n", p=P)).then_inc(S["wr_loaded"], 16)
                act.dma_start(wr[:, :, NG:], A["w_router_expert"][layer].rearrange("(k p) n -> p k n", p=P)).then_inc(S["wr_loaded"], 16)
                for i in range(2):
                    split_to(layer, "q", i)
                    evac(layer, "q", i, qraw[:, 2 * i:2 * i + 2, :], "qraw_ready")
                split_to(layer, "kv", 0)
                evac(layer, "k", 0, kraw[:, 0, :], "qraw_ready", view=lambda a: a[:, 0:T])
                evac(layer, "v", 0, vtok[:, 0:2, :], "v_ready", view=lambda a: a.rearrange("p (t c) -> p t c", t=2)[:, :, P:])
                post(act.copy(vtok[0:64, 2, :], vtok[0:64, 1, :]), "v_ready")
                post(act.copy(vtok[64:P, 2, :], vtok[64:P, 0, :]), "v_ready")
                for i in range(2):
                    split_to(layer, "u", i)
                    evac(layer, "u", i, uT[:, 2 * i:2 * i + 2, :], "gelu_ready", func=ACT.Gelu_apprx_tanh)
                for i in range(2):
                    split_to(layer, "vg", i)
                    evac(layer, "vg", i, vg[:, :, i * 256:i * 256 + 256], "gelu_ready", func=ACT.Gelu_apprx_tanh)
                evac(layer, "ws", 0, wsT[:, :, :], "ws_ready", view=lambda a: a.rearrange("p (g i) -> p g i", g=4))
                split_to(layer, "cx", 0)
                for i in range(4):
                    act.wait_ge(S["s_shifted"], 4 * layer + i + 1)
                    flat = prob[:, i].rearrange("p h k -> p (h k)")
                    link(act.activation(flat, flat, ACT.Exp))
                    post(act.activation(small[:, 32 + 4 * i:36 + 4 * i], small[:, 32 + 4 * i:36 + 4 * i], ACT.Exp), "s_exped")
                act.wait_ge(S["ln_var"], layer + 1)
                post(act.activation(small[:, 8:16], small[:, 0:8], ACT.Sqrt, bias=small[:, 95:96], scale=1.0 / P), "ln_std")
                for i in range(2):
                    split_to(layer, "cx", i)
                    evac(layer, "cx", i, cx[:, 2 * i:2 * i + 2, :], "c_ready")
                for i in range(4):
                    evac(layer, "pt", i, probT[:, i, :], "probT_ready", view=lambda a: a)
                for i in range(2):
                    split_to(layer, "cb", i)
                    evac(layer, "cb", i, cb[:, 2 * i:2 * i + 2, :], "c_ready")
                for i in range(2):
                    acc = job_wait(act, layer, "pv", i)
                    post(act.copy(ya_hi[:, 2 * i:2 * i + 2, :], two(acc)), "y_high")
                for i in range(2):
                    split_to(layer, "cc", i)
                split_to(layer, "gate00", 0, ahead=0)
                act.wait_ge(S["y_full"], 2 * layer + 1)
                post(act.copy(yc_hi[:, :, :], ycT[:, :, :]), "y_high")
                act.wait_ge(S["y_full"], 2 * layer + 2)
                post(act.copy(yb_hi[:, :, :], uT[:, :, :]), "y_high")
                n = 12 * layer
                for h in range(2):
                    for i in range(3):
                        for j in range(2):
                            split_to(layer, f"gate{i}{h}", j)
                            acc = job_wait(act, layer, f"gate{i}{h}", j)
                            if n >= 2:
                                act.wait_ge(S["sig_used"], n - 1)
                            for c in range(2):
                                col = ROW_GATE + i * KC + h * 4 + j * 2 + c
                                link(act.activation(sig[:, j, c * T:(c + 1) * T], acc[:, c * T:(c + 1) * T], ACT.Sigmoid,
                                                    bias=vec[:, layer, col:col + 1]))
                            act.sem_inc(free(layer, f"gate{i}{h}", j), 1)
                            act.sem_inc(S["sig_ready"], 1)
                            n += 1
                        for j in range(2):
                            split_to(layer, f"br{i}{h}", j)
                act.wait_ge(S["acc_ready"], JOB[layer, "gate21", 1][1])
                for i in range(4):
                    act.wait_ge(S["merged_full"], 4 * layer + i + 1)
                    post(act.copy(h_hi[:, 2 * i:2 * i + 2, :], merged[:, 2 * i:2 * i + 2, :]), "merged_high")
                act.wait_ge(S["acc_ready"], JOB[layer, "br21", 1][1])
                act.wait_ge(S["merged_high"], 4 * layer + 4)
                act.wait_ge(S["merged_ready"], 4 * layer + 4)
                act.wait_ge(S["kv_stored"], 32 * (layer + 1))
                act.dma_start(kxT.rearrange("p a b -> p (a b)"), kv_dram[layer, 0]).then_inc(S["kv_loaded"], 16)
                act.dma_start(vx.rearrange("p a b -> p (a b)"), kv_dram[layer, 1]).then_inc(S["kv_loaded"], 16)
                for i in range(4):
                    split_to(layer, f"wo{i // 2}", i % 2)
                x_norm(layer, "norm1", True)
                for i in range(4):
                    split_to(layer, f"xq{i // 2}", i % 2)
                    evac(layer, "xq", i, qxT[:, 2 * i:2 * i + 2, :], "qx_ready")
                for i in range(4):
                    act.wait_ge(S["xs_shifted"], 4 * layer + i + 1)
                    post(act.activation(xprob[:, i, :], xprob[:, i, :], ACT.Exp), "xs_exped")
                for i in range(4):
                    tb, hp = i // 2, i % 2
                    acc = job_wait(act, layer, "xpt", i)
                    for kb in range(2):
                        link(act.copy(xprobT[:, kb, 2 * hp:2 * hp + 2, tb * P:(tb + 1) * P],
                                      acc.rearrange("p (h b q) -> p h b q", h=2, b=2)[:, :, kb, :]))
                    act.sem_inc(free(layer, "xpt", i), 1)
                    act.sem_inc(S["xprobT_ready"], 1)
                if layer + 1 < L:
                    act.wait_ge(S["acc_ready"], JOB[layer, "xpt", 3][1])
                    act.wait_ge(S["mhat_stored"], 16)
                    act.dma_start(mhatT.rearrange("p a b -> p (a b)"), mhat_dram).then_inc(S["mhat_loaded"], 16)
                for i in range(4):
                    acc = job_wait(act, layer, "xpv", i)
                    post(act.copy(h_hi[:, 2 * i:2 * i + 2, :], two(acc)), "o_high")
                for i in range(4):
                    split_to(layer, f"xo{i // 2}", i % 2)
                if layer + 1 < L:
                    act.wait_ge(S["mhat_loaded"], 16)
                    memory_high(layer + 1)
                x_norm(layer, "norm2", False)
                for i in range(4):
                    evac(layer, "htok", i, htok[:, i // 2, (i % 2) * 512:(i % 2) * 512 + 512], "htok_ready", view=lambda a: a)
                act.wait_ge(S["r_shift"], layer + 1)
                link(act.activation(rt[:, 20, 0:8], rt[:, 20, 0:8], ACT.Exp))
                post(act.activation(rt[:, 21, 0:2], rt[:, 21, 0:2], ACT.Exp), "r_exp")
                if layer + 1 < L:
                    make_k(layer + 1)
                    make_v(layer + 1)

                def experts(Q, turn, ne):
                    n0 = turn * ne
                    for e in range(ne):
                        act.wait_ge(Q["swt_turned"], n0 + (e + 1))
                        act.copy(swt[:, e, :], psum[:, 6, 0:T]).then_inc(Q["swt_ready"], 1)
                    for r in range(4):
                        act.wait_ge(Q["gathered"], turn * 4 + (r + 1))
                        act.copy(xTe[:, 2 * r:2 * r + 2, 0:ne * SL],
                                 psum[:, 7, :].rearrange("p (c s) -> p c s", c=2)[:, :, 0:ne * SL]).then_inc(Q["xe_ready"], 1)
                    for e in range(ne):
                        act.wait_ge(Q["gu_ready"], n0 + (e + 1))
                        act.activation(sg, psum[:, 4, (e % 2) * T:(e % 2) * T + P], ACT.Silu).then_inc(Q["silu_ready"], 1)
                        act.wait_ge(Q["hid_turned"], n0 + (e + 1))
                        act.copy(hhT, psum[:, 6, T:T + P]).then_inc(Q["hidT_ready"], 1)

                base = layer * TURNS
                with act.Fori(base, base + TURNS) as turn:
                    experts(main_sems, turn, EI)
                act.wait_ge(S["table_ready"], layer + 1)
                count = act.value_load(tabi[0:1, 32:33], min_val=0, max_val=XB)
                with act.If(count > 0):
                    with act.Fori(0, count) as k:
                        experts(extra_sems[layer], k, 1)
            x_norm(L, "norm0", False)
            for i in range(4):
                evac(L, "out", i, arena[:, i * 512:(i + 1) * 512], "out_ready", view=lambda a: a)
            act.wait_ge(S["kv_stored"], 32 * L)

        @block.vector
        def _(dve):
            steps = [0]

            def link(ins):
                steps[0] += 1
                ins.then_inc(S["dve_step"], 1)
                dve.wait_ge(S["dve_step"], steps[0])

            def post(ins, stage):
                link(ins)
                dve.sem_inc(S[stage], 1)

            split = [0]

            def split_to(layer, unit, half, ahead=2):
                while split[0] <= ahead_of(layer, unit, half, ahead):
                    key = PIECES[split[0]]
                    if not by_pool(key[1]):
                        dve.wait_ge(S["w_high"], split[0] + 1)
                        post(dve.tensor_tensor(piece_view(w_lo, *key), piece_view(ring, *key), high_view(*key).bitcast(F32),
                                               ALU.subtract), "w_split_dve")
                    split[0] += 1

            def bc(v, n):
                return v.unsqueeze(2).broadcast_to([P, v.shape[1], n])

            two = lambda acc: acc.rearrange("p (c t) -> p c t", c=2)
            flat = lambda v: v.rearrange("p a b -> p (a b)")

            post(dve.memset(zero[:, :], 0.0), "zero_ready")
            post(dve.memset(small[:, 95:96], EPS), "eps_ready")
            dve.wait_ge(S["cst_loaded"], 80)
            ang, turns_f, dst = region(256, T), region(512, T), cosT[:, :]
            link(dve.tensor_copy(dst, posrow[:, :]))
            link(dve.tensor_scalar(ang, dst, inv, None, ALU.mult))
            C1, C2 = 6.28125, 0.0019350051879882812
            C3 = 2 * np.pi - C1 - C2
            for half in range(2):
                if half:
                    dve.wait_ge(S["rope_ready"], 1)
                    link(dve.tensor_scalar(turns_f, ang, 1.0 / (2 * np.pi), 0.25, ALU.mult, ALU.add))
                else:
                    link(dve.tensor_scalar(turns_f, ang, 1.0 / (2 * np.pi), None, ALU.mult))
                link(dve.tensor_copy(posrow[:, :], turns_f))
                link(dve.tensor_copy(turns_f, posrow[:, :]))
                link(dve.scalar_tensor_tensor(dst, turns_f, -C1, ang, ALU.mult, ALU.add))
                link(dve.scalar_tensor_tensor(dst, turns_f, -C2, dst, ALU.mult, ALU.add))
                link(dve.scalar_tensor_tensor(dst, turns_f, -C3, dst, ALU.mult, ALU.add))
                if half:
                    link(dve.tensor_scalar(dst, dst, np.pi / 2, None, ALU.add))
                link(dve.tensor_scalar(turns_f, dst, float(np.pi), -2 * np.pi, ALU.is_gt, ALU.mult))
                link(dve.tensor_tensor(dst, dst, turns_f, ALU.add))
                link(dve.tensor_scalar(turns_f, dst, -float(np.pi), 2 * np.pi, ALU.is_lt, ALU.mult))
                link(dve.tensor_tensor(dst, dst, turns_f, ALU.add))
                post(dve.tensor_scalar(dst, dst, 3.1415925, -3.1415925, ALU.min, ALU.max), "angles")
            dve.wait_ge(S["rope_ready"], 2)
            for i in range(2):
                acc = job_wait(dve, 0, "vec", i)
                post(dve.tensor_copy(vec[:, i, :], acc[:, 0:ROWS]), "vec_ready")
                dve.sem_inc(free(0, "vec", i), 1)

            n_norm, n_high, n_x = [0], [0], [4]

            def norm(col, layer, split_low):
                dve.wait_ge(S["std_ready"], n_norm[0] + 1)
                n_norm[0] += 1
                link(dve.reciprocal(rstd, std))
                for k in range(KC):
                    ins = dve.scalar_tensor_tensor(hT[:, k, :], xT[:, k, :], vec[:, layer, col + k:col + k + 1], rstd,
                                                   ALU.mult, ALU.mult)
                    if k % 2:
                        post(ins, "h_full")
                    else:
                        link(ins)
                if split_low:
                    for i in range(4):
                        n_high[0] += 1
                        dve.wait_ge(S["h_high"], n_high[0])
                        part = slice(2 * i, 2 * i + 2)
                        post(dve.tensor_tensor(h_lo[:, part, :], hT[:, part, :], h_hi[:, part, :].bitcast(F32), ALU.subtract), "h_ready")

            def memory_low(layer):
                for k in range(KC):
                    dve.wait_ge(S["m_high"], KC * layer + k + 1)
                    post(dve.scalar_tensor_tensor(m_lo[:, k, :], mhatT[:, k, :], vec[:, layer, ROW_MN + k:ROW_MN + k + 1],
                                                  m_hi[:, k, :].bitcast(F32), ALU.mult, ALU.subtract), "m_ready")

            dve.wait_ge(S["std_ready"], 1)
            n_norm[0] = 1
            link(dve.reciprocal(rstd, std))
            for k in range(KC):
                link(dve.tensor_tensor(mhatT[:, k, :], mhatT[:, k, :], rstd, ALU.mult))
            for i in range(4):
                dve.sem_inc(S["h_full"], 1)
            dve.sem_inc(S["mhat_ready"], 1)
            dve.sem_inc(S["h_ready"], 1)
            dve.wait_ge(S["mhat_stored"], 16)
            memory_low(0)
            dve.wait_ge(S["x_ready"], 4)

            def add_x(layer, name, i):
                acc = job_wait(dve, layer, name, i)
                dst = xT[:, 2 * i:2 * i + 2, :]
                post(dve.tensor_tensor(dst, dst, two(acc), ALU.add), "x_ready")
                dve.sem_inc(free(layer, name, i), 1)

            for layer in range(L):
                norm(ROW_MIX, layer, True)
                split_to(layer, "q", 0)
                split_to(layer, "q", 1)
                if layer == 0:
                    dve.wait_ge(S["kv_stored"], 32)
                link(dve.memset(kbd[:, :, :, :], 0.0))
                split_to(layer, "kv", 0)
                split_to(layer, "u", 0)
                split_to(layer, "u", 1)
                cos2 = cosT[:, :].unsqueeze(1).broadcast_to([P, 2, T])
                sin2 = sinT[:, :].unsqueeze(1).broadcast_to([P, 2, T])
                tmp = two(stat[:, :])
                for i in range(3):
                    acc = two(job_wait(dve, layer, "rot", i))
                    link(dve.tensor_tensor(tmp, acc, sin2, ALU.mult))
                    dve.sem_inc(free(layer, "rot", i), 1)
                    dve.wait_ge(S["qraw_ready"], 3 * layer + i + 1)
                    if i < 2:
                        raw = qraw[:, 2 * i:2 * i + 2, :]
                        link(dve.tensor_tensor(raw, raw, cos2, ALU.mult))
                        link(dve.tensor_tensor(qT[:, 2 * i:2 * i + 2, :], raw, tmp, ALU.add))
                    else:
                        swapped = job_wait(dve, layer, "rot", 3)
                        link(dve.tensor_tensor(kraw[:, 0, :], kraw[:, 0, :], cosT[:, :], ALU.mult))
                        link(dve.tensor_tensor(kraw[:, 1, :], swapped[:, 0:T], cosT[:, :], ALU.mult))
                        dve.sem_inc(free(layer, "rot", 3), 1)
                        link(dve.tensor_tensor(kbd[0:64, 0, 0, :], kraw[0:64, 0, :], tmp[0:64, 0, :], ALU.add))
                        link(dve.tensor_tensor(kbd[64:P, 1, 1, :], kraw[64:P, 0, :], tmp[64:P, 0, :], ALU.add))
                        link(dve.tensor_tensor(kbd[64:P, 0, 1, :], kraw[64:P, 1, :], tmp[64:P, 1, :], ALU.add))
                        link(dve.tensor_tensor(kbd[0:64, 1, 0, :], kraw[0:64, 1, :], tmp[0:64, 1, :], ALU.add))
                    dve.sem_inc(S["qk_ready"], 1)
                split_to(layer, "vg", 0)
                split_to(layer, "vg", 1)
                dve.wait_ge(S["ws_ready"], layer + 1)
                post(dve.memset(wsT[64:P, :, 0:64], 0.0), "ws_masked")
                for i in range(4):
                    g, p = i // 2, i % 2
                    acc = job_wait(dve, layer, "s", i).rearrange("p (h k) -> p h k", h=4)
                    mx = small[:, 24:28]
                    if p == 0:
                        link(dve.memset(acc[0:64, :, 64:P], NEG))
                    link(dve.tensor_reduce(mx, acc, AX.X, ALU.max))
                    link(dve.scalar_tensor_tensor(mx, mx, 0.125, sinks[:, layer, 4 * g:4 * g + 4], ALU.mult, ALU.max))
                    link(dve.tensor_tensor(small[:, 32 + 4 * i:36 + 4 * i], sinks[:, layer, 4 * g:4 * g + 4], mx, ALU.subtract))
                    link(dve.scalar_tensor_tensor(prob[:, i], acc, 0.125, bc(mx, P), ALU.mult, ALU.subtract))
                    dve.sem_inc(free(layer, "s", i), 1)
                    dve.sem_inc(S["s_shifted"], 1)
                split_to(layer, "cx", 0)
                dve.wait_ge(S["gelu_ready"], 4 * layer + 4)
                vgv = vg[:, :, :].rearrange("p t (g c) -> p (t g) c", c=P)
                link(dve.tensor_reduce(small[:, 0:8], vgv, AX.X, ALU.add))
                link(dve.tensor_scalar(small[:, 0:8], small[:, 0:8], 1.0 / P, None, ALU.mult))
                link(dve.tensor_tensor(vgv, vgv, bc(small[:, 0:8], P), ALU.subtract))
                link(dve.tensor_tensor(ln_sq, vgv, vgv, ALU.mult))
                post(dve.tensor_reduce(small[:, 0:8], ln_sq, AX.X, ALU.add), "ln_var")
                for i in range(4):
                    dve.wait_ge(S["s_exped"], 4 * layer + i + 1)
                    link(dve.tensor_reduce(small[:, 24:28], prob[:, i], AX.X, ALU.add))
                    link(dve.tensor_tensor(small[:, 24:28], small[:, 24:28], small[:, 32 + 4 * i:36 + 4 * i], ALU.add))
                    link(dve.reciprocal(small[:, 24:28], small[:, 24:28]))
                    post(dve.tensor_tensor(prob[:, i], prob[:, i], bc(small[:, 24:28], P), ALU.mult), "prob_ready")
                    if i == 1:
                        split_to(layer, "cx", 1)
                dve.wait_ge(S["ln_loaded"], 48 * (layer + 1))
                dve.wait_ge(S["ln_std"], layer + 1)
                link(dve.reciprocal(small[:, 16:24], small[:, 8:16]))
                link(dve.tensor_tensor(vgv, vgv, bc(small[:, 16:24], P), ALU.mult))
                link(dve.tensor_tensor(vg[:, :, :], vg[:, :, :], lnt[:, 0:1, :].broadcast_to([P, TB, MW]), ALU.mult))
                split_to(layer, "cb", 0)
                post(dve.tensor_tensor(vg[:, :, :], vg[:, :, :], lnt[:, 1:2, :].broadcast_to([P, TB, MW]), ALU.add), "vn_ready")
                split_to(layer, "cb", 1)
                for i in range(2):
                    dve.wait_ge(S["y_high"], 4 * layer + i + 1)
                    acc = job_wait(dve, layer, "pv", i)
                    post(dve.tensor_tensor(ya_lo[:, 2 * i:2 * i + 2, :], two(acc), ya_hi[:, 2 * i:2 * i + 2, :].bitcast(F32),
                                           ALU.subtract), "y_ready")
                    dve.sem_inc(free(layer, "pv", i), 1)
                link(dve.memset(z[:, :, 0:2], 0.0))
                for i in range(2):
                    split_to(layer, "cc", i)
                    dve.wait_ge(S["c_ready"], 4 * layer + 2)
                    acc = job_wait(dve, layer, "cc", i)
                    link(dve.tensor_tensor(z[:, 2 * i:2 * i + 2, 2:T + 2], cx[:, 2 * i:2 * i + 2, :], two(acc), ALU.mult))
                    dve.sem_inc(free(layer, "cc", i), 1)
                for c in range(MC):
                    w = [vec[:, layer, ROW_CONV + 4 * k + c:ROW_CONV + 4 * k + c + 1] for k in range(3)]
                    link(dve.tensor_scalar(ycT[:, c, :], z[:, c, 0:T], w[0], None, ALU.mult))
                    link(dve.scalar_tensor_tensor(ycT[:, c, :], z[:, c, 1:T + 1], w[1], ycT[:, c, :], ALU.mult, ALU.add))
                    link(dve.scalar_tensor_tensor(ycT[:, c, :], z[:, c, 2:T + 2], w[2], ycT[:, c, :], ALU.mult, ALU.add))
                dve.wait_ge(S["c_ready"], 4 * layer + 4)
                post(dve.tensor_tensor(ycT[:, :, :], ycT[:, :, :], cb[:, :, :], ALU.mult), "y_full")
                for tb in range(TB):
                    acc = job_wait(dve, layer, "mixed", tb)
                    link(dve.tensor_tensor(uT[:, :, tb * P:(tb + 1) * P], uT[:, :, tb * P:(tb + 1) * P],
                                           acc.rearrange("p (g i) -> p g i", g=4), ALU.mult))
                    dve.sem_inc(free(layer, "mixed", tb), 1)
                dve.sem_inc(S["y_full"], 1)
                dve.wait_ge(S["y_high"], 4 * layer + 3)
                post(dve.tensor_tensor(flat(yc_lo), flat(ycT), flat(yc_hi).bitcast(F32), ALU.subtract), "y_ready")
                dve.wait_ge(S["y_high"], 4 * layer + 4)
                post(dve.tensor_tensor(flat(yb_lo), flat(uT), flat(yb_hi).bitcast(F32), ALU.subtract), "y_ready")
                n = 12 * layer
                for h in range(2):
                    for i in range(3):
                        for j in range(2):
                            split_to(layer, f"gate{i}{h}", j)
                        for j in range(2):
                            split_to(layer, f"br{i}{h}", j)
                            acc = job_wait(dve, layer, f"br{i}{h}", j)
                            dve.wait_ge(S["sig_ready"], n + 1)
                            c0 = 4 * h + 2 * j
                            dst = flat(merged[:, c0:c0 + 2, :])
                            if i == 0:
                                link(dve.tensor_tensor(dst, sig[:, j, :], acc, ALU.mult))
                            else:
                                link(dve.tensor_tensor(gtmp, sig[:, j, :], acc, ALU.mult))
                                link(dve.tensor_tensor(dst, dst, gtmp, ALU.add))
                            dve.sem_inc(free(layer, f"br{i}{h}", j), 1)
                            dve.sem_inc(S["sig_used"], 1)
                            if i == 2:
                                dve.sem_inc(S["merged_full"], 1)
                            n += 1
                for i in range(4):
                    dve.wait_ge(S["merged_high"], 4 * layer + i + 1)
                    part = slice(2 * i, 2 * i + 2)
                    post(dve.tensor_tensor(merged_lo[:, part, :], merged[:, part, :], h_hi[:, part, :].bitcast(F32),
                                           ALU.subtract), "merged_ready")
                for i in range(4):
                    split_to(layer, f"wo{i // 2}", i % 2)
                    add_x(layer, "wo", i)
                norm(ROW_XN, layer, True)
                for i in range(4):
                    split_to(layer, f"xq{i // 2}", i % 2)
                for i in range(4):
                    acc = job_wait(dve, layer, "xs", i).rearrange("p (h k) -> p h k", h=2)
                    mx = small[:, 24:26]
                    buf = xprob[:, i, :].rearrange("p (h k) -> p h k", h=2)
                    link(dve.tensor_reduce(mx, acc, AX.X, ALU.max))
                    link(dve.tensor_scalar(mx, mx, 0.0625, None, ALU.mult))
                    link(dve.scalar_tensor_tensor(buf, acc, 0.0625, bc(mx, T), ALU.mult, ALU.subtract))
                    dve.sem_inc(free(layer, "xs", i), 1)
                    dve.sem_inc(S["xs_shifted"], 1)
                for i in range(4):
                    buf = xprob[:, i, :].rearrange("p (h k) -> p h k", h=2)
                    dve.wait_ge(S["xs_exped"], 4 * layer + i + 1)
                    link(dve.tensor_reduce(small[:, 24:26], buf, AX.X, ALU.add))
                    link(dve.reciprocal(small[:, 24:26], small[:, 24:26]))
                    post(dve.tensor_tensor(buf, buf, bc(small[:, 24:26], T), ALU.mult), "xprob_ready")
                for i in range(4):
                    dve.wait_ge(S["o_high"], 4 * layer + i + 1)
                    acc = job_wait(dve, layer, "xpv", i)
                    part = slice(2 * i, 2 * i + 2)
                    post(dve.tensor_tensor(o_lo[:, part, :], two(acc), h_hi[:, part, :].bitcast(F32), ALU.subtract), "o_ready")
                    dve.sem_inc(free(layer, "xpv", i), 1)
                for i in range(4):
                    split_to(layer, f"xo{i // 2}", i % 2)
                    add_x(layer, "xo", i)
                if layer + 1 < L:
                    memory_low(layer + 1)
                norm(ROW_FF, layer, False)
                acc = job_wait(dve, layer, "router")
                link(dve.tensor_tensor(logit[:, :, :], acc[:, 0:TB * (NG + NE)].rearrange("p (t n) -> p t n", t=TB),
                                       rbias[:, layer:layer + 1, :].broadcast_to([P, TB, NG + NE]), ALU.add))
                dve.sem_inc(free(layer, "router"), 1)
                gm, ge, gi = rt[:, 0, 0:2], rt[:, 1, 0:8].rearrange("p (t n) -> p t n", t=2), rt[:, 2, 0:2]
                ex = rt[:, 20, 0:8].rearrange("p (t n) -> p t n", t=2)
                gl, el = logit[:, :, 0:NG], logit[:, :, NG:]

                def first_max(values, n, best, onehot, where):
                    io = iota[:, 0:n].unsqueeze(1).broadcast_to([P, TB, n])
                    link(dve.tensor_reduce(best, values, AX.X, ALU.max))
                    link(dve.tensor_tensor(onehot, values, bc(best, n), ALU.is_lt))
                    link(dve.scalar_tensor_tensor(onehot, onehot, 1000.0, io, ALU.mult, ALU.add))
                    link(dve.tensor_reduce(where, onehot, AX.X, ALU.min))
                    link(dve.tensor_tensor(onehot, io, bc(where, n), ALU.is_equal))

                first_max(gl, NG, gm, ge, gi)
                link(dve.tensor_tensor(ex, gl, bc(gm, NG), ALU.subtract))
                lem = rt[:, 4:6, :]
                oh1, oh2 = rt[:, 6:8, :], rt[:, 8:10, :]
                t1, t2, wi = rt[:, 10, 0:2], rt[:, 11, 0:2], rt[:, 12, 0:2]
                off = rt[:, 13, 0:8].rearrange("p (t n) -> p t n", t=2)
                link(dve.tensor_scalar(off, ge, -NEG, NEG, ALU.mult, ALU.add))
                for tb in range(TB):
                    e4 = el[:, tb, :].rearrange("p (g e) -> p g e", g=NG)
                    l4 = lem[:, tb, :].rearrange("p (g e) -> p g e", g=NG)
                    link(dve.tensor_tensor(l4, e4, bc(ge[:, tb, :], EPG), ALU.mult))
                    link(dve.tensor_tensor(l4, l4, bc(off[:, tb, :], EPG), ALU.add))
                first_max(lem, NE, t1, oh1, wi)
                link(dve.scalar_tensor_tensor(lem, oh1, 2 * NEG, lem, ALU.mult, ALU.add))
                first_max(lem, NE, t2, oh2, wi)
                link(dve.tensor_tensor(rt[:, 21, 0:2], t2, t1, ALU.subtract))
                dve.sem_inc(S["r_shift"], 1)
                post(dve.tensor_tensor(mask[:, :, :], oh1, oh2, ALU.add), "mask_ready")
                dve.wait_ge(S["r_exp"], layer + 1)
                gs, w1, w2 = rt[:, 14, 0:2], rt[:, 15, 0:2], rt[:, 16, 0:2]
                link(dve.tensor_reduce(gs, ex, AX.X, ALU.add))
                link(dve.tensor_scalar(w1, rt[:, 21, 0:2], 1.0, None, ALU.add))
                link(dve.tensor_tensor(w1, w1, gs, ALU.mult))
                link(dve.reciprocal(w1, w1))
                link(dve.tensor_tensor(w2, w1, rt[:, 21, 0:2], ALU.mult))
                link(dve.tensor_tensor(oh1, oh1, bc(w1, NE), ALU.mult))
                link(dve.tensor_tensor(oh2, oh2, bc(w2, NE), ALU.mult))
                link(dve.tensor_tensor(wtok[:, :, :], oh1, oh2, ALU.add))
                acc = job_wait(dve, layer, "place")
                pl = acc[:, 0:TB * NE].rearrange("p (t n) -> p t n", t=TB)
                dve.wait_ge(S["mask_ready"], layer + 1)
                link(dve.scalar_tensor_tensor(place[:, :, :], pl, 1.0, mask[:, :, :], ALU.add, ALU.mult))
                link(dve.tensor_scalar(place[:, :, :], place[:, :, :], -1.0, None, ALU.add))
                link(dve.tensor_scalar(tab[0:NE, 0:7], thr[0:NE], acc[0:NE, 64:65], None, ALU.is_lt))
                dve.sem_inc(free(layer, "place"), 1)
                link(dve.tensor_reduce(tab[0:NE, 8:9], tab[0:NE, 0:7], AX.X, ALU.add))
                dve.sem_inc(S["extra_ready"], 1)
                acc = job_wait(dve, layer, "start")
                link(dve.tensor_copy(tab[0:NE, 9:10], acc[0:NE, 0:1]))
                dve.sem_inc(free(layer, "start"), 1)
                link(dve.tensor_tensor(tab[0:NE, 10:11], tab[0:NE, 9:10], tab[0:NE, 8:9], ALU.add))
                link(dve.tensor_scalar(tab[0:NE, 32:48], iota[0:NE, 0:16], tab[0:NE, 9:10], None, ALU.is_ge))
                link(dve.tensor_scalar(tab[0:NE, 48:64], iota[0:NE, 0:16], tab[0:NE, 10:11], None, ALU.is_lt))
                link(dve.tensor_tensor(tab[0:NE, 48:64], tab[0:NE, 48:64], tab[0:NE, 32:48], ALU.mult))
                link(dve.tensor_scalar(tab[0:NE, 16:32], iota[0:NE, 0:16], tab[0:NE, 9:10], 1.0, ALU.subtract, ALU.add))
                link(dve.tensor_tensor(tab[0:NE, 16:32], tab[0:NE, 16:32], tab[0:NE, 48:64], ALU.mult))
                link(dve.tensor_scalar(tab[0:NE, 0:8], iota[0:NE, 0:8], 0.0, None, ALU.mult))
                link(dve.tensor_scalar(tab[0:NE, 32:48], tab[0:NE, 48:64], idx[0:NE], None, ALU.mult))
                dve.sem_inc(S["span_ready"], 1)
                acc = job_wait(dve, layer, "table")
                link(dve.tensor_copy(tabi[0:1, 0:33], acc[0:1, 0:33]))
                dve.sem_inc(free(layer, "table"), 1)
                dve.sem_inc(S["table_ready"], 1)

                def experts(Q, turn, ne, build):
                    n0 = turn * ne
                    dve.wait_ge(Q["sel_used"], turn + 1)
                    build()
                    for e in range(ne):
                        dve.wait_ge(Q["silu_ready"], n0 + (e + 1))
                        dve.tensor_tensor(hh, sg, psum[:, 4, (e % 2) * T + P:(e % 2) * T + T], ALU.mult).then_inc(Q["hid_ready"], 1)
                        dve.wait_ge(Q["y_done"], n0 + (e + 1))
                        dve.tensor_copy(ysb, psum[:, 5, 0:T]).then_inc(Q["y_copied"], 1)

                if layer + 1 < L:
                    dve.wait_ge(S["kv_stored"], 32 * (layer + 2))
                base = layer * TURNS
                with dve.Fori(base, base + TURNS) as turn:
                    def build():
                        Q = main_sems
                        io = iota[:, 0:SL].unsqueeze(1).broadcast_to([P, EI, SL])
                        at = (turn - base) * EI
                        for tb in range(TB):
                            dve.tensor_tensor(sel[:, tb], bc(place[:, tb, bass.ds(at, EI)], SL), io,
                                              ALU.is_equal).then_inc(Q["sel_ready"], 1)
                        for tb in range(TB):
                            dve.wait_ge(Q["sel_ready"], turn * 4 + (tb * 2 + tb + 2 - tb * 2))
                            four = selw[:, tb].rearrange("p e (j s) -> p e j s", j=4)
                            w = wtok[:, tb, bass.ds(at, EI)].unsqueeze(2).unsqueeze(3).broadcast_to([P, EI, 4, SL])
                            dve.tensor_tensor(four, w, sel[:, tb].unsqueeze(2).broadcast_to([P, EI, 4, SL]), ALU.mult).then_inc(Q["sel_ready"], 1)
                    experts(main_sems, turn, EI, build)
                count = dve.value_load(tabi[0:1, 32:33], min_val=0, max_val=XB)
                with dve.If(count > 0):
                    with dve.Fori(0, count) as k:
                        e = dve.value_load(tabi[0:1, bass.ds(k, 1)], min_val=0, max_val=NE - 1)
                        b = dve.value_load(tabi[0:1, bass.ds(k + 16, 1)], min_val=0, max_val=7)

                        def build():
                            Q = extra_sems[layer]
                            for tb in range(TB):
                                dve.tensor_tensor(sel[:, tb, 0, :], place[:, tb, bass.ds(e, 1)].broadcast_to([P, SL]),
                                                  iota[:, bass.ds(b * SL, SL)], ALU.is_equal).then_inc(Q["sel_ready"], 1)
                            for tb in range(TB):
                                dve.wait_ge(Q["sel_ready"], k * 4 + (tb + 2))
                                four = selw[:, tb, 0, :].rearrange("p (j s) -> p j s", j=4)
                                w = wtok[:, tb, bass.ds(e, 1)].unsqueeze(2).broadcast_to([P, 4, SL])
                                dve.tensor_tensor(four, w, sel[:, tb, 0:1, :].broadcast_to([P, 4, SL]), ALU.mult).then_inc(Q["sel_ready"], 1)
                        experts(extra_sems[layer], k, 1, build)
                for i in range(4):
                    add_x(layer, "moe", i)
            norm(ROW_FIN, 0, False)

        @block.tensor
        def _(pe):
            def done(ins):
                ins.then_inc(S["acc_ready"], 1)

            def turn_in(name, src, loaded):
                pe.wait_ge(S[loaded], 16)
                for i in range(4):
                    acc = job_begin(pe, 0, name, i)
                    for c in range(2):
                        for tb in range(TB):
                            d = (2 * i + c) * P
                            ins = pe.transpose(acc[:, c * T + tb * P:c * T + (tb + 1) * P], src[:, tb, d:d + P], ident)
                    done(ins)

            n_norm = [0]

            def norm(layer, name):
                acc = job_begin(pe, layer, name)
                for k in range(KC):
                    if k % 2 == 0:
                        pe.wait_ge(S["sq_ready"], 4 * n_norm[0] + k // 2 + 1)
                    ins = pe.matmul(acc[:, 0:T], ones[:, :], hT[:, k, :], start=k == 0, stop=k == KC - 1)
                done(ins)
                n_norm[0] += 1

            def piece(layer, unit, half):
                n = PIECE_NO[layer, unit, half]
                pe.wait_ge(S["w_split_pool" if by_pool(unit) else "w_split_dve"], split_count(n))
                return high_view(layer, unit, half), piece_view(w_lo, layer, unit, half)

            def three(acc, w, x, kc, stationary, moving, waits=None):
                for k in range(kc):
                    if waits and k % 2 == 0:
                        waits(k // 2)
                    passes = ((0, 0), (0, 1), (1, 0))
                    for n, (a, b) in enumerate(passes):
                        ins = pe.matmul(acc, stationary(a, k), moving(b, k), start=k == 0 and n == 0,
                                        stop=k == kc - 1 and n == 2)
                return ins

            def dense(layer, unit, job, x, kc=KC, i0=0, waits=None):
                for half in range(2):
                    w = piece(layer, unit, half)
                    acc = job_begin(pe, layer, job, i0 + half)
                    for c in range(2):
                        ins = three(acc[:, c * T:(c + 1) * T], w, x, kc, lambda a, k: w[a][:, k, c * P:(c + 1) * P],
                                    lambda b, k: x[b][:, k, :], waits if half == 0 and c == 0 else None)
                    done(ins)

            def dense_tokens(layer, unit, job, x, i0=0):
                for half in range(2):
                    w = piece(layer, unit, half)
                    acc = job_begin(pe, layer, job, i0 + half)
                    for tb in range(TB):
                        ins = three(acc[:, tb * T:(tb + 1) * T], w, x, KC, lambda a, k: x[a][:, k, tb * P:(tb + 1) * P],
                                    lambda b, k: w[b][:, k, :])
                    done(ins)

            h, m, o = (h_hi, h_lo), (m_hi, m_lo), (h_hi, o_lo)
            n_h = [0]

            def h_part(i):
                pe.wait_ge(S["h_ready"], 1 + 4 * n_h[0] + i + 1)

            def m_part(layer):
                return lambda i: pe.wait_ge(S["m_ready"], KC * layer + 2 * i + 2)

            pe.wait_ge(S["cst_loaded"], 16 * 5)
            turn_in("mem", mem_raw, "mem_loaded")
            pe.wait_ge(S["rows_loaded"], 16 * 14)
            for layer in range(L):
                acc = job_begin(pe, 0, "vec", layer)
                done(pe.transpose(acc[:, 0:ROWS], vecrows[:, layer, :], ident[0:ROWS, 0:ROWS]))
            pe.wait_ge(S["pool_step"], 1)
            norm(0, "memnorm")
            turn_in("x", x_raw, "x_loaded")
            for i in range(2):
                dense(0, f"xk{i}", "xk", m, i0=2 * i, waits=m_part(0) if i == 0 else None)
            norm(0, "norm0")
            for i in range(2):
                dense_tokens(0, f"xv{i}", "xv", m, i0=2 * i)
            for layer in range(L):
                if layer:
                    norm(layer, "norm0")
                dense(layer, "q", "q", h, waits=h_part)
                n_h[0] += 1
                w = piece(layer, "kv", 0)
                acc = job_begin(pe, layer, "k")
                done(three(acc[:, 0:T], w, h, KC, lambda a, k: w[a][:, k, 0:P], lambda b, k: h[b][:, k, :]))
                acc = job_begin(pe, layer, "v")
                for tb in range(TB):
                    ins = three(acc[:, tb * T:(tb + 1) * T], w, h, KC, lambda a, k: h[a][:, k, tb * P:(tb + 1) * P],
                                lambda b, k: w[b][:, k, :])
                done(ins)
                dense(layer, "u", "u", h)
                pe.wait_ge(S["qraw_ready"], 3 * layer + 3)
                for i in range(2):
                    acc = job_begin(pe, layer, "rot", i)
                    done(pe.matmul(acc, rotm, qraw[:, 2 * i:2 * i + 2, :].rearrange("p c t -> p (c t)"), start=True, stop=True))
                acc = job_begin(pe, layer, "rot", 2)
                pe.matmul(acc[:, 0:T], rotm, kraw[:, 0, :], start=True, stop=True)
                done(pe.matmul(acc[:, T:2 * T], rotswap, kraw[:, 0, :], start=True, stop=True))
                acc = job_begin(pe, layer, "rot", 3)
                done(pe.matmul(acc[:, 0:T], swapm, kraw[:, 0, :], start=True, stop=True))
                dense_tokens(layer, "vg", "vg", h)
                pe.wait_ge(S["ws_loaded"], 16 * (layer + 1))
                acc = job_begin(pe, layer, "ws")
                for g in range(4):
                    ins = pe.transpose(acc[:, g * P:(g + 1) * P], wsr[:, g, :], ident)
                done(ins)
                pe.wait_ge(S["qk_ready"], 3 * layer + 3)
                for i in range(4):
                    g, p = i // 2, i % 2
                    acc = job_begin(pe, layer, "s", i).rearrange("p (h k) -> p h k", h=4)
                    for half in range(2):
                        c = 2 * p + half
                        for hp in range(2):
                            q = qT[:, 2 * g + hp, c * 64:(c + 1) * 64]
                            rows = slice(half * 64, half * 64 + 64)
                            wins = [(0, 128, 64), (64, 64, 64)] if c == 2 else [(0, (0, 0, None, 128)[c], 128)]
                            for at, first, n in wins:
                                ins = pe.matmul(acc[rows, 2 * hp:2 * hp + 2, at:at + n], q, kbd[:, g, :, first:first + n],
                                                start=True, stop=True)
                    done(ins)
                dense(layer, "cx", "cx", h)
                for i in range(4):
                    pe.wait_ge(S["prob_ready"], 4 * layer + i + 1)
                    acc = job_begin(pe, layer, "pt", i)
                    for hd in range(4):
                        ins = pe.transpose(acc[:, hd * P:(hd + 1) * P], prob[:, i, hd, :], ident)
                    done(ins)
                dense(layer, "cb", "cb", h)
                pe.wait_ge(S["v_ready"], 3 * layer + 3)
                pe.wait_ge(S["probT_ready"], 4 * layer + 4)
                for g in range(2):
                    acc = job_begin(pe, layer, "pv", g).rearrange("p (c t) -> p c t", c=2)
                    for c in range(4):
                        v = vtok[:, (0, 0, 2, 1)[c], g * 64:g * 64 + 64]
                        pt = probT[:, 2 * g + c // 2, :].rearrange("p (a b q) -> p a b q", a=2, b=2)
                        for par in range(2):
                            ins = pe.matmul(acc[par * 64:par * 64 + 64, :, c * 64:(c + 1) * 64], v,
                                            pt[:, :, par, (c % 2) * 64:(c % 2) * 64 + 64], start=True, stop=True)
                    done(ins)
                dense(layer, "cc", "cc", h)
                pe.wait_ge(S["vn_ready"], layer + 1)
                pe.wait_ge(S["ws_masked"], layer + 1)
                pe.wait_ge(S["ln_loaded"], 48 * (layer + 1))
                for tb in range(TB):
                    acc = job_begin(pe, layer, "mixed", tb)
                    pe.matmul(acc, ones[0:1, :], bs[0:1, :], start=True, stop=False, skip_group_check=True)
                    for g in range(4):
                        ins = pe.matmul(acc[:, g * P:(g + 1) * P], vg[:, tb, g * P:(g + 1) * P], wsT[:, g, :],
                                        start=False, stop=g == 3, skip_group_check=True)
                    done(ins)
                for hf in range(2):
                    for i in range(3):
                        dense(layer, f"gate{i}{hf}", f"gate{i}{hf}", h)
                        if hf == 0:
                            pe.wait_ge(S["y_ready"], 4 * layer + (2, 4, 4)[i])
                        dense(layer, f"br{i}{hf}", f"br{i}{hf}", ((ya_hi, ya_lo), (yb_hi, yb_lo), (yc_hi, yc_lo))[i], kc=MC)
                for i in range(2):
                    dense(layer, f"wo{i}", "wo", (h_hi, merged_lo), i0=2 * i,
                          waits=(lambda j: pe.wait_ge(S["merged_ready"], 4 * layer + j + 1)) if i == 0 else None)
                norm(layer, "norm1")
                for i in range(2):
                    dense(layer, f"xq{i}", "xq", h, i0=2 * i, waits=h_part if i == 0 else None)
                n_h[0] += 1
                pe.wait_ge(S["kv_loaded"], 32 * (layer + 1))
                for i in range(4):
                    tb, hp = i // 2, i % 2
                    if tb == 0:
                        pe.wait_ge(S["qx_ready"], 4 * layer + (2, 4)[hp])
                    acc = job_begin(pe, layer, "xs", i)
                    for hd in range(2):
                        for k in range(2):
                            c = 2 * (2 * hp + hd) + k
                            ins = pe.matmul(acc[:, hd * T:(hd + 1) * T], qxT[:, c, tb * P:(tb + 1) * P], kxT[:, c, :],
                                            start=k == 0, stop=k == 1)
                    done(ins)
                for i in range(4):
                    pe.wait_ge(S["xprob_ready"], 4 * layer + i + 1)
                    acc = job_begin(pe, layer, "xpt", i)
                    for j in range(4):
                        ins = pe.transpose(acc[:, j * P:(j + 1) * P], xprob[:, i, j * P:(j + 1) * P], ident)
                    done(ins)
                pe.wait_ge(S["xprobT_ready"], 4 * layer + 4)
                for hd in range(4):
                    acc = job_begin(pe, layer, "xpv", hd)
                    for c in range(2):
                        for kb in range(2):
                            ins = pe.matmul(acc[:, c * T:(c + 1) * T], vx[:, kb, (2 * hd + c) * P:(2 * hd + c + 1) * P],
                                            xprobT[:, kb, hd, :], start=kb == 0, stop=kb == 1)
                    done(ins)
                for i in range(2):
                    dense(layer, f"xo{i}", "xo", o, i0=2 * i,
                          waits=(lambda j: pe.wait_ge(S["o_ready"], 4 * layer + j + 1)) if i == 0 else None)
                norm(layer, "norm2")
                pe.wait_ge(S["h_full"], 4 * n_norm[0])
                pe.wait_ge(S["wr_loaded"], 32 * (layer + 1))
                acc = job_begin(pe, layer, "router")
                for tb in range(TB):
                    for k in range(KC):
                        ins = pe.matmul(acc[:, tb * (NG + NE):(tb + 1) * (NG + NE)], hT[:, k, tb * P:(tb + 1) * P], wr[:, k, :],
                                        start=k == 0, stop=k == KC - 1)
                done(ins)
                for i in range(4):
                    tb, half = i // 2, i % 2
                    acc = job_begin(pe, layer, "htok", i)
                    for c in range(4):
                        ins = pe.transpose(acc[:, c * P:(c + 1) * P], hT[:, 4 * half + c, tb * P:(tb + 1) * P], ident)
                    done(ins)
                for i in range(2) if layer + 1 < L else []:
                    dense(layer + 1, f"xk{i}", "xk", m, i0=2 * i, waits=m_part(layer + 1) if i == 0 else None)
                for i in range(2) if layer + 1 < L else []:
                    dense_tokens(layer + 1, f"xv{i}", "xv", m, i0=2 * i)
                pe.wait_ge(S["mask_ready"], layer + 1)
                acc = job_begin(pe, layer, "place")
                pe.matmul(acc[:, 0:NE], tri, mask[:, 0, :], start=True, stop=True)
                pe.matmul(acc[:, NE:2 * NE], tri, mask[:, 1, :], start=True, stop=False)
                pe.matmul(acc[:, NE:2 * NE], ones[:, :], mask[:, 0, :], start=False, stop=True)
                pe.matmul(acc[0:NE, 64:65], mask[:, 0, :], ones[:, 0:1], start=True, stop=False)
                done(pe.matmul(acc[0:NE, 64:65], mask[:, 1, :], ones[:, 0:1], start=False, stop=True))
                pe.wait_ge(S["extra_ready"], layer + 1)
                acc = job_begin(pe, layer, "start")
                done(pe.matmul(acc[0:NE, 0:1], tri[0:NE, 0:NE], tab[0:NE, 8:9], start=True, stop=True))
                pe.wait_ge(S["span_ready"], layer + 1)
                acc = job_begin(pe, layer, "table")
                pe.matmul(acc[0:1, 0:16], ones[0:NE, 0:1], tab[0:NE, 32:48], start=True, stop=True)
                pe.matmul(acc[0:1, 16:32], ones[0:NE, 0:1], tab[0:NE, 16:32], start=True, stop=True)
                done(pe.matmul(acc[0:1, 32:33], ones[0:NE, 0:1], tab[0:NE, 8:9], start=True, stop=True))
                any2 = iota.unsqueeze(1).broadcast_to([P, 2, T])
                pe.wait_ge(S["zero_ready"], 1)
                for j in range(4):
                    acc = job_begin(pe, layer, "moe", j)
                    row = slice(32 * j, 32 * j + 1)
                    pe.matmul(acc, zero[row, :], any2[row], start=True, stop=False, skip_group_check=True,
                              tile_position=(32 * j, 0))
                pe.wait_ge(S["htok_ready"], 4 * layer + 4)

                def experts(Q, turn, ne, slot_wait, slot_done, slot):
                    n0 = turn * ne
                    sel_n = turn * 4 + 4
                    pe.wait_ge(Q["sel_ready"], sel_n)
                    for e in range(ne):
                        if e:
                            pe.wait_ge(Q["swt_ready"], n0 + e)
                        for tb in range(TB):
                            ins = pe.transpose(psum[:, 6, tb * P:(tb + 1) * P], selw[:, tb, e, :], ident)
                        ins.then_inc(Q["swt_turned"], 1)
                    for r in range(4):
                        if r:
                            pe.wait_ge(Q["xe_ready"], turn * 4 + r)
                        for c in range(2):
                            for tb in range(TB):
                                d = (2 * r + c) * P
                                ins = pe.matmul(psum[:, 7, c * T:c * T + ne * SL], htok[:, tb, d:d + P],
                                                sel[:, tb, 0:ne, :].rearrange("p e s -> p (e s)"), start=tb == 0, stop=tb == 1)
                        ins.then_inc(Q["gathered"], 1)
                    pe.wait_ge(Q["xe_ready"], turn * 4 + 4)
                    pe.wait_ge(Q["swt_ready"], n0 + ne)
                    for e in range(ne):
                        G = psum[:, 4, (e % 2) * T:(e % 2) * T + T]
                        for k in range(KC):
                            if k % 4 == 0:
                                slot_wait(e, k // 4)
                            w = ring[:, slot(e, k // 4), :].rearrange("p (k a b) -> p k a b", k=4, a=2)
                            for j in range(4):
                                ins = pe.matmul(G[32 * j:32 * j + 32, :], xTe[:, k, e * SL:(e + 1) * SL],
                                                w[:, k % 4, :, j * P:(j + 1) * P], start=k == 0, stop=k == KC - 1,
                                                tile_position=(0, 32 * j))
                                if e == 0 and k == 0 and j == 0:
                                    ins.then_inc(Q["sel_used"], 1)
                            if k == 3:
                                slot_done(ins)
                        ins.then_inc(Q["gu_ready"], 1)
                        pe.wait_ge(Q["hid_ready"], n0 + (e + 1))
                        pe.transpose(psum[:, 6, T:T + P], hh, ident).then_inc(Q["hid_turned"], 1)
                        pe.wait_ge(Q["hidT_ready"], n0 + (e + 1))
                        slot_wait(e, 2)
                        w = ring[:, slot(e, 2), :].rearrange("p (k n) -> p k n", k=4)
                        for k in range(4):
                            for j in range(4):
                                ins = pe.matmul(psum[32 * j:32 * j + 32, 5, 0:T], hhT[:, k * SL:(k + 1) * SL],
                                                w[:, k, j * T:(j + 1) * T], start=k == 0, stop=k == 3, tile_position=(0, 32 * j))
                                if k == 0 and j == 0:
                                    slot_done(ins)
                        ins.then_inc(Q["y_done"], 1)
                        pe.wait_ge(Q["y_copied"], n0 + (e + 1))
                        for c in range(2):
                            for j in range(4):
                                ins = pe.matmul(psum[:, j, c * T:(c + 1) * T], ysb[32 * j:32 * j + 32, c * P:(c + 1) * P],
                                                swt[32 * j:32 * j + 32, e, :], start=False, stop=False,
                                                skip_group_check=True, tile_position=(32 * j, 0))
                                if c == 0 and j == 0:
                                    slot_done(ins)
                    return ins

                base = layer * TURNS
                pe.drain().then_inc(main_sems["sel_used"], 1) if layer == 0 else None
                u0 = FIRST_EXPERT[layer]
                with pe.Fori(base, base + TURNS) as turn:
                    def slot(e, x):
                        return (u0 + 3 * e + x) % R

                    def slot_wait(e, x):
                        u = u0 + 3 * e + x
                        per = 3 * EI // R
                        pe.wait_ge(slot_loaded[u % R], turn * (16 * per) + 16 * (u // R + 1 - base * per))

                    def slot_done(ins):
                        ins.then_inc(S["units_used"], 1)
                    experts(main_sems, turn, EI, slot_wait, slot_done, slot)
                X = extra_sems[layer]
                pe.drain().then_inc(X["sel_used"], 1)
                pe.drain().then_inc(X["used"], 1)
                pe.wait_ge(S["table_ready"], layer + 1)
                count = pe.value_load(tabi[0:1, 32:33], min_val=0, max_val=XB)
                u1 = FIRST_EXPERT[layer] + 3 * NE
                with pe.If(count > 0):
                    with pe.Fori(0, count) as k:
                        def slot(e, x):
                            return (u1 + x) % R

                        def slot_wait(e, x):
                            pe.wait_ge(X["loaded"], k * 48 + 48)

                        def slot_done(ins):
                            pass
                        experts(X, k, 1, slot_wait, slot_done, slot).then_inc(X["used"], 1)
                for j in range(4):
                    row = slice(32 * j, 32 * j + 1)
                    done(pe.matmul(psum[:, j, :], zero[row, :], any2[row], start=False, stop=True, skip_group_check=True,
                                   tile_position=(32 * j, 0)))
            norm(L, "norm0")
            pe.wait_ge(S["h_full"], 4 * n_norm[0])
            for i in range(4):
                acc = job_begin(pe, L, "out", i)
                for c in range(4):
                    ins = pe.transpose(acc[:, c * P:(c + 1) * P], hT[:, 4 * (i % 2) + c, (i // 2) * P:(i // 2 + 1) * P], ident)
                done(ins)


_INS = ['x', 'mem', 'positions', 'mix_norm', 'w_in', 'b_gate', 'attn_sinks', 'gmlp_ln_g', 'gmlp_ln_b',
        'gmlp_w_s', 'gmlp_b_s', 'conv_w', 'w_branch', 'w_out', 'xattn_norm', 'mem_norm', 'w_xq', 'w_xkv',
        'w_xo', 'ffn_norm', 'w_router_group', 'b_router_group', 'w_router_expert', 'b_router_expert',
        'w_expert_in', 'w_expert_out', 'final_norm']


def constants():
    c = np.zeros((P, C_END), np.float32)
    p = np.arange(P)
    c[:, C_ID:C_ID + P] = np.eye(P)
    c[:, C_TRI:C_TRI + P] = p[:, None] < p[None, :]
    for m in range(P):
        source = m + 32 if m % 64 < 32 else m - 32
        c[source, C_ROT + m] = c[(source + 64) % P, C_RSW + m] = -1.0 if m % 64 < 32 else 1.0
        c[(m + 64) % P, C_SWAP + m] = 1.0
    half = 32
    inv = np.power(np.float32(10000.0), -np.arange(half, dtype=np.float32) / np.float32(half)).astype(np.float32)
    c[:, C_INV] = inv[p % half]
    c[:, C_IOTA:C_IOTA + T] = np.arange(T)
    c[:, C_IDX] = p
    c[:, C_THR:C_THR + 7] = SL * np.arange(1, 8)
    return c


def kernel(**inputs):
    import concourse.bacc as bacc
    from concourse.bass_utils import run_bass_kernel_spmd

    nc = bacc.Bacc("TRN2", target_bir_lowering=False, num_devices=1)
    arrays, aps = {}, {}
    for name in _INS:
        a = np.ascontiguousarray(inputs[name])
        arrays[f"in_{name}"] = a
        aps[name] = nc.dram_tensor(f"in_{name}", a.shape, mybir.dt.from_np(a.dtype), kind="ExternalInput").ap()
    arrays["in_cst"] = constants()
    aps["cst"] = nc.dram_tensor("in_cst", (P, C_END), F32, kind="ExternalInput").ap()
    out = nc.dram_tensor("out", (1, T, D), F32, kind="ExternalOutput").ap()
    trunk(nc, aps, out)
    r = run_bass_kernel_spmd(nc, [arrays], core_ids=[0])
    return r.results[0]["out"]
```

```python
from contextlib import ExitStack

import numpy as np

import concourse.bass as bass
from concourse import mybir

F32 = mybir.dt.float32
F32R = mybir.dt.float32r
I32 = mybir.dt.int32
ALU = mybir.AluOpType
ACT = mybir.ActivationFunctionType
AX = mybir.AxisListType

P = 128
D = 1024
T = 256
L = 2
KC = D // P
TB = T // P
MW = 512
MC = MW // P
NE = 32
NG = 4
EPG = NE // NG
SL = 32
XB = (2 * T) // SL - 1
EPS = 1e-6
NEG = -1e30
R = 6
UNIT = 4096
EI = 8
TURNS = NE // EI

ROW_MIX, ROW_GATE, ROW_CONV, ROW_XN, ROW_MN, ROW_FF, ROW_FIN = 0, 8, 32, 44, 52, 60, 68
ROWS = 76
C_ID, C_TRI, C_ROT, C_SWAP, C_RSW, C_INV, C_IOTA, C_IDX, C_THR, C_END = 0, 128, 256, 384, 512, 640, 641, 897, 898, 905

KV_UNITS = ["xk0", "xk1", "xv0", "xv1"]
MIX_UNITS = (["q", "kv", "u", "vg", "cx", "cb", "cc"]
             + [f"{n}{i}{h}" for h in range(2) for i in range(3) for n in ("gate", "br")]
             + ["wo0", "wo1", "xq0", "xq1", "xo0", "xo1"])


def plan_units():
    number, first_expert, pieces, at = {}, [], [], 0
    for layer in range(L):
        names = [(layer, n) for n in (KV_UNITS if layer == 0 else []) + MIX_UNITS]
        names += [(layer + 1, n) for n in KV_UNITS if layer + 1 < L]
        for key in names:
            number[key] = at
            at += 1
            pieces += [key + (h,) for h in range(1 if key[1] == "kv" else 2)]
        first_expert.append(at)
        at += 3 * NE + 3
    return number, first_expert, pieces


UNIT_NO, FIRST_EXPERT, PIECES = plan_units()
PIECE_NO = {key: n for n, key in enumerate(PIECES)}
HI = 3

MIX_JOBS = ([("q", 2), ("k", 1), ("v", 1), ("u", 2), ("rot", 4), ("vg", 2), ("ws", 1), ("s", 4),
             ("cx", 2), ("cb", 2), ("pt", 4), ("cc", 2), ("pv", 2), ("mixed", 2)]
            + [(f"{n}{i}{h}", 2) for h in range(2) for i in range(3) for n in ("gate", "br")]
            + [("wo", 4), ("norm1", 1), ("xq", 2), ("xs", 2), ("xq", 2, 2), ("xpt", 2), ("xs", 2, 2), ("xpv", 2),
               ("xpt", 2, 2), ("xpv", 2, 2), ("xo", 4), ("norm2", 1), ("moe", 4)])
ROUTER_JOBS = [("router", 1), ("htok", 4)]
K_JOBS, V_JOBS = [("xk", 4)], [("xv", 4)]


def plan_jobs():
    def jobs(layer, table):
        return [(layer, row[0], i + (row[2] if len(row) > 2 else 0)) for row in table for i in range(row[1])]

    order = jobs(0, [("mem", 4), ("vec", 2), ("memnorm", 1), ("x", 4), ("xk", 2), ("norm0", 1), ("xk", 2, 2), ("xv", 4)])
    for layer in range(L):
        order += jobs(layer, ([("norm0", 1)] if layer else []) + MIX_JOBS)
        order += jobs(layer + 1, K_JOBS) if layer + 1 < L else []
        order += jobs(layer, ROUTER_JOBS)
        order += jobs(layer + 1, V_JOBS) if layer + 1 < L else []
        order += jobs(layer, [("place", 1), ("start", 1), ("table", 1)])
    order += jobs(L, [("norm0", 1), ("out", 4)])
    bank_of = {"moe": None, "place": 4, "start": 5, "table": 5}
    plan, used, at, held = {}, [0] * 8, 0, 0
    for key in order:
        bank = bank_of.get(key[1], at % 8)
        if bank is None:
            bank, held = key[2], 4
        elif key[1] == "norm0":
            held = 0
        if key[1] not in bank_of and bank < held:
            bank = held
        plan[key] = [bank, 0, used[bank]]
        used[bank] += 1
        at = bank + 1
    ended = []
    for n, key in enumerate(order):
        if key[1] != "moe":
            ended.append(key)
        if key[1] == "table":
            ended += [(key[0], "moe", i) for i in range(4)]
    for n, key in enumerate(ended):
        plan[key][1] = n + 1
    return plan


JOB = plan_jobs()


def piece_job(layer, unit, half):
    if unit == "kv":
        return JOB[layer, "v", 0]
    if unit[:2] in ("xk", "xv", "wo", "xq", "xo"):
        return JOB[layer, unit[:2], 2 * int(unit[2]) + half]
    return JOB[layer, unit, half]


def trunk(nc, A, out):
    with ExitStack() as ctx:
        def sb(name, shape, dt=F32):
            return ctx.enter_context(nc.sbuf_tensor(name, shape, dt))

        def sem(name):
            return ctx.enter_context(nc.semaphore(name))

        def placed(name, shape, dt=F32):
            at = -(-nc.sbuf_base // 32) * 32
            return sb(name, shape, dt), at

        ring, ring_at = placed("ring", [P, R, UNIT])
        xT = sb("xT", [P, KC, T])
        hT, hT_at = placed("hT", [P, KC, T])
        AW = 10640
        h_hi, hhi_at = placed("h_hi", [P, KC, T], F32R)
        w_hi = sb("w_hi", [P, HI, UNIT // 2], F32R)
        arena, arena_at = placed("arena", [P, AW])
        psum = ctx.enter_context(nc.psum_tensor("banks", [P, 8, 512], F32))
        cst = sb("cst", [P, C_END])
        ones = sb("ones", [P, P])
        cosT = sb("cosT", [P, T])
        sinT = sb("sinT", [P, T])
        vec = sb("vec", [P, L, ROWS])
        sinks = sb("sinks", [P, L, 8])
        rbias = sb("rbias", [P, L, NG + NE])
        bs = sb("bs", [1, 512])
        stat = sb("stat", [P, 512])
        rstd = stat[:, 0:T]
        std = stat[:, T:2 * T]
        small = sb("small", [P, 96])
        wr = sb("wr", [P, KC, NG + NE])
        lnt = sb("lnt", [P, 2, MW])
        wsT = sb("wsT", [P, 4, P])
        tabi = sb("tabi", [1, 2 * 16 + 1], I32)
        zero = sb("zero", [P, P])
        mhat_dram = nc.dram_tensor("mhat", (P, KC * T), F32).ap()
        kv_dram = nc.dram_tensor("kv", (L, 2, P, KC * T), F32).ap()

        ident = cst[:, C_ID:C_ID + P]
        tri = cst[:, C_TRI:C_TRI + P]
        rotm = cst[:, C_ROT:C_ROT + P]
        swapm = cst[:, C_SWAP:C_SWAP + P]
        rotswap = cst[:, C_RSW:C_RSW + P]
        inv = cst[:, C_INV:C_INV + 1]
        iota = cst[:, C_IOTA:C_IOTA + T]
        idx = cst[:, C_IDX:C_IDX + 1]
        thr = cst[:, C_THR:C_THR + 7]

        def shaped(v, shape):
            if len(shape) == 2:
                v = v.rearrange("p (a b) -> p a b", b=shape[1])
            if len(shape) == 3:
                v = v.rearrange("p (a b c) -> p a b c", b=shape[1], c=shape[2])
            return v

        def region(at, *shape):
            n = int(np.prod(shape))
            assert at + n <= AW, (at, n)
            return shaped(arena[:, at:at + n], shape)

        def over(name, base, at, *shape, dt=F32R):
            v = nc.alloc_sbuf_tensor_at(name, [P, int(np.prod(shape))], dt, offset=base + 4 * at)
            return shaped(v[:, :], shape)

        w_lo = over("w_lo", ring_at, 0, R, UNIT)
        h_lo = over("h_lo", hT_at, 0, KC, T)
        htok = over("htok", hhi_at, 0, TB, D, dt=F32)

        mhatT = region(2048, KC, T)
        m_lo = over("m_lo", arena_at, 2048, KC, T)
        m_hi = over("m_hi", arena_at, 4480, KC, T)
        k_made = region(6528, KC, T)
        v_made = region(0, TB, D)
        mem_raw = region(6528, TB, D)
        x_raw = region(8576, TB, D)
        vecrows = region(4096, L, P)[0:ROWS]
        mem_T = region(0, KC, T)
        posrow = lnt[:, 0, 0:T].bitcast(I32)
        qT = region(0, MC, T)
        kbd = region(1024, 2, 2, T)
        cx = region(0, MC, T)
        cb = region(1024, MC, T)
        merged = region(0, KC, T)
        merged_lo = over("merged_lo", arena_at, 0, KC, T)
        vtok = region(2048, 3, P)
        uT = region(2432, MC, T)
        yb_lo = over("yb_lo", arena_at, 2432, MC, T)
        vg = region(3456, TB, MW)
        gtmp = region(3456, 512)
        prob = region(4480, 4, 4, P)
        qraw = region(4480, MC, T)
        kraw = region(5504, 2, T)
        z = region(4480, MC, T + 2)
        sig = region(4480, 2, 512)
        ycT = region(5512, MC, T)
        yc_lo = over("yc_lo", arena_at, 5512, MC, T)
        probT = region(6536, 4, 512)
        yb_hi = over("yb_hi", arena_at, 6536, MC, T)
        yc_hi = over("yc_hi", arena_at, 7560, MC, T)
        wsr = region(8584, 4, P)
        ya_lo = over("ya_lo", arena_at, 8584, MC, T)
        ya_hi = over("ya_hi", arena_at, 9608, MC, T)
        ln_sq = region(8584, 2 * MC, P)
        qxT = region(0, KC, T)
        o_lo = over("o_lo", arena_at, 0, KC, T)
        xprob = region(2048, 4, 512)
        kxT = region(4480, KC, T)
        vx = region(6528, TB, D)
        xprobT = region(8576, TB, 4, T)
        xTe = region(2048, KC, EI * SL)
        swt = region(4480, EI, T)
        selw = region(6528, TB, EI, 4 * SL)
        logit = region(8576, TB, NG + NE)
        rt = region(8660, 22, NE)
        place = region(9370, TB, NE)
        wtok = region(9434, TB, NE)
        mask = region(9498, TB, NE)
        tab = region(9562, 64)
        sg = region(9626, P)
        hh = region(9754, P)
        hhT = region(9882, P)
        sel = region(10010, TB, EI, SL)
        ysb = region(0, T)

        slot_loaded = [sem(f"slot_loaded{i}") for i in range(R)]
        bank_free = [sem(f"bank_free{i}") for i in range(8)]
        S = {n: sem(n) for n in (
            "acc_ready", "units_used", "act_step", "dve_step", "pool_step", "x_loaded", "mem_loaded", "cst_loaded", "small_loaded", "rows_loaded",
            "ws_loaded", "ln_loaded", "wr_loaded", "x_ready", "mem_ready", "sq_ready", "sum_ready", "std_ready", "h_full", "h_high", "h_ready",
            "vec_ready", "angles", "rope_ready", "qraw_ready", "qk_ready", "v_ready", "gelu_ready", "ln_std", "ln_var", "vn_ready",
            "ws_ready", "ws_masked", "s_shifted", "s_exped", "prob_ready", "probT_ready", "c_ready", "y_full", "y_high", "y_ready",
            "sig_ready", "sig_used", "merged_full", "merged_high", "merged_ready", "kv_made", "k_stored", "v_stored", "kv_loaded",
            "mhat_ready", "mhat_stored", "mhat_loaded", "m_high", "m_ready",
            "qx_ready", "xs_shifted", "xs_exped", "xprob_ready", "xprobT_ready", "o_high", "o_ready", "htok_ready", "r_shift",
            "r_exp", "mask_ready", "extra_ready", "span_ready", "table_ready", "out_ready", "stored", "zero_ready", "eps_ready",
            "w_high", "w_split_dve", "w_split_pool")}

        def moe_sems(tag):
            return {n: sem(f"{n}_{tag}") for n in (
                "sel_ready", "sel_used", "swt_turned", "swt_ready", "gathered", "xe_ready", "gu_ready", "silu_ready",
                "hid_ready", "hid_turned", "hidT_ready", "y_done", "y_copied")}

        main_sems = moe_sems("main")
        extra_sems = [dict(moe_sems(f"extra{i}"), loaded=sem(f"extra_loaded{i}"), used=sem(f"extra_used{i}")) for i in range(L)]

        def piece_view(tensor, layer, unit, half):
            kc = MC if unit.startswith("br") else KC
            n = 256 if unit == "kv" else 512
            w = tensor[:, UNIT_NO[layer, unit] % R, 0:kc * n].rearrange("p (k n) -> p k n", k=kc)
            return w[:, :, half * 256:half * 256 + 256]

        def high_view(layer, unit, half):
            kc = MC if unit.startswith("br") else KC
            return w_hi[:, PIECE_NO[layer, unit, half] % HI, 0:kc * 256].rearrange("p (k n) -> p k n", k=kc)

        def ahead_of(layer, unit, half, ahead):
            n = PIECE_NO[layer, unit, half]
            ends = [PIECE_NO[i + 1, KV_UNITS[-1], 1] for i in range(L - 1)] + [len(PIECES) - 1]
            return min([n + ahead] + [end for end in ends if end >= n])

        def by_pool(piece):
            layer, unit, half = piece
            return unit[:2] in ("xk", "xv") or unit == "br00" or (layer > 0 and unit in ("q", "kv")) or (unit, half) in (("wo0", 1), ("cc", 1))

        def split_count(n):
            mine = by_pool(PIECES[n])
            return sum(by_pool(p) == mine for p in PIECES[:n + 1])

        def job_begin(pe, layer, name, i=0):
            bank, _, before = JOB[layer, name, i]
            if before:
                pe.wait_ge(bank_free[bank], before)
            return psum[:, bank, :]

        def job_wait(eng, layer, name, i=0):
            bank, ready, _ = JOB[layer, name, i]
            eng.wait_ge(S["acc_ready"], ready)
            return psum[:, bank, :]

        def free(layer, name, i=0):
            return bank_free[JOB[layer, name, i][0]]

        block = ctx.enter_context(nc.Block())

        @block.sync
        def _(sp):
            def cols(w, a, b):
                return w.rearrange("(k p) n -> p k n", p=P)[:, :, a:b]

            def source(layer, name):
                if name in ("q", "kv", "u", "vg", "cx", "cb", "cc"):
                    a = {"q": 0, "kv": 512, "u": 768, "vg": 1280, "cx": 1792, "cb": 2304, "cc": 2816}[name]
                    return cols(A["w_in"][layer], a, a + (256 if name == "kv" else 512))
                if name.startswith("gate"):
                    a = 3328 + int(name[4]) * D + int(name[5]) * 512
                    return cols(A["w_in"][layer], a, a + 512)
                if name.startswith("br"):
                    h = int(name[3])
                    return cols(A["w_branch"][layer, int(name[2])], h * 512, h * 512 + 512)
                w, a = {"wo": ("w_out", 0), "xk": ("w_xkv", 0), "xv": ("w_xkv", D), "xq": ("w_xq", 0),
                        "xo": ("w_xo", 0)}[name[:2]]
                a += int(name[2]) * 512
                return cols(A[w][layer], a, a + 512)

            def slot_is_free(u):
                if u < R:
                    return
                before = [key for key, n in UNIT_NO.items() if n == u - R]
                reserved = any(0 <= u - R - FIRST_EXPERT[i] - 3 * NE < 3 for i in range(L))
                if reserved:
                    return
                if before:
                    layer, name = before[0]
                    sp.wait_ge(S["acc_ready"], piece_job(layer, name, 0 if name == "kv" else 1)[1])
                else:
                    layer = max(i for i in range(L) if FIRST_EXPERT[i] <= u - R)
                    sp.wait_ge(S["units_used"], 3 * NE * layer + u - R - FIRST_EXPERT[layer] + 1)

            def load_dense(layer, name):
                u = UNIT_NO[layer, name]
                src = source(layer, name)
                slot_is_free(u)
                _, kc, n = src.shape
                sp.dma_start(ring[:, u % R, 0:kc * n].rearrange("p (k n) -> p k n", k=kc), src).then_inc(slot_loaded[u % R], 16)

            sp.dma_start(mem_raw, A["mem"][0].rearrange("(t p) d -> p t d", p=P)).then_inc(S["mem_loaded"], 16)
            sp.dma_start(x_raw, A["x"][0].rearrange("(t p) d -> p t d", p=P)).then_inc(S["x_loaded"], 16)
            for src, at in ((A["mix_norm"], ROW_MIX), (A["b_gate"], ROW_GATE), (A["conv_w"].rearrange("l k n -> l (k n)"), ROW_CONV),
                            (A["xattn_norm"], ROW_XN), (A["mem_norm"], ROW_MN), (A["ffn_norm"], ROW_FF),
                            (A["final_norm"].unsqueeze(0).broadcast_to([L, D]), ROW_FIN)):
                rows = src.rearrange("l (r p) -> r l p", p=P)
                sp.dma_start(vecrows[at:at + rows.shape[0], :, :], rows).then_inc(S["rows_loaded"], 16)
            for name in KV_UNITS:
                load_dense(0, name)
            for layer in range(L):
                for name in MIX_UNITS[3:] if layer else MIX_UNITS:
                    load_dense(layer, name)
                for name in KV_UNITS if layer + 1 < L else []:
                    load_dense(layer + 1, name)
                u0 = FIRST_EXPERT[layer]
                w1 = A["w_expert_in"][layer].rearrange("e (h k p) n -> e h p k n", h=2, p=P)
                w2 = A["w_expert_out"][layer].rearrange("e (k p) n -> e p k n", p=P)

                def expert_unit(slot, e, x, loaded):
                    src = w1[bass.ds(e, 1), x] if x < 2 else w2[bass.ds(e, 1)]
                    sp.dma_start(ring[:, slot, :].rearrange("p (k n) -> p k n", k=4), src.squeeze(0)).then_inc(loaded, 16)

                for n in range(R):
                    slot_is_free(u0 + n)
                    expert_unit((u0 + n) % R, n // 3, n % 3, slot_loaded[(u0 + n) % R])
                with sp.Fori(0, TURNS - 1) as turn:
                    for n in range(R, R + 3 * EI):
                        sp.wait_ge(S["units_used"], turn * (3 * EI) + (3 * NE * layer + n - R + 1))
                        expert_unit((u0 + n) % R, turn * EI + n // 3, n % 3, slot_loaded[(u0 + n) % R])
                for n in range(R + 3 * EI * (TURNS - 1), 3 * NE):
                    slot_is_free(u0 + n)
                    expert_unit((u0 + n) % R, n // 3, n % 3, slot_loaded[(u0 + n) % R])
                X = extra_sems[layer]
                u1 = u0 + 3 * NE
                for x in range(3):
                    slot_is_free(u1 + x)
                sp.sem_inc(X["used"], 1)
                sp.wait_ge(S["table_ready"], layer + 1)
                count = sp.value_load(tabi[0:1, 32:33], min_val=0, max_val=XB)
                with sp.If(count > 0):
                    with sp.Fori(0, count) as k:
                        e = sp.value_load(tabi[0:1, bass.ds(k, 1)], min_val=0, max_val=NE - 1)
                        sp.wait_ge(X["used"], k + 1)
                        for x in range(3):
                            expert_unit((u1 + x) % R, e, x, X["loaded"])
                for name in MIX_UNITS[:3] if layer + 1 < L else []:
                    load_dense(layer + 1, name)
                sp.wait_ge(X["used"], count + 1)
                for x in range(3) if layer + 1 < L else []:
                    sp.sem_inc(slot_loaded[(u1 + x) % R], 16)
            for i in range(4):
                sp.wait_ge(S["out_ready"], i + 1)
                sp.dma_start(out[0].rearrange("(t p) d -> t p d", p=P)[i % 2, :, (i // 2) * 512:(i // 2) * 512 + 512],
                             arena[:, i * 512:(i + 1) * 512]).then_inc(S["stored"], 16)
            sp.wait_ge(S["stored"], 64)

        @block.gpsimd
        def _(pool):
            pool.memset(ones[:, :], 1.0).then_inc(S["pool_step"], 1)
            for n, key in enumerate(PIECES):
                if by_pool(key):
                    pool.wait_ge(S["w_high"], n + 1)
                    pool.tensor_tensor(piece_view(w_lo, *key), piece_view(ring, *key), high_view(*key).bitcast(F32),
                                       ALU.subtract).then_inc(S["w_split_pool"], 1)

        @block.scalar
        def _(act):
            steps = [0]

            def link(ins):
                steps[0] += 1
                ins.then_inc(S["act_step"], 1)
                act.wait_ge(S["act_step"], steps[0])

            def post(ins, stage):
                link(ins)
                act.sem_inc(S[stage], 1)

            split = [0]

            def split_to(layer, unit, half, ahead=2):
                while split[0] <= ahead_of(layer, unit, half, ahead):
                    n = split[0]
                    key = PIECES[n]
                    u = UNIT_NO[key[:2]]
                    act.wait_ge(slot_loaded[u % R], 16 * (u // R + 1))
                    if n >= HI:
                        act.wait_ge(S["acc_ready"], piece_job(*PIECES[n - HI])[1])
                    post(act.copy(high_view(*key), piece_view(ring, *key)), "w_high")
                    split[0] += 1

            act.dma_start(cst[:, :], A["cst"]).then_inc(S["cst_loaded"], 16)
            act.dma_start(posrow[:, :], A["positions"].broadcast_to([P, T])).then_inc(S["small_loaded"], 16)
            act.dma_start(sinks[:, :, :], A["attn_sinks"].unsqueeze(0).broadcast_to([P, L, 8])).then_inc(S["small_loaded"], 16)
            act.dma_start(rbias[:, :, 0:NG], A["b_router_group"].unsqueeze(0).broadcast_to([P, L, NG])).then_inc(S["small_loaded"], 16)
            act.dma_start(rbias[:, :, NG:], A["b_router_expert"].unsqueeze(0).broadcast_to([P, L, NE])).then_inc(S["small_loaded"], 16)

            two = lambda acc: acc.rearrange("p (c t) -> p c t", c=2)

            def evac(layer, name, i, dst, signal, func=None, view=two):
                src = view(job_wait(act, layer, name, i))
                post(act.copy(dst, src) if func is None else act.activation(dst, src, func), signal)
                act.sem_inc(free(layer, name, i), 1)

            def root(no, layer, name):
                acc = job_wait(act, layer, name)
                post(act.activation(std, acc[:, 0:T], ACT.Sqrt, bias=small[:, 95:96], scale=1.0 / D), "std_ready")
                act.sem_inc(free(layer, name), 1)

            n_norm, n_x = [1], [0]

            def x_squares():
                for i in range(4):
                    act.wait_ge(S["x_ready"], 4 * n_x[0] + i + 1)
                    post(act.activation(hT[:, 2 * i:2 * i + 2, :], xT[:, 2 * i:2 * i + 2, :], ACT.Square), "sq_ready")
                n_x[0] += 1

            def x_root(layer, name):
                root(n_norm[0], layer, name)
                n_norm[0] += 1

            def x_high():
                for i in range(4):
                    act.wait_ge(S["h_full"], 4 * (n_norm[0] - 1) + i + 1)
                    post(act.copy(h_hi[:, 2 * i:2 * i + 2, :], hT[:, 2 * i:2 * i + 2, :]), "h_high")

            def x_norm(layer, name, split_high):
                x_squares()
                x_root(layer, name)
                if split_high:
                    x_high()

            def memory_high(layer, memory):
                for k in range(KC):
                    if layer == 0:
                        act.wait_ge(S["mhat_ready"], k // 2 + 1)
                    post(act.activation(m_hi[:, k, :], memory[:, k, :], ACT.Copy,
                                        scale=vec[:, layer, ROW_MN + k:ROW_MN + k + 1]), "m_high")

            def make_k(layer, between=lambda: None):
                for i in range(4):
                    split_to(layer, f"xk{i // 2}", i % 2)
                    evac(layer, "xk", i, k_made[:, 2 * i:2 * i + 2, :], "kv_made")
                    if i == 1:
                        between()
                act.dma_start(kv_dram[layer, 0], k_made.rearrange("p a b -> p (a b)")).then_inc(S["k_stored"], 16)

            def make_v(layer):
                for i in range(4):
                    split_to(layer, f"xv{i // 2}", i % 2)
                    evac(layer, "xv", i, v_made[:, :, i * 256:i * 256 + 256], "kv_made")
                act.dma_start(kv_dram[layer, 1], v_made.rearrange("p a b -> p (a b)")).then_inc(S["v_stored"], 16)

            act.wait_ge(S["eps_ready"], 1)
            for i in range(4):
                evac(0, "mem", i, mem_T[:, 2 * i:2 * i + 2, :], "mem_ready")
                post(act.activation(hT[:, 2 * i:2 * i + 2, :], mem_T[:, 2 * i:2 * i + 2, :], ACT.Square), "sq_ready")
            root(0, 0, "memnorm")
            for i in range(4):
                evac(0, "x", i, xT[:, 2 * i:2 * i + 2, :], "x_ready")
            split_to(0, "xk0", 0, ahead=0)
            act.wait_ge(S["vec_ready"], 1)
            memory_high(0, mem_T)
            act.dma_start(mhat_dram, mem_T.rearrange("p a b -> p (a b)")).then_inc(S["mhat_stored"], 16)
            split_to(0, "xk0", 0)
            x_squares()
            make_k(0, lambda: x_root(0, "norm0"))
            x_high()
            act.wait_ge(S["mhat_stored"], 16)
            make_v(0)
            for n, table in enumerate((sinT, cosT)):
                act.wait_ge(S["angles"], n + 1)
                post(act.activation(table[:, :], table[:, :], ACT.Sin), "rope_ready")
            for layer in range(L):
                if layer:
                    split_to(layer, "q", 0)
                    x_norm(layer, "norm0", True)
                act.dma_start(wsr[:, :, :], A["gmlp_w_s"][layer].rearrange("g i j -> i g j")).then_inc(S["ws_loaded"], 16)
                act.dma_start(lnt[:, 0, :], A["gmlp_ln_g"][layer:layer + 1].broadcast_to([P, MW])).then_inc(S["ln_loaded"], 16)
                act.dma_start(lnt[:, 1, :], A["gmlp_ln_b"][layer:layer + 1].broadcast_to([P, MW])).then_inc(S["ln_loaded"], 16)
                act.dma_start(bs[0:1, :], A["gmlp_b_s"][layer].rearrange("g i -> (g i)").unsqueeze(0)).then_inc(S["ln_loaded"], 16)
                act.dma_start(wr[:, :, 0:NG], A["w_router_group"][layer].rearrange("(k p) n -> p k n", p=P)).then_inc(S["wr_loaded"], 16)
                act.dma_start(wr[:, :, NG:], A["w_router_expert"][layer].rearrange("(k p) n -> p k n", p=P)).then_inc(S["wr_loaded"], 16)
                for i in range(2):
                    split_to(layer, "q", i)
                    evac(layer, "q", i, qraw[:, 2 * i:2 * i + 2, :], "qraw_ready")
                split_to(layer, "kv", 0)
                evac(layer, "k", 0, kraw[:, 0, :], "qraw_ready", view=lambda a: a[:, 0:T])
                evac(layer, "v", 0, vtok[:, 0:2, :], "v_ready", view=lambda a: a.rearrange("p (t c) -> p t c", t=2)[:, :, P:])
                post(act.copy(vtok[0:64, 2, :], vtok[0:64, 1, :]), "v_ready")
                post(act.copy(vtok[64:P, 2, :], vtok[64:P, 0, :]), "v_ready")
                for i in range(2):
                    split_to(layer, "u", i)
                    evac(layer, "u", i, uT[:, 2 * i:2 * i + 2, :], "gelu_ready", func=ACT.Gelu_apprx_tanh)
                for i in range(2):
                    split_to(layer, "vg", i)
                    evac(layer, "vg", i, vg[:, :, i * 256:i * 256 + 256], "gelu_ready", func=ACT.Gelu_apprx_tanh)
                evac(layer, "ws", 0, wsT[:, :, :], "ws_ready", view=lambda a: a.rearrange("p (g i) -> p g i", g=4))
                split_to(layer, "cx", 0)
                for i in range(4):
                    if i == 2:
                        split_to(layer, "cx", 1)
                    act.wait_ge(S["s_shifted"], 4 * layer + i + 1)
                    flat = prob[:, i].rearrange("p h k -> p (h k)")
                    link(act.activation(flat, flat, ACT.Exp))
                    post(act.activation(small[:, 32 + 4 * i:36 + 4 * i], small[:, 32 + 4 * i:36 + 4 * i], ACT.Exp), "s_exped")
                for i in range(2):
                    evac(layer, "cx", i, cx[:, 2 * i:2 * i + 2, :], "c_ready")
                split_to(layer, "cb", 0)
                evac(layer, "cb", 0, cb[:, 0:2, :], "c_ready")
                split_to(layer, "cb", 1)
                act.wait_ge(S["ln_var"], layer + 1)
                post(act.activation(small[:, 8:16], small[:, 0:8], ACT.Sqrt, bias=small[:, 95:96], scale=1.0 / P), "ln_std")
                evac(layer, "cb", 1, cb[:, 2:4, :], "c_ready")
                for i in range(4):
                    evac(layer, "pt", i, probT[:, i, :], "probT_ready", view=lambda a: a)
                for i in range(2):
                    split_to(layer, "cc", i)
                for i in range(2):
                    acc = job_wait(act, layer, "pv", i)
                    post(act.copy(ya_hi[:, 2 * i:2 * i + 2, :], two(acc)), "y_high")
                split_to(layer, "gate00", 0)
                split_to(layer, "gate00", 1)
                act.wait_ge(S["y_full"], 2 * layer + 1)
                post(act.copy(yc_hi[:, :, :], ycT[:, :, :]), "y_high")
                split_to(layer, "br00", 0)
                act.wait_ge(S["y_full"], 2 * layer + 2)
                post(act.copy(yb_hi[:, :, :], uT[:, :, :]), "y_high")
                n = 12 * layer
                for h in range(2):
                    for i in range(3):
                        for j in range(2):
                            split_to(layer, f"gate{i}{h}", j)
                            acc = job_wait(act, layer, f"gate{i}{h}", j)
                            if n >= 2:
                                act.wait_ge(S["sig_used"], n - 1)
                            for c in range(2):
                                col = ROW_GATE + i * KC + h * 4 + j * 2 + c
                                link(act.activation(sig[:, j, c * T:(c + 1) * T], acc[:, c * T:(c + 1) * T], ACT.Sigmoid,
                                                    bias=vec[:, layer, col:col + 1]))
                            act.sem_inc(free(layer, f"gate{i}{h}", j), 1)
                            act.sem_inc(S["sig_ready"], 1)
                            n += 1
                        for j in range(2) if (i, h) != (2, 1) else ():
                            split_to(layer, f"br{i}{h}", j)
                act.wait_ge(S["acc_ready"], JOB[layer, "gate21", 1][1])
                for i in range(4):
                    if i == 2:
                        split_to(layer, "br21", 0)
                        split_to(layer, "br21", 1)
                    act.wait_ge(S["merged_full"], 4 * layer + i + 1)
                    post(act.copy(h_hi[:, 2 * i:2 * i + 2, :], merged[:, 2 * i:2 * i + 2, :]), "merged_high")
                act.wait_ge(S["acc_ready"], JOB[layer, "br21", 1][1])
                act.wait_ge(S["merged_high"], 4 * layer + 4)
                act.wait_ge(S["merged_ready"], 4 * layer + 4)
                act.wait_ge(S["k_stored"], 16 * (layer + 1))
                act.wait_ge(S["v_stored"], 16 * (layer + 1))
                act.dma_start(kxT.rearrange("p a b -> p (a b)"), kv_dram[layer, 0]).then_inc(S["kv_loaded"], 16)
                act.dma_start(vx.rearrange("p a b -> p (a b)"), kv_dram[layer, 1]).then_inc(S["kv_loaded"], 16)
                for i in range(4):
                    split_to(layer, f"wo{i // 2}", i % 2)
                x_norm(layer, "norm1", True)
                def exps(i):
                    act.wait_ge(S["xs_shifted"], 4 * layer + i + 1)
                    post(act.activation(xprob[:, i, :], xprob[:, i, :], ACT.Exp), "xs_exped")

                def turned(i):
                    hp, tb = i // 2, i % 2
                    acc = job_wait(act, layer, "xpt", i)
                    for kb in range(2):
                        link(act.copy(xprobT[:, kb, 2 * hp:2 * hp + 2, tb * P:(tb + 1) * P],
                                      acc.rearrange("p (h b q) -> p h b q", h=2, b=2)[:, :, kb, :]))
                    act.sem_inc(free(layer, "xpt", i), 1)
                    act.sem_inc(S["xprobT_ready"], 1)

                for i in range(4):
                    if i != 1:
                        split_to(layer, f"xq{i // 2}", i % 2)
                    if i == 2:
                        exps(0)
                        exps(1)
                    evac(layer, "xq", i, qxT[:, 2 * i:2 * i + 2, :], "qx_ready")
                    if i == 1:
                        split_to(layer, "xq0", 1)
                turned(0)
                turned(1)
                exps(2)
                exps(3)
                for i in range(4):
                    if i == 2:
                        turned(2)
                        turned(3)
                        if layer + 1 < L:
                            act.wait_ge(S["acc_ready"], JOB[layer, "xpt", 3][1])
                            act.wait_ge(S["mhat_stored"], 16)
                            act.dma_start(mhatT.rearrange("p a b -> p (a b)"), mhat_dram).then_inc(S["mhat_loaded"], 16)
                    acc = job_wait(act, layer, "xpv", i)
                    post(act.copy(h_hi[:, 2 * i:2 * i + 2, :], two(acc)), "o_high")
                for i in range(4):
                    split_to(layer, f"xo{i // 2}", i % 2)
                if layer + 1 < L:
                    act.wait_ge(S["mhat_loaded"], 16)
                    memory_high(layer + 1, mhatT)
                x_norm(layer, "norm2", False)
                if layer + 1 < L:
                    make_k(layer + 1)
                for i in range(4):
                    evac(layer, "htok", i, htok[:, i // 2, (i % 2) * 512:(i % 2) * 512 + 512], "htok_ready", view=lambda a: a)
                act.wait_ge(S["r_shift"], layer + 1)
                link(act.activation(rt[:, 20, 0:8], rt[:, 20, 0:8], ACT.Exp))
                post(act.activation(rt[:, 21, 0:2], rt[:, 21, 0:2], ACT.Exp), "r_exp")
                if layer + 1 < L:
                    make_v(layer + 1)

                def experts(Q, turn, ne):
                    n0 = turn * ne
                    for r in range(4):
                        act.wait_ge(Q["gathered"], turn * 4 + (r + 1))
                        act.copy(xTe[:, 2 * r:2 * r + 2, 0:ne * SL],
                                 psum[:, (7, 5)[r % 2], :].rearrange("p (c s) -> p c s", c=2)[:, :, 0:ne * SL]).then_inc(Q["xe_ready"], 1)
                    for e in range(ne):
                        act.wait_ge(Q["gu_ready"], n0 + (e + 1))
                        act.activation(sg, psum[:, 4, (e % 2) * T:(e % 2) * T + P], ACT.Silu).then_inc(Q["silu_ready"], 1)
                        act.wait_ge(Q["swt_turned"], n0 + (e + 1))
                        act.copy(swt[:, e, :], psum[:, 7, 0:T]).then_inc(Q["swt_ready"], 1)
                        act.wait_ge(Q["hid_turned"], n0 + (e + 1))
                        act.copy(hhT, psum[:, 6, T:T + P]).then_inc(Q["hidT_ready"], 1)

                base = layer * TURNS
                experts(main_sems, base, EI)
                with act.Fori(base + 1, base + TURNS) as turn:
                    experts(main_sems, turn, EI)
                act.wait_ge(S["table_ready"], layer + 1)
                count = act.value_load(tabi[0:1, 32:33], min_val=0, max_val=XB)
                with act.If(count > 0):
                    with act.Fori(0, count) as k:
                        experts(extra_sems[layer], k, 1)
            x_norm(L, "norm0", False)
            for i in range(4):
                evac(L, "out", i, arena[:, i * 512:(i + 1) * 512], "out_ready", view=lambda a: a)
            act.wait_ge(S["k_stored"], 16 * L)
            act.wait_ge(S["v_stored"], 16 * L)

        @block.vector
        def _(dve):
            steps = [0]

            def link(ins):
                steps[0] += 1
                ins.then_inc(S["dve_step"], 1)
                dve.wait_ge(S["dve_step"], steps[0])

            def post(ins, stage):
                link(ins)
                dve.sem_inc(S[stage], 1)

            split = [0]

            def split_to(layer, unit, half, ahead=2):
                while split[0] <= ahead_of(layer, unit, half, ahead):
                    key = PIECES[split[0]]
                    if not by_pool(key):
                        dve.wait_ge(S["w_high"], split[0] + 1)
                        post(dve.tensor_tensor(piece_view(w_lo, *key), piece_view(ring, *key), high_view(*key).bitcast(F32),
                                               ALU.subtract), "w_split_dve")
                    split[0] += 1

            def bc(v, n):
                return v.unsqueeze(2).broadcast_to([P, v.shape[1], n])

            two = lambda acc: acc.rearrange("p (c t) -> p c t", c=2)
            flat = lambda v: v.rearrange("p a b -> p (a b)")

            post(dve.memset(zero[:, :], 0.0), "zero_ready")
            post(dve.memset(small[:, 95:96], EPS), "eps_ready")

            n_norm, n_high, n_x, n_sum = [0], [0], [4], [0]

            def pair_sums(*pairs):
                for i in pairs:
                    n_sum[0] += 1
                    dve.wait_ge(S["sq_ready"], n_sum[0])
                    post(dve.tensor_tensor(hT[:, 2 * i, :], hT[:, 2 * i, :], hT[:, 2 * i + 1, :], ALU.add), "sum_ready")

            pair_sums(0, 1, 2, 3)

            def norm(col, layer, split_low):
                dve.wait_ge(S["std_ready"], n_norm[0] + 1)
                n_norm[0] += 1
                link(dve.reciprocal(rstd, std))
                for i in range(5):
                    for k in (2 * i, 2 * i + 1) if i < 4 else ():
                        ins = dve.scalar_tensor_tensor(hT[:, k, :], xT[:, k, :], vec[:, layer, col + k:col + k + 1], rstd,
                                                       ALU.mult, ALU.mult)
                        if k % 2:
                            post(ins, "h_full")
                    if split_low and i:
                        n_high[0] += 1
                        dve.wait_ge(S["h_high"], n_high[0])
                        part = slice(2 * i - 2, 2 * i)
                        post(dve.tensor_tensor(h_lo[:, part, :], hT[:, part, :], h_hi[:, part, :].bitcast(F32), ALU.subtract), "h_ready")

            def memory_low(layer, memory):
                for k in range(KC):
                    dve.wait_ge(S["m_high"], KC * layer + k + 1)
                    post(dve.scalar_tensor_tensor(m_lo[:, k, :], memory[:, k, :], vec[:, layer, ROW_MN + k:ROW_MN + k + 1],
                                                  m_hi[:, k, :].bitcast(F32), ALU.mult, ALU.subtract), "m_ready")

            for i in range(2):
                acc = job_wait(dve, 0, "vec", i)
                post(dve.tensor_copy(vec[:, i, :], acc[:, 0:ROWS]), "vec_ready")
                dve.sem_inc(free(0, "vec", i), 1)
            dve.wait_ge(S["std_ready"], 1)
            n_norm[0] = 1
            link(dve.reciprocal(rstd, std))
            for i in range(4):
                part = mem_T[:, 2 * i:2 * i + 2, :]
                post(dve.tensor_tensor(part, part, rstd.unsqueeze(1).broadcast_to([P, 2, T]), ALU.mult), "mhat_ready")
                dve.sem_inc(S["h_full"], 1)
            memory_low(0, mem_T)
            dve.wait_ge(S["x_ready"], 4)
            pair_sums(0, 1, 2, 3)

            def angles():
                dve.wait_ge(S["small_loaded"], 64)
                ang, turns_f = lnt[:, 0, T:2 * T], lnt[:, 1, 0:T]
                link(dve.tensor_copy(ang, posrow[:, :]))
                link(dve.tensor_scalar(ang, ang, inv, None, ALU.mult))
                C1, C2 = 6.28125, 0.0019350051879882812
                C3 = 2 * np.pi - C1 - C2
                for dst, ahead in ((sinT[:, :], 0.0), (cosT[:, :], 0.25)):
                    link(dve.tensor_scalar(turns_f, ang, 1.0 / (2 * np.pi), ahead, ALU.mult, ALU.add))
                    link(dve.tensor_copy(posrow[:, :], turns_f))
                    link(dve.tensor_copy(turns_f, posrow[:, :]))
                    link(dve.scalar_tensor_tensor(dst, turns_f, -C1, ang, ALU.mult, ALU.add))
                    link(dve.scalar_tensor_tensor(dst, turns_f, -C2, dst, ALU.mult, ALU.add))
                    link(dve.scalar_tensor_tensor(dst, turns_f, -C3, dst, ALU.mult, ALU.add))
                    if ahead:
                        link(dve.tensor_scalar(dst, dst, np.pi / 2, None, ALU.add))
                    link(dve.tensor_scalar(turns_f, dst, float(np.pi), -2 * np.pi, ALU.is_gt, ALU.mult))
                    link(dve.tensor_tensor(dst, dst, turns_f, ALU.add))
                    link(dve.tensor_scalar(turns_f, dst, -float(np.pi), 2 * np.pi, ALU.is_lt, ALU.mult))
                    link(dve.tensor_tensor(dst, dst, turns_f, ALU.add))
                    post(dve.tensor_scalar(dst, dst, 3.1415925, -3.1415925, ALU.min, ALU.max), "angles")

            def add_x(layer, name, i):
                acc = job_wait(dve, layer, name, i)
                dst = xT[:, 2 * i:2 * i + 2, :]
                post(dve.tensor_tensor(dst, dst, two(acc), ALU.add), "x_ready")
                dve.sem_inc(free(layer, name, i), 1)

            for layer in range(L):
                norm(ROW_MIX, layer, True)
                if layer == 0:
                    angles()
                split_to(layer, "q", 0)
                split_to(layer, "q", 1)
                if layer == 0:
                    dve.wait_ge(S["k_stored"], 16)
                    dve.wait_ge(S["v_stored"], 16)
                link(dve.memset(kbd[:, :, :, :], 0.0))
                split_to(layer, "kv", 0)
                split_to(layer, "u", 0)
                split_to(layer, "u", 1)
                cos2 = cosT[:, :].unsqueeze(1).broadcast_to([P, 2, T])
                sin2 = sinT[:, :].unsqueeze(1).broadcast_to([P, 2, T])
                tmp = two(stat[:, :])
                dve.wait_ge(S["rope_ready"], 2)
                for i in range(3):
                    acc = two(job_wait(dve, layer, "rot", i))
                    link(dve.tensor_tensor(tmp, acc, sin2, ALU.mult))
                    dve.sem_inc(free(layer, "rot", i), 1)
                    dve.wait_ge(S["qraw_ready"], 3 * layer + i + 1)
                    if i < 2:
                        raw = qraw[:, 2 * i:2 * i + 2, :]
                        link(dve.tensor_tensor(raw, raw, cos2, ALU.mult))
                        link(dve.tensor_tensor(qT[:, 2 * i:2 * i + 2, :], raw, tmp, ALU.add))
                    else:
                        swapped = job_wait(dve, layer, "rot", 3)
                        link(dve.tensor_tensor(kraw[:, 0, :], kraw[:, 0, :], cosT[:, :], ALU.mult))
                        link(dve.tensor_tensor(kraw[:, 1, :], swapped[:, 0:T], cosT[:, :], ALU.mult))
                        dve.sem_inc(free(layer, "rot", 3), 1)
                        link(dve.tensor_tensor(kbd[0:64, 0, 0, :], kraw[0:64, 0, :], tmp[0:64, 0, :], ALU.add))
                        link(dve.tensor_tensor(kbd[64:P, 1, 1, :], kraw[64:P, 0, :], tmp[64:P, 0, :], ALU.add))
                        link(dve.tensor_tensor(kbd[64:P, 0, 1, :], kraw[64:P, 1, :], tmp[64:P, 1, :], ALU.add))
                        link(dve.tensor_tensor(kbd[0:64, 1, 0, :], kraw[0:64, 1, :], tmp[0:64, 1, :], ALU.add))
                    dve.sem_inc(S["qk_ready"], 1)
                split_to(layer, "vg", 0)
                split_to(layer, "vg", 1)
                dve.wait_ge(S["ws_ready"], layer + 1)
                post(dve.memset(wsT[64:P, :, 0:64], 0.0), "ws_masked")
                for i in range(4):
                    g, p = i // 2, i % 2
                    acc = job_wait(dve, layer, "s", i).rearrange("p (h k) -> p h k", h=4)
                    mx = small[:, 24:28]
                    if p == 0:
                        link(dve.memset(acc[0:64, :, 64:P], NEG))
                    link(dve.tensor_reduce(mx, acc, AX.X, ALU.max))
                    link(dve.scalar_tensor_tensor(mx, mx, 0.125, sinks[:, layer, 4 * g:4 * g + 4], ALU.mult, ALU.max))
                    link(dve.tensor_tensor(small[:, 32 + 4 * i:36 + 4 * i], sinks[:, layer, 4 * g:4 * g + 4], mx, ALU.subtract))
                    link(dve.scalar_tensor_tensor(prob[:, i], acc, 0.125, bc(mx, P), ALU.mult, ALU.subtract))
                    dve.sem_inc(free(layer, "s", i), 1)
                    dve.sem_inc(S["s_shifted"], 1)
                split_to(layer, "cx", 0)
                for i in range(4):
                    if i == 2:
                        split_to(layer, "cx", 1)
                    dve.wait_ge(S["s_exped"], 4 * layer + i + 1)
                    link(dve.tensor_reduce(small[:, 24:28], prob[:, i], AX.X, ALU.add))
                    link(dve.tensor_tensor(small[:, 24:28], small[:, 24:28], small[:, 32 + 4 * i:36 + 4 * i], ALU.add))
                    link(dve.reciprocal(small[:, 24:28], small[:, 24:28]))
                    post(dve.tensor_tensor(prob[:, i], prob[:, i], bc(small[:, 24:28], P), ALU.mult), "prob_ready")
                split_to(layer, "cb", 0)
                dve.wait_ge(S["gelu_ready"], 4 * layer + 4)
                vgv = vg[:, :, :].rearrange("p t (g c) -> p (t g) c", c=P)
                link(dve.tensor_reduce(small[:, 0:8], vgv, AX.X, ALU.add))
                link(dve.tensor_scalar(small[:, 0:8], small[:, 0:8], 1.0 / P, None, ALU.mult))
                link(dve.tensor_tensor(vgv, vgv, bc(small[:, 0:8], P), ALU.subtract))
                link(dve.tensor_tensor(ln_sq, vgv, vgv, ALU.mult))
                post(dve.tensor_reduce(small[:, 0:8], ln_sq, AX.X, ALU.add), "ln_var")
                split_to(layer, "cb", 1)
                dve.wait_ge(S["ln_loaded"], 48 * (layer + 1))
                dve.wait_ge(S["ln_std"], layer + 1)
                link(dve.reciprocal(small[:, 16:24], small[:, 8:16]))
                link(dve.tensor_tensor(vgv, vgv, bc(small[:, 16:24], P), ALU.mult))
                link(dve.tensor_tensor(vg[:, :, :], vg[:, :, :], lnt[:, 0:1, :].broadcast_to([P, TB, MW]), ALU.mult))
                post(dve.tensor_tensor(vg[:, :, :], vg[:, :, :], lnt[:, 1:2, :].broadcast_to([P, TB, MW]), ALU.add), "vn_ready")
                job_wait(dve, layer, "pt", 3)
                link(dve.memset(z[:, :, 0:2], 0.0))
                for i in range(2):
                    split_to(layer, "cc", i)
                    dve.wait_ge(S["c_ready"], 4 * layer + 2)
                    acc = job_wait(dve, layer, "cc", i)
                    link(dve.tensor_tensor(z[:, 2 * i:2 * i + 2, 2:T + 2], cx[:, 2 * i:2 * i + 2, :], two(acc), ALU.mult))
                    dve.sem_inc(free(layer, "cc", i), 1)
                for i in range(2):
                    dve.wait_ge(S["y_high"], 4 * layer + i + 1)
                    acc = job_wait(dve, layer, "pv", i)
                    post(dve.tensor_tensor(ya_lo[:, 2 * i:2 * i + 2, :], two(acc), ya_hi[:, 2 * i:2 * i + 2, :].bitcast(F32),
                                           ALU.subtract), "y_ready")
                    dve.sem_inc(free(layer, "pv", i), 1)
                for c in range(MC):
                    w = [vec[:, layer, ROW_CONV + 4 * k + c:ROW_CONV + 4 * k + c + 1] for k in range(3)]
                    link(dve.tensor_scalar(ycT[:, c, :], z[:, c, 0:T], w[0], None, ALU.mult))
                    link(dve.scalar_tensor_tensor(ycT[:, c, :], z[:, c, 1:T + 1], w[1], ycT[:, c, :], ALU.mult, ALU.add))
                    link(dve.scalar_tensor_tensor(ycT[:, c, :], z[:, c, 2:T + 2], w[2], ycT[:, c, :], ALU.mult, ALU.add))
                dve.wait_ge(S["c_ready"], 4 * layer + 4)
                post(dve.tensor_tensor(ycT[:, :, :], ycT[:, :, :], cb[:, :, :], ALU.mult), "y_full")
                for tb in range(TB):
                    acc = job_wait(dve, layer, "mixed", tb)
                    link(dve.tensor_tensor(uT[:, :, tb * P:(tb + 1) * P], uT[:, :, tb * P:(tb + 1) * P],
                                           acc.rearrange("p (g i) -> p g i", g=4), ALU.mult))
                    dve.sem_inc(free(layer, "mixed", tb), 1)
                dve.sem_inc(S["y_full"], 1)
                dve.wait_ge(S["y_high"], 4 * layer + 3)
                post(dve.tensor_tensor(flat(yc_lo), flat(ycT), flat(yc_hi).bitcast(F32), ALU.subtract), "y_ready")
                split_to(layer, "br00", 0)
                dve.wait_ge(S["y_high"], 4 * layer + 4)
                post(dve.tensor_tensor(flat(yb_lo), flat(uT), flat(yb_hi).bitcast(F32), ALU.subtract), "y_ready")
                n = 12 * layer
                def merged_part(i):
                    dve.wait_ge(S["merged_high"], 4 * layer + i + 1)
                    part = slice(2 * i, 2 * i + 2)
                    post(dve.tensor_tensor(merged_lo[:, part, :], merged[:, part, :], h_hi[:, part, :].bitcast(F32),
                                           ALU.subtract), "merged_ready")

                for h in range(2):
                    for i in range(3):
                        for j in range(2):
                            split_to(layer, f"gate{i}{h}", j)
                        for j in range(2):
                            if (i, h) != (2, 1):
                                split_to(layer, f"br{i}{h}", j)
                            elif j == 0:
                                merged_part(0)
                                merged_part(1)
                            else:
                                split_to(layer, "br21", 0)
                            acc = job_wait(dve, layer, f"br{i}{h}", j)
                            dve.wait_ge(S["sig_ready"], n + 1)
                            c0 = 4 * h + 2 * j
                            dst = flat(merged[:, c0:c0 + 2, :])
                            if i == 0:
                                link(dve.tensor_tensor(dst, sig[:, j, :], acc, ALU.mult))
                            else:
                                link(dve.tensor_tensor(gtmp, sig[:, j, :], acc, ALU.mult))
                                link(dve.tensor_tensor(dst, dst, gtmp, ALU.add))
                            dve.sem_inc(free(layer, f"br{i}{h}", j), 1)
                            dve.sem_inc(S["sig_used"], 1)
                            if i == 2:
                                dve.sem_inc(S["merged_full"], 1)
                            n += 1
                split_to(layer, "br21", 1)
                merged_part(2)
                merged_part(3)
                for i in range(4):
                    split_to(layer, f"wo{i // 2}", i % 2)
                    if i == 3:
                        pair_sums(0, 1)
                    add_x(layer, "wo", i)
                pair_sums(2, 3)
                norm(ROW_XN, layer, True)
                def shift(i):
                    acc = job_wait(dve, layer, "xs", i).rearrange("p (h k) -> p h k", h=2)
                    mx = small[:, 24:26]
                    buf = xprob[:, i, :].rearrange("p (h k) -> p h k", h=2)
                    link(dve.tensor_reduce(mx, acc, AX.X, ALU.max))
                    link(dve.tensor_scalar(mx, mx, 0.0625, None, ALU.mult))
                    link(dve.scalar_tensor_tensor(buf, acc, 0.0625, bc(mx, T), ALU.mult, ALU.subtract))
                    dve.sem_inc(free(layer, "xs", i), 1)
                    dve.sem_inc(S["xs_shifted"], 1)

                def scale(i):
                    buf = xprob[:, i, :].rearrange("p (h k) -> p h k", h=2)
                    dve.wait_ge(S["xs_exped"], 4 * layer + i + 1)
                    link(dve.tensor_reduce(small[:, 24:26], buf, AX.X, ALU.add))
                    link(dve.reciprocal(small[:, 24:26], small[:, 24:26]))
                    post(dve.tensor_tensor(buf, buf, bc(small[:, 24:26], T), ALU.mult), "xprob_ready")

                def o_part(i):
                    dve.wait_ge(S["o_high"], 4 * layer + i + 1)
                    acc = job_wait(dve, layer, "xpv", i)
                    part = slice(2 * i, 2 * i + 2)
                    post(dve.tensor_tensor(o_lo[:, part, :], two(acc), h_hi[:, part, :].bitcast(F32), ALU.subtract), "o_ready")
                    dve.sem_inc(free(layer, "xpv", i), 1)

                split_to(layer, "xq0", 0)
                split_to(layer, "xq0", 1)
                shift(0)
                shift(1)
                split_to(layer, "xq1", 0)
                scale(0)
                scale(1)
                split_to(layer, "xq1", 1)
                shift(2)
                shift(3)
                scale(2)
                scale(3)
                for i in range(4):
                    o_part(i)
                for i in range(4):
                    split_to(layer, f"xo{i // 2}", i % 2)
                    if i == 3:
                        pair_sums(0, 1)
                    add_x(layer, "xo", i)
                pair_sums(2, 3)
                if layer + 1 < L:
                    memory_low(layer + 1, mhatT)
                norm(ROW_FF, layer, False)
                acc = job_wait(dve, layer, "router")
                link(dve.tensor_tensor(logit[:, :, :], acc[:, 0:TB * (NG + NE)].rearrange("p (t n) -> p t n", t=TB),
                                       rbias[:, layer:layer + 1, :].broadcast_to([P, TB, NG + NE]), ALU.add))
                dve.sem_inc(free(layer, "router"), 1)
                gm, ge, gi = rt[:, 0, 0:2], rt[:, 1, 0:8].rearrange("p (t n) -> p t n", t=2), rt[:, 2, 0:2]
                ex = rt[:, 20, 0:8].rearrange("p (t n) -> p t n", t=2)
                gl, el = logit[:, :, 0:NG], logit[:, :, NG:]

                def first_max(values, n, best, onehot, where):
                    io = iota[:, 0:n].unsqueeze(1).broadcast_to([P, TB, n])
                    link(dve.tensor_reduce(best, values, AX.X, ALU.max))
                    link(dve.tensor_tensor(onehot, values, bc(best, n), ALU.is_lt))
                    link(dve.scalar_tensor_tensor(onehot, onehot, 1000.0, io, ALU.mult, ALU.add))
                    link(dve.tensor_reduce(where, onehot, AX.X, ALU.min))
                    link(dve.tensor_tensor(onehot, io, bc(where, n), ALU.is_equal))

                first_max(gl, NG, gm, ge, gi)
                link(dve.tensor_tensor(ex, gl, bc(gm, NG), ALU.subtract))
                lem = rt[:, 4:6, :]
                oh1, oh2 = rt[:, 6:8, :], rt[:, 8:10, :]
                t1, t2, wi = rt[:, 10, 0:2], rt[:, 11, 0:2], rt[:, 12, 0:2]
                off = rt[:, 13, 0:8].rearrange("p (t n) -> p t n", t=2)
                link(dve.tensor_scalar(off, ge, -NEG, NEG, ALU.mult, ALU.add))
                for tb in range(TB):
                    e4 = el[:, tb, :].rearrange("p (g e) -> p g e", g=NG)
                    l4 = lem[:, tb, :].rearrange("p (g e) -> p g e", g=NG)
                    link(dve.tensor_tensor(l4, e4, bc(ge[:, tb, :], EPG), ALU.mult))
                    link(dve.tensor_tensor(l4, l4, bc(off[:, tb, :], EPG), ALU.add))
                first_max(lem, NE, t1, oh1, wi)
                link(dve.scalar_tensor_tensor(lem, oh1, 2 * NEG, lem, ALU.mult, ALU.add))
                first_max(lem, NE, t2, oh2, wi)
                link(dve.tensor_tensor(rt[:, 21, 0:2], t2, t1, ALU.subtract))
                dve.sem_inc(S["r_shift"], 1)
                post(dve.tensor_tensor(mask[:, :, :], oh1, oh2, ALU.add), "mask_ready")
                acc = job_wait(dve, layer, "place")
                pl = acc[:, 0:TB * NE].rearrange("p (t n) -> p t n", t=TB)
                dve.wait_ge(S["mask_ready"], layer + 1)
                link(dve.scalar_tensor_tensor(place[:, :, :], pl, 1.0, mask[:, :, :], ALU.add, ALU.mult))
                link(dve.tensor_scalar(place[:, :, :], place[:, :, :], -1.0, None, ALU.add))
                link(dve.tensor_scalar(tab[0:NE, 0:7], thr[0:NE], acc[0:NE, 64:65], None, ALU.is_lt))
                dve.sem_inc(free(layer, "place"), 1)

                def experts(Q, turn, ne, build):
                    n0 = turn * ne
                    dve.wait_ge(Q["sel_used"], turn + 1)
                    build()
                    for e in range(ne):
                        dve.wait_ge(Q["silu_ready"], n0 + (e + 1))
                        dve.tensor_tensor(hh, sg, psum[:, 4, (e % 2) * T + P:(e % 2) * T + T], ALU.mult).then_inc(Q["hid_ready"], 1)
                        dve.wait_ge(Q["y_done"], n0 + (e + 1))
                        dve.tensor_copy(ysb, psum[:, 5, 0:T]).then_inc(Q["y_copied"], 1)

                if layer + 1 < L:
                    dve.wait_ge(S["k_stored"], 16 * (layer + 2))
                base = layer * TURNS

                def weights():
                    dve.wait_ge(S["r_exp"], layer + 1)
                    gs, w1, w2 = rt[:, 14, 0:2], rt[:, 15, 0:2], rt[:, 16, 0:2]
                    link(dve.tensor_reduce(gs, ex, AX.X, ALU.add))
                    link(dve.tensor_scalar(w1, rt[:, 21, 0:2], 1.0, None, ALU.add))
                    link(dve.tensor_tensor(w1, w1, gs, ALU.mult))
                    link(dve.reciprocal(w1, w1))
                    link(dve.tensor_tensor(w2, w1, rt[:, 21, 0:2], ALU.mult))
                    link(dve.tensor_tensor(oh1, oh1, bc(w1, NE), ALU.mult))
                    link(dve.tensor_tensor(oh2, oh2, bc(w2, NE), ALU.mult))
                    link(dve.tensor_tensor(wtok[:, :, :], oh1, oh2, ALU.add))

                def main_turn(turn, before=lambda: None, between=lambda: None):
                    def build():
                        Q = main_sems
                        io = iota[:, 0:SL].unsqueeze(1).broadcast_to([P, EI, SL])
                        at = (turn - base) * EI
                        for tb in range(TB):
                            dve.tensor_tensor(sel[:, tb], bc(place[:, tb, bass.ds(at, EI)], SL), io,
                                              ALU.is_equal).then_inc(Q["sel_ready"], 1)
                        before()
                        for tb in range(TB):
                            dve.wait_ge(Q["sel_ready"], turn * 4 + (tb * 2 + tb + 2 - tb * 2))
                            four = selw[:, tb].rearrange("p e (j s) -> p e j s", j=4)
                            w = wtok[:, tb, bass.ds(at, EI)].unsqueeze(2).unsqueeze(3).broadcast_to([P, EI, 4, SL])
                            dve.tensor_tensor(four, w, sel[:, tb].unsqueeze(2).broadcast_to([P, EI, 4, SL]), ALU.mult).then_inc(Q["sel_ready"], 1)
                        between()
                    experts(main_sems, turn, EI, build)

                def small_tables():
                    if layer + 1 < L:
                        dve.wait_ge(S["v_stored"], 16 * (layer + 2))
                    link(dve.tensor_reduce(tab[0:NE, 8:9], tab[0:NE, 0:7], AX.X, ALU.add))
                    dve.sem_inc(S["extra_ready"], 1)
                    acc = job_wait(dve, layer, "start")
                    link(dve.tensor_copy(tab[0:NE, 9:10], acc[0:NE, T:T + 1]))
                    dve.sem_inc(free(layer, "start"), 1)
                    link(dve.tensor_tensor(tab[0:NE, 10:11], tab[0:NE, 9:10], tab[0:NE, 8:9], ALU.add))
                    link(dve.tensor_scalar(tab[0:NE, 32:48], iota[0:NE, 0:16], tab[0:NE, 9:10], None, ALU.is_ge))
                    link(dve.tensor_scalar(tab[0:NE, 48:64], iota[0:NE, 0:16], tab[0:NE, 10:11], None, ALU.is_lt))
                    link(dve.tensor_tensor(tab[0:NE, 48:64], tab[0:NE, 48:64], tab[0:NE, 32:48], ALU.mult))
                    link(dve.tensor_scalar(tab[0:NE, 16:32], iota[0:NE, 0:16], tab[0:NE, 9:10], 1.0, ALU.subtract, ALU.add))
                    link(dve.tensor_tensor(tab[0:NE, 16:32], tab[0:NE, 16:32], tab[0:NE, 48:64], ALU.mult))
                    link(dve.tensor_scalar(tab[0:NE, 0:8], iota[0:NE, 0:8], 0.0, None, ALU.mult))
                    link(dve.tensor_scalar(tab[0:NE, 32:48], tab[0:NE, 48:64], idx[0:NE], None, ALU.mult))
                    dve.sem_inc(S["span_ready"], 1)
                    acc = job_wait(dve, layer, "table")
                    link(dve.tensor_copy(tabi[0:1, 0:33], acc[0:1, T:T + 33]))
                    dve.sem_inc(free(layer, "table"), 1)
                    dve.sem_inc(S["table_ready"], 1)

                main_turn(base, weights, small_tables)
                with dve.Fori(base + 1, base + TURNS) as turn:
                    main_turn(turn)
                count = dve.value_load(tabi[0:1, 32:33], min_val=0, max_val=XB)
                with dve.If(count > 0):
                    with dve.Fori(0, count) as k:
                        e = dve.value_load(tabi[0:1, bass.ds(k, 1)], min_val=0, max_val=NE - 1)
                        b = dve.value_load(tabi[0:1, bass.ds(k + 16, 1)], min_val=0, max_val=7)

                        def build():
                            Q = extra_sems[layer]
                            for tb in range(TB):
                                dve.tensor_tensor(sel[:, tb, 0, :], place[:, tb, bass.ds(e, 1)].broadcast_to([P, SL]),
                                                  iota[:, bass.ds(b * SL, SL)], ALU.is_equal).then_inc(Q["sel_ready"], 1)
                            for tb in range(TB):
                                dve.wait_ge(Q["sel_ready"], k * 4 + (tb + 2))
                                four = selw[:, tb, 0, :].rearrange("p (j s) -> p j s", j=4)
                                w = wtok[:, tb, bass.ds(e, 1)].unsqueeze(2).broadcast_to([P, 4, SL])
                                dve.tensor_tensor(four, w, sel[:, tb, 0:1, :].broadcast_to([P, 4, SL]), ALU.mult).then_inc(Q["sel_ready"], 1)
                        experts(extra_sems[layer], k, 1, build)
                for i in range(4):
                    add_x(layer, "moe", i)
                    if i:
                        pair_sums(i - 1)
                pair_sums(3)
            norm(ROW_FIN, 0, False)

        @block.tensor
        def _(pe):
            def done(ins):
                ins.then_inc(S["acc_ready"], 1)

            def turn_in(name, src, loaded):
                pe.wait_ge(S[loaded], 16)
                for i in range(4):
                    acc = job_begin(pe, 0, name, i)
                    for c in range(2):
                        for tb in range(TB):
                            d = (2 * i + c) * P
                            ins = pe.transpose(acc[:, c * T + tb * P:c * T + (tb + 1) * P], src[:, tb, d:d + P], ident)
                    done(ins)

            n_norm = [0]

            def norm(layer, name):
                acc = job_begin(pe, layer, name)
                for i in range(4):
                    pe.wait_ge(S["sum_ready"], 4 * n_norm[0] + i + 1)
                    ins = pe.matmul(acc[:, 0:T], ones[:, :], hT[:, 2 * i, :], start=i == 0, stop=i == 3)
                done(ins)
                n_norm[0] += 1

            def piece(layer, unit, half):
                n = PIECE_NO[layer, unit, half]
                pe.wait_ge(S["w_split_pool" if by_pool((layer, unit, half)) else "w_split_dve"], split_count(n))
                return high_view(layer, unit, half), piece_view(w_lo, layer, unit, half)

            def three(acc, w, x, kc, stationary, moving, waits=None):
                for k in range(kc):
                    if waits and k % 2 == 0:
                        waits(k // 2)
                    passes = ((0, 0), (0, 1), (1, 0))
                    for n, (a, b) in enumerate(passes):
                        ins = pe.matmul(acc, stationary(a, k), moving(b, k), start=k == 0 and n == 0,
                                        stop=k == kc - 1 and n == 2)
                return ins

            def dense(layer, unit, job, x, kc=KC, i0=0, waits=None):
                for half in range(2):
                    w = piece(layer, unit, half)
                    acc = job_begin(pe, layer, job, i0 + half)
                    for c in range(2):
                        ins = three(acc[:, c * T:(c + 1) * T], w, x, kc, lambda a, k: w[a][:, k, c * P:(c + 1) * P],
                                    lambda b, k: x[b][:, k, :], waits if half == 0 and c == 0 else None)
                    done(ins)

            def dense_by_parts(layer, unit, job, x, waits, i0=0):
                w, acc = {}, {}
                for part, half in ((0, 0), (1, 0), (0, 1), (1, 1), (2, 0), (2, 1), (3, 0), (3, 1)):
                    if half == 0:
                        waits(part)
                    if part == 0:
                        w[half] = piece(layer, unit, half)
                        acc[half] = job_begin(pe, layer, job, i0 + half)
                    for c in range(2):
                        for k in (2 * part, 2 * part + 1):
                            for n, (a, b) in enumerate(((0, 0), (0, 1), (1, 0))):
                                ins = pe.matmul(acc[half][:, c * T:(c + 1) * T], w[half][a][:, k, c * P:(c + 1) * P], x[b][:, k, :],
                                                start=c == 0 and k == 0 and n == 0, stop=k == KC - 1 and n == 2,
                                                skip_group_check=True)
                    if part == KC // 2 - 1:
                        done(ins)

            def dense_tokens(layer, unit, job, x, i0=0):
                for half in range(2):
                    w = piece(layer, unit, half)
                    acc = job_begin(pe, layer, job, i0 + half)
                    for tb in range(TB):
                        ins = three(acc[:, tb * T:(tb + 1) * T], w, x, KC, lambda a, k: x[a][:, k, tb * P:(tb + 1) * P],
                                    lambda b, k: w[b][:, k, :])
                    done(ins)

            h, m, o = (h_hi, h_lo), (m_hi, m_lo), (h_hi, o_lo)
            n_h = [0]

            def h_part(i):
                pe.wait_ge(S["h_ready"], 4 * n_h[0] + i + 1)

            def m_part(layer):
                return lambda i: pe.wait_ge(S["m_ready"], KC * layer + 2 * i + 2)

            pe.wait_ge(S["cst_loaded"], 16)
            turn_in("mem", mem_raw, "mem_loaded")
            pe.wait_ge(S["rows_loaded"], 16 * 7)
            for layer in range(L):
                acc = job_begin(pe, 0, "vec", layer)
                done(pe.transpose(acc[:, 0:ROWS], vecrows[:, layer, :], ident[0:ROWS, 0:ROWS]))
            pe.wait_ge(S["pool_step"], 1)
            norm(0, "memnorm")
            turn_in("x", x_raw, "x_loaded")
            dense(0, "xk0", "xk", m, waits=m_part(0))
            norm(0, "norm0")
            dense(0, "xk1", "xk", m, i0=2)
            for i in range(2):
                dense_tokens(0, f"xv{i}", "xv", m, i0=2 * i)
            for layer in range(L):
                if layer:
                    norm(layer, "norm0")
                dense_by_parts(layer, "q", "q", h, h_part)
                n_h[0] += 1
                w = piece(layer, "kv", 0)
                acc = job_begin(pe, layer, "k")
                done(three(acc[:, 0:T], w, h, KC, lambda a, k: w[a][:, k, 0:P], lambda b, k: h[b][:, k, :]))
                acc = job_begin(pe, layer, "v")
                for tb in range(TB):
                    ins = three(acc[:, tb * T:(tb + 1) * T], w, h, KC, lambda a, k: h[a][:, k, tb * P:(tb + 1) * P],
                                lambda b, k: w[b][:, k, :])
                done(ins)
                dense(layer, "u", "u", h)
                pe.wait_ge(S["qraw_ready"], 3 * layer + 3)
                for i in range(2):
                    acc = job_begin(pe, layer, "rot", i)
                    done(pe.matmul(acc, rotm, qraw[:, 2 * i:2 * i + 2, :].rearrange("p c t -> p (c t)"), start=True, stop=True))
                acc = job_begin(pe, layer, "rot", 2)
                pe.matmul(acc[:, 0:T], rotm, kraw[:, 0, :], start=True, stop=True)
                done(pe.matmul(acc[:, T:2 * T], rotswap, kraw[:, 0, :], start=True, stop=True))
                acc = job_begin(pe, layer, "rot", 3)
                done(pe.matmul(acc[:, 0:T], swapm, kraw[:, 0, :], start=True, stop=True))
                dense_tokens(layer, "vg", "vg", h)
                pe.wait_ge(S["ws_loaded"], 16 * (layer + 1))
                acc = job_begin(pe, layer, "ws")
                for g in range(4):
                    ins = pe.transpose(acc[:, g * P:(g + 1) * P], wsr[:, g, :], ident)
                done(ins)
                pe.wait_ge(S["qk_ready"], 3 * layer + 3)
                for i in range(4):
                    g, p = i // 2, i % 2
                    acc = job_begin(pe, layer, "s", i).rearrange("p (h k) -> p h k", h=4)
                    for half in range(2):
                        c = 2 * p + half
                        for hp in range(2):
                            q = qT[:, 2 * g + hp, c * 64:(c + 1) * 64]
                            rows = slice(half * 64, half * 64 + 64)
                            wins = [(0, 128, 64), (64, 64, 64)] if c == 2 else [(0, (0, 0, None, 128)[c], 128)]
                            for at, first, n in wins:
                                ins = pe.matmul(acc[rows, 2 * hp:2 * hp + 2, at:at + n], q, kbd[:, g, :, first:first + n],
                                                start=True, stop=True)
                    done(ins)
                dense(layer, "cx", "cx", h)
                dense(layer, "cb", "cb", h)
                for i in range(4):
                    pe.wait_ge(S["prob_ready"], 4 * layer + i + 1)
                    acc = job_begin(pe, layer, "pt", i)
                    for hd in range(4):
                        ins = pe.transpose(acc[:, hd * P:(hd + 1) * P], prob[:, i, hd, :], ident)
                    done(ins)
                dense(layer, "cc", "cc", h)
                pe.wait_ge(S["v_ready"], 3 * layer + 3)
                pe.wait_ge(S["probT_ready"], 4 * layer + 4)
                for g in range(2):
                    acc = job_begin(pe, layer, "pv", g).rearrange("p (c t) -> p c t", c=2)
                    for c in range(4):
                        v = vtok[:, (0, 0, 2, 1)[c], g * 64:g * 64 + 64]
                        pt = probT[:, 2 * g + c // 2, :].rearrange("p (a b q) -> p a b q", a=2, b=2)
                        for par in range(2):
                            ins = pe.matmul(acc[par * 64:par * 64 + 64, :, c * 64:(c + 1) * 64], v,
                                            pt[:, :, par, (c % 2) * 64:(c % 2) * 64 + 64], start=True, stop=True)
                    done(ins)
                pe.wait_ge(S["vn_ready"], layer + 1)
                pe.wait_ge(S["ws_masked"], layer + 1)
                pe.wait_ge(S["ln_loaded"], 48 * (layer + 1))
                for tb in range(TB):
                    acc = job_begin(pe, layer, "mixed", tb)
                    pe.matmul(acc, ones[0:1, :], bs[0:1, :], start=True, stop=False, skip_group_check=True)
                    for g in range(4):
                        ins = pe.matmul(acc[:, g * P:(g + 1) * P], vg[:, tb, g * P:(g + 1) * P], wsT[:, g, :],
                                        start=False, stop=g == 3, skip_group_check=True)
                    done(ins)
                for hf in range(2):
                    for i in range(3):
                        dense(layer, f"gate{i}{hf}", f"gate{i}{hf}", h)
                        if hf == 0:
                            pe.wait_ge(S["y_ready"], 4 * layer + (2, 4, 4)[i])
                        dense(layer, f"br{i}{hf}", f"br{i}{hf}", ((ya_hi, ya_lo), (yb_hi, yb_lo), (yc_hi, yc_lo))[i], kc=MC)
                merged_parts = lambda i: pe.wait_ge(S["merged_ready"], 4 * layer + i + 1)
                dense_by_parts(layer, "wo0", "wo", (h_hi, merged_lo), merged_parts)
                dense(layer, "wo1", "wo", (h_hi, merged_lo), i0=2)
                norm(layer, "norm1")

                def scores(i):
                    hp, tb = i // 2, i % 2
                    if tb == 0:
                        pe.wait_ge(S["qx_ready"], 4 * layer + (2, 4)[hp])
                    acc = job_begin(pe, layer, "xs", i)
                    for hd in range(2):
                        for k in range(2):
                            c = 2 * (2 * hp + hd) + k
                            ins = pe.matmul(acc[:, hd * T:(hd + 1) * T], qxT[:, c, tb * P:(tb + 1) * P], kxT[:, c, :],
                                            start=k == 0, stop=k == 1)
                    done(ins)

                def turn_probs(i):
                    pe.wait_ge(S["xprob_ready"], 4 * layer + i + 1)
                    acc = job_begin(pe, layer, "xpt", i)
                    for j in range(4):
                        ins = pe.transpose(acc[:, j * P:(j + 1) * P], xprob[:, i, j * P:(j + 1) * P], ident)
                    done(ins)

                def values(hd):
                    pe.wait_ge(S["xprobT_ready"], 4 * layer + (2, 4)[hd // 2])
                    acc = job_begin(pe, layer, "xpv", hd)
                    for c in range(2):
                        for kb in range(2):
                            ins = pe.matmul(acc[:, c * T:(c + 1) * T], vx[:, kb, (2 * hd + c) * P:(2 * hd + c + 1) * P],
                                            xprobT[:, kb, hd, :], start=kb == 0, stop=kb == 1)
                    done(ins)

                dense_by_parts(layer, "xq0", "xq", h, h_part)
                n_h[0] += 1
                pe.wait_ge(S["kv_loaded"], 32 * (layer + 1))
                scores(0)
                scores(1)
                dense(layer, "xq1", "xq", h, i0=2)
                turn_probs(0)
                turn_probs(1)
                scores(2)
                scores(3)
                values(0)
                values(1)
                turn_probs(2)
                turn_probs(3)
                values(2)
                values(3)
                dense_by_parts(layer, "xo0", "xo", o, lambda i: pe.wait_ge(S["o_ready"], 4 * layer + i + 1))
                dense(layer, "xo1", "xo", o, i0=2)
                norm(layer, "norm2")
                pe.wait_ge(S["zero_ready"], 1)
                for j in range(4):
                    acc = job_begin(pe, layer, "moe", j)
                    row = slice(32 * j, 32 * j + 1)
                    pe.matmul(acc[:, 0:2], zero[row, :], iota[row, 0:2], start=True, stop=False, skip_group_check=True,
                              tile_position=(32 * j, 0))
                for i in range(2) if layer + 1 < L else []:
                    dense(layer + 1, f"xk{i}", "xk", m, i0=2 * i, waits=m_part(layer + 1) if i == 0 else None)
                pe.wait_ge(S["wr_loaded"], 32 * (layer + 1))
                acc = job_begin(pe, layer, "router")
                for k in range(KC):
                    if k % 2 == 0:
                        pe.wait_ge(S["h_full"], 4 * n_norm[0] - 3 + k // 2)
                    for tb in range(TB):
                        ins = pe.matmul(acc[:, tb * (NG + NE):(tb + 1) * (NG + NE)], hT[:, k, tb * P:(tb + 1) * P], wr[:, k, :],
                                        start=k == 0 and tb == 0, stop=k == KC - 1, skip_group_check=True)
                done(ins)
                for i in range(4):
                    tb, half = i // 2, i % 2
                    acc = job_begin(pe, layer, "htok", i)
                    for c in range(4):
                        ins = pe.transpose(acc[:, c * P:(c + 1) * P], hT[:, 4 * half + c, tb * P:(tb + 1) * P], ident)
                    done(ins)
                for i in range(2) if layer + 1 < L else []:
                    dense_tokens(layer + 1, f"xv{i}", "xv", m, i0=2 * i)
                pe.wait_ge(S["mask_ready"], layer + 1)
                acc = job_begin(pe, layer, "place")
                pe.matmul(acc[:, 0:NE], tri, mask[:, 0, :], start=True, stop=True)
                pe.matmul(acc[:, NE:2 * NE], tri, mask[:, 1, :], start=True, stop=False)
                pe.matmul(acc[:, NE:2 * NE], ones[:, :], mask[:, 0, :], start=False, stop=True)
                pe.matmul(acc[0:NE, 64:65], mask[:, 0, :], ones[:, 0:1], start=True, stop=False)
                done(pe.matmul(acc[0:NE, 64:65], mask[:, 1, :], ones[:, 0:1], start=False, stop=True))

                def starts():
                    pe.wait_ge(S["extra_ready"], layer + 1)
                    acc = job_begin(pe, layer, "start")[:, T:]
                    done(pe.matmul(acc[0:NE, 0:1], tri[0:NE, 0:NE], tab[0:NE, 8:9], start=True, stop=True))

                def tables():
                    pe.wait_ge(S["span_ready"], layer + 1)
                    acc = job_begin(pe, layer, "table")[:, T:]
                    pe.matmul(acc[0:1, 0:16], ones[0:NE, 0:1], tab[0:NE, 32:48], start=True, stop=True)
                    pe.matmul(acc[0:1, 16:32], ones[0:NE, 0:1], tab[0:NE, 16:32], start=True, stop=True)
                    done(pe.matmul(acc[0:1, 32:33], ones[0:NE, 0:1], tab[0:NE, 8:9], start=True, stop=True))
                pe.wait_ge(S["htok_ready"], 4 * layer + 4)

                def experts(Q, turn, ne, slot_wait, slot_done, slot, small_jobs=()):
                    n0 = turn * ne
                    pe.wait_ge(Q["sel_ready"], turn * 4 + 2)

                    def first_product(e, chunks):
                        G = psum[:, 4, (e % 2) * T:(e % 2) * T + T]
                        for k in chunks:
                            if k % 4 == 0:
                                slot_wait(e, k // 4)
                            w = ring[:, slot(e, k // 4), :].rearrange("p (k a b) -> p k a b", k=4, a=2)
                            for j in range(4):
                                ins = pe.matmul(G[32 * j:32 * j + 32, :], xTe[:, k, e * SL:(e + 1) * SL],
                                                w[:, k % 4, :, j * P:(j + 1) * P], start=k == 0, stop=k == KC - 1,
                                                tile_position=(0, 32 * j))
                            if k == 3:
                                slot_done(ins)
                        return ins

                    for r in range(4):
                        if r >= 2:
                            pe.wait_ge(Q["xe_ready"], turn * 4 + (r - 1))
                        bank = (7, 5)[r % 2]
                        for c in range(2):
                            for tb in range(TB):
                                d = (2 * r + c) * P
                                ins = pe.matmul(psum[:, bank, c * T:c * T + ne * SL], htok[:, tb, d:d + P],
                                                sel[:, tb, 0:ne, :].rearrange("p e s -> p (e s)"), start=tb == 0, stop=tb == 1)
                        ins.then_inc(Q["gathered"], 1)
                        if r and small_jobs:
                            pe.wait_ge(Q["xe_ready"], turn * 4 + r)
                            first_product(0, (2 * r - 2, 2 * r - 1))
                    pe.wait_ge(Q["xe_ready"], turn * 4 + 4)
                    if small_jobs:
                        small_jobs[0]()
                    pe.wait_ge(Q["sel_ready"], turn * 4 + 4)
                    for e in range(ne):
                        ins = first_product(e, (6, 7) if small_jobs and e == 0 else range(KC))
                        if small_jobs and e == 0:
                            small_jobs[1]()
                        ins.then_inc(Q["gu_ready"], 1)
                        if ne > 1 and e:
                            pe.wait_ge(Q["swt_ready"], n0 + e)
                        for tb in range(TB):
                            ins = pe.transpose(psum[:, 7, tb * P:(tb + 1) * P], selw[:, tb, e, :], ident)
                        ins.then_inc(Q["swt_turned"], 1)
                        pe.wait_ge(Q["hid_ready"], n0 + (e + 1))
                        pe.transpose(psum[:, 6, T:T + P], hh, ident).then_inc(Q["hid_turned"], 1)
                        pe.wait_ge(Q["hidT_ready"], n0 + (e + 1))
                        slot_wait(e, 2)
                        w = ring[:, slot(e, 2), :].rearrange("p (k n) -> p k n", k=4)
                        for k in range(4):
                            for j in range(4):
                                ins = pe.matmul(psum[32 * j:32 * j + 32, 5, 0:T], hhT[:, k * SL:(k + 1) * SL],
                                                w[:, k, j * T:(j + 1) * T], start=k == 0, stop=k == 3, tile_position=(0, 32 * j))
                                if k == 0 and j == 0:
                                    slot_done(ins)
                                if e == ne - 1 and k == 1 and j == 0:
                                    ins.then_inc(Q["sel_used"], 1)
                        ins.then_inc(Q["y_done"], 1)
                        pe.wait_ge(Q["y_copied"], n0 + (e + 1))
                        pe.wait_ge(Q["swt_ready"], n0 + (e + 1))
                        for c in range(2):
                            for j in range(4):
                                ins = pe.matmul(psum[:, j, c * T:(c + 1) * T], ysb[32 * j:32 * j + 32, c * P:(c + 1) * P],
                                                swt[32 * j:32 * j + 32, e, :], start=False, stop=False,
                                                skip_group_check=True, tile_position=(32 * j, 0))
                                if c == 0 and j == 0:
                                    slot_done(ins)
                    return ins

                base = layer * TURNS
                pe.drain().then_inc(main_sems["sel_used"], 1) if layer == 0 else None
                u0 = FIRST_EXPERT[layer]

                def slot(e, x):
                    return (u0 + 3 * e + x) % R

                def unit_done(ins):
                    ins.then_inc(S["units_used"], 1)

                def main_turn(turn, small_jobs=()):
                    def slot_wait(e, x):
                        u = u0 + 3 * e + x
                        per = 3 * EI // R
                        pe.wait_ge(slot_loaded[u % R], turn * (16 * per) + 16 * (u // R + 1 - base * per))
                    experts(main_sems, turn, EI, slot_wait, unit_done, slot, small_jobs)

                main_turn(base, (starts, tables))
                with pe.Fori(base + 1, base + TURNS) as turn:
                    main_turn(turn)
                X = extra_sems[layer]
                pe.drain().then_inc(X["sel_used"], 1)
                pe.wait_ge(S["table_ready"], layer + 1)
                count = pe.value_load(tabi[0:1, 32:33], min_val=0, max_val=XB)
                u1 = FIRST_EXPERT[layer] + 3 * NE
                with pe.If(count > 0):
                    with pe.Fori(0, count) as k:
                        def slot(e, x):
                            return (u1 + x) % R

                        def slot_wait(e, x):
                            pe.wait_ge(X["loaded"], k * 48 + 48)

                        def slot_done(ins):
                            pass
                        experts(X, k, 1, slot_wait, slot_done, slot).then_inc(X["used"], 1)
                for j in range(4):
                    row = slice(32 * j, 32 * j + 1)
                    done(pe.matmul(psum[:, j, 0:2], zero[row, :], iota[row, 0:2], start=False, stop=True, skip_group_check=True,
                                   tile_position=(32 * j, 0)))
            norm(L, "norm0")
            for i in range(4):
                pe.wait_ge(S["h_full"], 4 * n_norm[0] - (2, 0)[i // 2])
                acc = job_begin(pe, L, "out", i)
                for c in range(4):
                    ins = pe.transpose(acc[:, c * P:(c + 1) * P], hT[:, 4 * (i // 2) + c, (i % 2) * P:(i % 2 + 1) * P], ident)
                done(ins)


_INS = ['x', 'mem', 'positions', 'mix_norm', 'w_in', 'b_gate', 'attn_sinks', 'gmlp_ln_g', 'gmlp_ln_b',
        'gmlp_w_s', 'gmlp_b_s', 'conv_w', 'w_branch', 'w_out', 'xattn_norm', 'mem_norm', 'w_xq', 'w_xkv',
        'w_xo', 'ffn_norm', 'w_router_group', 'b_router_group', 'w_router_expert', 'b_router_expert',
        'w_expert_in', 'w_expert_out', 'final_norm']


def constants():
    c = np.zeros((P, C_END), np.float32)
    p = np.arange(P)
    c[:, C_ID:C_ID + P] = np.eye(P)
    c[:, C_TRI:C_TRI + P] = p[:, None] < p[None, :]
    for m in range(P):
        source = m + 32 if m % 64 < 32 else m - 32
        c[source, C_ROT + m] = c[(source + 64) % P, C_RSW + m] = -1.0 if m % 64 < 32 else 1.0
        c[(m + 64) % P, C_SWAP + m] = 1.0
    half = 32
    inv = np.power(np.float32(10000.0), -np.arange(half, dtype=np.float32) / np.float32(half)).astype(np.float32)
    c[:, C_INV] = inv[p % half]
    c[:, C_IOTA:C_IOTA + T] = np.arange(T)
    c[:, C_IDX] = p
    c[:, C_THR:C_THR + 7] = SL * np.arange(1, 8)
    return c


def kernel(**inputs):
    import concourse.bacc as bacc
    from concourse.bass_utils import run_bass_kernel_spmd

    nc = bacc.Bacc("TRN2", target_bir_lowering=False, num_devices=1)
    arrays, aps = {}, {}
    for name in _INS:
        a = np.ascontiguousarray(inputs[name])
        arrays[f"in_{name}"] = a
        aps[name] = nc.dram_tensor(f"in_{name}", a.shape, mybir.dt.from_np(a.dtype), kind="ExternalInput").ap()
    arrays["in_cst"] = constants()
    aps["cst"] = nc.dram_tensor("in_cst", (P, C_END), F32, kind="ExternalInput").ap()
    out = nc.dram_tensor("out", (1, T, D), F32, kind="ExternalOutput").ap()
    trunk(nc, aps, out)
    r = run_bass_kernel_spmd(nc, [arrays], core_ids=[0])
    return r.results[0]["out"]
```
